# Optimizing a Trainium2 kernel written in Bass

```python
import jax
import jax.numpy as jnp
from jax import lax
import numpy as np

D_MODEL = 1024
BATCH = 1
SEQ = 512
DEPTH = 2
DEC_BATCH = 8
DEC_SEQ = 4
PAST_LEN = 4096
PAGE_SIZE = 128

D_MIX = 2 * D_MODEL
D_CONV = D_MIX // 2
D_SSD = D_MIX - D_CONV
SSD_HEAD_DIM = 64
SSD_HEADS = D_SSD // SSD_HEAD_DIM
SSD_GROUPS = 2
SSD_HEADS_PER_GROUP = SSD_HEADS // SSD_GROUPS
SSD_STATE = 128
SSD_CONV = 4
SSD_CHUNK = 128
SHORT_CONV = 3
D_XBC = D_SSD + 2 * SSD_GROUPS * SSD_STATE
D_IN_PROJ = 3 * D_CONV + D_SSD + D_XBC + SSD_HEADS
D_FF = 2816
N_EXPERTS = 8
TOP_K = 2
D_FF_EXPERT = D_FF // TOP_K
N_DENSE = (DEPTH + 1) // 2
N_MOE = DEPTH // 2
EPS = 1e-6

kernel_name = 'hymba_style_shortconv_ssd_hybrid_step'

def _rmsnorm(x, g):
    xf = x.astype(jnp.float32)
    y = xf * lax.rsqrt(jnp.mean(xf * xf, axis=-1, keepdims=True) + EPS)
    return (y * g.astype(jnp.float32)).astype(x.dtype)

def _causal_dwconv(u, state, w):
    L = u.shape[1]
    k = w.shape[0]
    full = jnp.concatenate([state.astype(u.dtype), u], axis=1)
    out = full[:, 0:L] * w[0]
    for j in range(1, k):
        out = out + full[:, j:j + L] * w[j]
    return out, full[:, L:]

def _ssd_chunked(x, dt, a, bm, cm, s0):
    bsz, L, H, P = x.shape
    N = bm.shape[-1]
    G, HG = SSD_GROUPS, SSD_HEADS_PER_GROUP
    f32 = jnp.float32
    q = min(SSD_CHUNK, L)
    nc = -(-L // q)
    pad = nc * q - L
    x = x.astype(f32)
    dt = dt.astype(f32)
    bm = bm.astype(f32)
    cm = cm.astype(f32)
    if pad:
        x = jnp.pad(x, ((0, 0), (0, pad), (0, 0), (0, 0)))
        dt = jnp.pad(dt, ((0, 0), (0, pad), (0, 0)))
        bm = jnp.pad(bm, ((0, 0), (0, pad), (0, 0), (0, 0)))
        cm = jnp.pad(cm, ((0, 0), (0, pad), (0, 0), (0, 0)))
    x = x.reshape(bsz, nc, q, G, HG, P)
    dt = dt.reshape(bsz, nc, q, G, HG)
    bm = bm.reshape(bsz, nc, q, G, N)
    cm = cm.reshape(bsz, nc, q, G, N)
    cum = jnp.cumsum(dt * a.astype(f32).reshape(G, HG), axis=2)
    xdt = x * dt[..., None]
    causal = jnp.tril(jnp.ones((q, q), dtype=bool))[None, None, :, :, None, None]
    seg = cum[:, :, :, None] - cum[:, :, None, :]
    decay = jnp.exp(jnp.where(causal, seg, -jnp.inf))
    cb = jnp.einsum('bcqgn,bcsgn->bcqsg', cm, bm)
    y_diag = jnp.einsum('bcqsgh,bcsghp->bcqghp', cb[..., None] * decay, xdt)
    to_end = jnp.exp(cum[:, :, -1:] - cum)
    chunk_states = jnp.einsum('bcsgn,bcsghp->bcghpn', bm, xdt * to_end[..., None])
    chunk_decay = jnp.exp(cum[:, :, -1])

    def step(s, inp):
        st, dec = inp
        return s * dec[..., None, None] + st, s

    s_init = s0.astype(f32).reshape(bsz, G, HG, P, N)
    s_fin, s_prev = lax.scan(step, s_init, (jnp.moveaxis(chunk_states, 1, 0), jnp.moveaxis(chunk_decay, 1, 0)))
    s_prev = jnp.moveaxis(s_prev, 0, 1)
    y_off = jnp.einsum('bcqgn,bcghpn->bcqghp', cm, s_prev) * jnp.exp(cum)[..., None]
    y = (y_diag + y_off).reshape(bsz, nc * q, H, P)[:, :L]
    return y, s_fin.reshape(bsz, H, P, N)

def _token_mixer(h, conva_state, convb_state, ssm_state, w_in, w_out, conva_w, convb_w, convb_b,
                 dt_bias, a_log, d_skip, ssd_norm):
    bsz, L, _ = h.shape
    proj = jnp.einsum('bld,de->ble', h, w_in)
    sizes = [D_CONV, D_CONV, D_CONV, D_SSD, D_XBC, SSD_HEADS]
    gb, gc, hv, z, xbc, dt_raw = jnp.split(proj, list(np.cumsum(sizes)[:-1]), axis=-1)
    u = gc * hv
    v, new_conva = _causal_dwconv(u, conva_state, conva_w)
    ya = gb * v
    xbc_c, new_convb = _causal_dwconv(xbc, convb_state, convb_w)
    xbc_c = jax.nn.silu(xbc_c + convb_b)
    gn = SSD_GROUPS * SSD_STATE
    xs = xbc_c[..., :D_SSD].reshape(bsz, L, SSD_HEADS, SSD_HEAD_DIM)
    bm = xbc_c[..., D_SSD:D_SSD + gn].reshape(bsz, L, SSD_GROUPS, SSD_STATE)
    cm = xbc_c[..., D_SSD + gn:].reshape(bsz, L, SSD_GROUPS, SSD_STATE)
    dt = jax.nn.softplus(dt_raw.astype(jnp.float32) + dt_bias.astype(jnp.float32))
    a = -jnp.exp(a_log.astype(jnp.float32))
    y, new_ssm = _ssd_chunked(xs, dt, a, bm, cm, ssm_state)
    y = y + d_skip.astype(jnp.float32)[:, None] * xs.astype(jnp.float32)
    y = y.reshape(bsz, L, D_SSD) * jax.nn.silu(z.astype(jnp.float32))
    yg = y.reshape(bsz, L, SSD_GROUPS, D_SSD // SSD_GROUPS)
    yg = yg * lax.rsqrt(jnp.mean(yg * yg, axis=-1, keepdims=True) + EPS)
    yb = (yg.reshape(bsz, L, D_SSD) * ssd_norm.astype(jnp.float32)).astype(h.dtype)
    out = jnp.einsum('ble,ed->bld', jnp.concatenate([ya, yb], axis=-1), w_out)
    return out, new_conva, new_convb, new_ssm.astype(ssm_state.dtype)

def _swiglu(h, wg, wu, wd):
    g = jnp.einsum('bld,df->blf', h, wg)
    up = jnp.einsum('bld,df->blf', h, wu)
    return jnp.einsum('blf,fd->bld', jax.nn.silu(g) * up, wd)

def _moe_swiglu(h, router, wg, wu, wd):
    logits = jnp.einsum('bld,de->ble', h, router).astype(jnp.float32)
    probs = jax.nn.softmax(logits, axis=-1)
    top_p, top_i = lax.top_k(probs, TOP_K)
    top_p = top_p / jnp.sum(top_p, axis=-1, keepdims=True)
    combine = jnp.sum(jax.nn.one_hot(top_i, N_EXPERTS, dtype=jnp.float32) * top_p[..., None], axis=-2)
    out = jnp.zeros(h.shape, jnp.float32)
    for e in range(N_EXPERTS):
        ye = _swiglu(h, wg[e], wu[e], wd[e]).astype(jnp.float32)
        out = out + combine[..., e:e + 1] * ye
    return out.astype(h.dtype)

def setup_inputs(seed: int = 0) -> dict:
    key = jax.random.key(seed)
    ks = jax.random.split(key, 32)
    f32 = jnp.float32
    nrm = lambda k, shape, s: jax.random.normal(k, shape, f32) * s
    gain = lambda k, shape: 1.0 + 0.02 * jax.random.normal(k, shape, f32)
    dt0 = jnp.exp(jax.random.uniform(ks[20], (DEPTH, SSD_HEADS), f32) * (np.log(0.1) - np.log(0.001)) + np.log(0.001))
    dt_bias = dt0 + jnp.log(-jnp.expm1(-dt0))
    return {
        'x_prompt': nrm(ks[0], (BATCH, SEQ, D_MODEL), 1.0),
        'x_sample': nrm(ks[1], (DEC_BATCH, DEC_SEQ, D_MODEL), 1.0),
        'c_prompt': nrm(ks[2], (BATCH, D_MODEL), 1.0),
        'c_sample': nrm(ks[3], (DEC_BATCH, D_MODEL), 1.0),
        'state_conva': nrm(ks[4], (DEPTH, DEC_BATCH, SHORT_CONV - 1, D_CONV), 1.0),
        'state_convb': nrm(ks[5], (DEPTH, DEC_BATCH, SSD_CONV - 1, D_XBC), 1.0),
        'state_ssm': nrm(ks[6], (DEPTH, DEC_BATCH, SSD_HEADS, SSD_HEAD_DIM, SSD_STATE), 0.3),
        'ada_w': nrm(ks[7], (DEPTH, D_MODEL, 6 * D_MODEL), 0.5 * D_MODEL ** -0.5),
        'ada_b': nrm(ks[8], (DEPTH, 6 * D_MODEL), 0.02),
        'norm_pre_mix': gain(ks[9], (DEPTH, D_MODEL)),
        'norm_post_mix': gain(ks[10], (DEPTH, D_MODEL)),
        'norm_pre_ffn': gain(ks[11], (DEPTH, D_MODEL)),
        'norm_post_ffn': gain(ks[12], (DEPTH, D_MODEL)),
        'w_in': nrm(ks[13], (DEPTH, D_MODEL, D_IN_PROJ), D_MODEL ** -0.5),
        'w_out': nrm(ks[14], (DEPTH, D_MIX, D_MODEL), D_MIX ** -0.5),
        'conva_w': nrm(ks[15], (DEPTH, SHORT_CONV, D_CONV), SHORT_CONV ** -0.5),
        'convb_w': nrm(ks[16], (DEPTH, SSD_CONV, D_XBC), SSD_CONV ** -0.5),
        'convb_b': nrm(ks[17], (DEPTH, D_XBC), 0.02),
        'dt_bias': dt_bias,
        'a_log': jnp.log(jax.random.uniform(ks[18], (DEPTH, SSD_HEADS), f32, 1.0, 16.0)),
        'd_skip': gain(ks[19], (DEPTH, SSD_HEADS)),
        'ssd_norm': gain(ks[21], (DEPTH, D_SSD)),
        'ffd_w_gate': nrm(ks[22], (N_DENSE, D_MODEL, D_FF), D_MODEL ** -0.5),
        'ffd_w_up': nrm(ks[23], (N_DENSE, D_MODEL, D_FF), D_MODEL ** -0.5),
        'ffd_w_down': nrm(ks[24], (N_DENSE, D_FF, D_MODEL), D_FF ** -0.5),
        'moe_router': nrm(ks[25], (N_MOE, D_MODEL, N_EXPERTS), D_MODEL ** -0.5),
        'moe_w_gate': nrm(ks[26], (N_MOE, N_EXPERTS, D_MODEL, D_FF_EXPERT), D_MODEL ** -0.5),
        'moe_w_up': nrm(ks[27], (N_MOE, N_EXPERTS, D_MODEL, D_FF_EXPERT), D_MODEL ** -0.5),
        'moe_w_down': nrm(ks[28], (N_MOE, N_EXPERTS, D_FF_EXPERT, D_MODEL), D_FF_EXPERT ** -0.5),
    }

def reference(x_prompt, x_sample, c_prompt, c_sample, state_conva, state_convb, state_ssm,
              ada_w, ada_b, norm_pre_mix, norm_post_mix, norm_pre_ffn, norm_post_ffn,
              w_in, w_out, conva_w, convb_w, convb_b, dt_bias, a_log, d_skip, ssd_norm,
              ffd_w_gate, ffd_w_up, ffd_w_down, moe_router, moe_w_gate, moe_w_up, moe_w_down):

    def run_group(x, c, conva, convb, ssm):
        new_a, new_b, new_s = [], [], []
        for i in range(DEPTH):
            mod = jnp.einsum('bd,de->be', jax.nn.silu(c), ada_w[i]) + ada_b[i]
            sh1, sc1, g1, sh2, sc2, g2 = [m[:, None, :] for m in jnp.split(mod, 6, axis=-1)]
            h = _rmsnorm(x, norm_pre_mix[i]) * (1.0 + sc1) + sh1
            mix, na, nb, ns = _token_mixer(h, conva[i], convb[i], ssm[i], w_in[i], w_out[i], conva_w[i],
                                           convb_w[i], convb_b[i], dt_bias[i], a_log[i], d_skip[i], ssd_norm[i])
            x = x + g1 * _rmsnorm(mix, norm_post_mix[i])
            h = _rmsnorm(x, norm_pre_ffn[i]) * (1.0 + sc2) + sh2
            j = i // 2
            if i % 2 == 0:
                f = _swiglu(h, ffd_w_gate[j], ffd_w_up[j], ffd_w_down[j])
            else:
                f = _moe_swiglu(h, moe_router[j], moe_w_gate[j], moe_w_up[j], moe_w_down[j])
            x = x + g2 * _rmsnorm(f, norm_post_ffn[i])
            new_a.append(na)
            new_b.append(nb)
            new_s.append(ns)
        return x, jnp.stack(new_a), jnp.stack(new_b), jnp.stack(new_s)

    bp = x_prompt.shape[0]
    zero_a = jnp.zeros((DEPTH, bp, SHORT_CONV - 1, D_CONV), x_prompt.dtype)
    zero_b = jnp.zeros((DEPTH, bp, SSD_CONV - 1, D_XBC), x_prompt.dtype)
    zero_s = jnp.zeros((DEPTH, bp, SSD_HEADS, SSD_HEAD_DIM, SSD_STATE), state_ssm.dtype)
    y_prompt, a_p, b_p, s_p = run_group(x_prompt, c_prompt, zero_a, zero_b, zero_s)
    y_sample, a_s, b_s, s_s = run_group(x_sample, c_sample, state_conva, state_convb, state_ssm)
    return (y_prompt, y_sample, a_p, b_p, s_p, a_s, b_s, s_s)


_drawn_inputs = setup_inputs


def setup_inputs(seed=0):
    import zlib

    import numpy as np

    out = dict(_drawn_inputs(seed))
    spreads = {}
    factors = {'d_skip': 11.41, 'ssd_norm': 13.785, 'norm_post_ffn': 3.145, 'state_conva': 3.021}
    for name, (base, spread) in spreads.items():
        noise = np.random.default_rng([zlib.crc32(name.encode()), seed]).standard_normal(out[name].shape)
        drawn = base * np.exp(spread * noise) if base else spread * noise
        out[name] = jnp.asarray(drawn.astype(out[name].dtype))
    for name, factor in factors.items():
        out[name] = (out[name] * factor).astype(out[name].dtype)
    return out
```

```python
from contextlib import ExitStack

import numpy as np

import concourse.bass as bass
from concourse import mybir

ALU = mybir.AluOpType
ACT = mybir.ActivationFunctionType
F32 = mybir.dt.float32
F32R = mybir.dt.float32r
AX_X = mybir.AxisListType.X

P = 128
D = 1024
KT = D // P
SEQ = 512
NB, TS = 8, 4
NS = NB * TS
T = SEQ + NS
HALF = T // 2
DEPTH = 2
HEADS, HD, NST = 16, 64, 128
GROUPS = 2
GH = HEADS // GROUPS
GT = KT // GROUPS
CH = 128
NCH = SEQ // CH
XBC = 12
FT = 11
NE = 8
NEXP = (2, NE)
SLAB = KT * P
SLABMAX = FT * P
EPS = 1e-6
MODS = 6 * KT
NM = 1 + NB
NG = 2 * MODS // 4
MOD_AT = {(0, "pre_mix"): (4, 5), (0, "cum"): (6,), (0, "gate"): (7,), (0, "post_mix"): (8, 9), (0, "pre_ffn"): (10, 11),
          (0, "post_ffn"): (20, 21), (1, "pre_mix"): (22, 23)}


def columns(*fields):
    at, out = 0, {}
    for name, n in fields:
        out[name] = (at, at + n)
        at += n
    return out, at


PACK, NPACK = columns(("ada_b", MODS), ("pre_mix", KT), ("post_mix", KT), ("pre_ffn", KT), ("post_ffn", KT),
                      ("conva", 3 * KT), ("convb", 4 * XBC), ("convb_b", XBC), ("ssd_norm", KT), ("d_skip", KT),
                      ("w_dt", KT * HEADS), ("dt_bias", HEADS), ("a_log", HEADS))
CONST, NCONST = columns(("tri", P), ("ident", P), ("ones", 1), ("tri_seq", NS), ("same_seq", NS), ("in_seq", NB),
                        ("eps", 1), ("before", NE * NE))

N_XBC, N_MIX, N_GU, N_DOWN = XBC, 4 * KT, 2 * FT, KT
EP = (N_GU + N_DOWN) // 2
LAYER_PAIRS = [(N_XBC + N_MIX + 2 * KT) // 2 + n * EP for n in NEXP]


class Tally:

    def __init__(self, sem, engine):
        self.sem, self.engine, self.base, self.n = sem, engine, 0, 0

    def step(self, ins):
        ins.then_inc(self.sem, 1)
        self.n += 1

    def settle(self):
        self.engine.wait_ge(self.sem, self.base + self.n)

    def enter(self, i, each):
        outer = (self.base, self.n, each)
        self.base, self.n = self.base + self.n + i * each, 0
        return outer

    def leave(self, outer, times):
        base, n, each = outer
        assert self.n == each, (self.n, each)
        self.base, self.n = base, n + times * each


def hybrid_decoder(nc, xT, cT, pack, const, w_router, s_conva, s_convb, s_ssm, w_ada, w_xbc, w_mix, w_out, w_gu0, w_dn0, w_gu1,
                   w_dn1, yT, o_ap, o_bp, o_sp, o_as, o_bs, o_ss):
    x_spill = nc.dram_tensor("x_spill", [P, KT * T], F32).ap()
    w_gu, w_dn = (w_gu0, w_gu1), (w_dn0, w_dn1)
    with ExitStack() as ctx:
        def sb(name, shape, dt=F32, where=ctx):
            return where.enter_context(nc.sbuf_tensor(name, shape, dt))

        def sem(name):
            return ctx.enter_context(nc.semaphore(name))

        raw = sb("raw", [P, 2, SLABMAX])
        whi = sb("whi", [P, 2, SLABMAX], F32R)
        wlo = sb("wlo", [P, 2, SLABMAX], F32R)
        adaw = sb("adaw", [P, 2, SLAB])
        cst = sb("cst", [P, NCONST])
        par = sb("par", [P, DEPTH, NPACK])
        cond = sb("cond", [P, KT, 32])
        modT = sb("modT", [P, 4, 32])
        router = sb("router", [P, KT * NE])
        mod = sb("mod", [P, DEPTH, MODS, NM])
        coef = sb("coef", [P, KT, NM])
        comb = sb("comb", [P, 5, NE])
        usb = sb("usb", [P, XBC, NB, 3 + TS])
        h_hi = sb("h_hi", [P, KT, T], F32R)
        h_lo = sb("h_lo", [P, KT, T], F32R)
        xreg = sb("xreg", [P, KT * T])
        wreg = sb("wreg", [P, 6480])
        with ExitStack() as mixer:
            ya_hi = sb("ya_hi", [P, KT, T], F32R, mixer)
            ya_lo = sb("ya_lo", [P, KT, T], F32R, mixer)
            mix = sb("mix", [P, XBC + KT, T], F32, mixer)
            usa = sb("usa", [P, KT, NB, 2 + TS], F32, mixer)
        with ExitStack() as experts:
            hid_hi = sb("hid_hi", [P, FT, T], F32R, experts)
            hid_lo = sb("hid_lo", [P, FT, T], F32R, experts)
            f = sb("f", [P, KT, T], F32, experts)
        ps = ctx.enter_context(nc.psum_tensor("ps", [P, 8, 512], F32))

        def con(name):
            a, b = CONST[name]
            return cst[:, a:b]

        def prm(layer, name):
            a, b = PACK[name]
            return par[:, layer, a:b]

        def view(buf, at, *shape):
            v = buf[:, at:at + int(np.prod(shape))]
            if len(shape) == 2:
                v = v.rearrange("p (a b) -> p a b", a=shape[0])
            if len(shape) == 3:
                v = v.rearrange("p (a b c) -> p a b c", a=shape[0], b=shape[1])
            return v

        def halves(v):
            return v.rearrange("p (a b) -> p a b", a=2)

        def seqs(v):
            return v.rearrange("p (b t) -> p b t", b=NB)

        def over(v, n):
            return v.unsqueeze(len(v.shape)).broadcast_to([*v.shape, n])

        ident, tri, ones = con("ident"), con("tri"), con("ones").to_broadcast([P, P])
        x = view(xreg, 0, KT, T)
        xs = mix[:, 0:KT, :]
        z = mix[:, XBC:XBC + KT, :]
        B0, C0 = KT, KT + GROUPS
        E = view(xreg, 0, GH, CH)
        Ce = view(xreg, 1024, GH, CH)
        S = view(xreg, 2048, GROUPS, GH * HD)
        xdt = view(xreg, 3072, GH * HD)
        xe = view(xreg, 3584, GH * HD)
        Bt = view(xreg, 4096, NST)
        cbm = view(xreg, 4224, CH)
        x_st = [raw[:, j // 2, SLAB + CH * (j % 2):SLAB + CH * (j % 2 + 1)] for j in range(GT)]
        B_st = raw[:, 0, SLAB + 2 * CH:SLAB + 3 * CH]
        dA_st = raw[:, 1, SLAB + 2 * CH:SLAB + 2 * CH + GH]
        diag = view(wreg, 1280, 5, P)
        yt = view(xreg, 0, KT, NS)
        E_s = view(xreg, 0, HEADS, NS)
        xdt_s = view(xreg, 1024, D)
        cbm_s = view(xreg, 4224, GROUPS, NS)
        S0 = view(wreg, 0, GROUPS, GH * HD)
        xe_s = view(wreg, 1024, D)
        Bt_s = view(wreg, 2048, 2 * NST)
        Bm = view(wreg, 2304, 2 * NST)
        ecum_s = view(wreg, 2560, HEADS, NS)
        yo_s = view(wreg, 3072, KT, NS)
        yd_s = view(wreg, 3328, KT, NS)
        ub = view(wreg, 3584, 3 + T)
        acc = view(wreg, 4131, T)
        gc_s = view(wreg, 4675, T)
        ya_f = view(wreg, 5219, T)
        dt_t = view(wreg, 5763, 5, HEADS)
        dA = view(wreg, 5843, 5, HEADS)
        cum = view(wreg, 5923, 5, HEADS)
        wend = view(wreg, 6003, 5, HEADS)
        dec = view(wreg, 6083, NCH, HEADS)
        dec_s = view(wreg, 6147, NB, HEADS)
        dA_s = view(wreg, 6275, NB, HEADS)
        nap = view(wreg, 6403, KT, 2)
        nbp = view(wreg, 6419, XBC, 3)
        expA = view(wreg, 6455, HEADS)
        sp_x = view(wreg, 4131, 5, HEADS)
        sp_e = view(wreg, 4211, 5, HEADS)
        sp_t = view(wreg, 4291, 5, HEADS)
        sp_l = view(wreg, 4371, 5, HEADS)
        sp_r = view(wreg, 4451, 5, HEADS)
        yb_t = (acc, ub[:, 0:T])
        rg = (gc_s, ya_f)
        sq = view(wreg, 0, KT, T)
        rstd = view(wreg, KT * T, T)
        ta = view(wreg, KT * T + T, T)
        tb = view(wreg, KT * T + 2 * T, T)
        smp = view(wreg, KT * T + 3 * T, KT, NS)
        cbr = view(wreg, 0, T)
        pr = view(wreg, 1024, 5, NE)
        pm = view(wreg, 1064, 5)
        rank = view(wreg, 1072, 5, NE)
        cmp = view(wreg, 1152, NE, NE)
        cmq = view(wreg, 1216, NE, NE)

        PRIME = 2
        params_in, x_in = sem("params_in"), sem("x_in")
        raw_landed = [sem("raw_landed0"), sem("raw_landed1")]
        hi_split = sem("hi_split")
        lo_split = sem("lo_split")
        slabs_used = sem("slabs_used")
        taken = [sem("taken0"), sem("taken1")]
        ada_landed = [sem("ada_landed0"), sem("ada_landed1")]
        ada_used = sem("ada_used")
        ada_out = sem("ada_out")
        cond_ready = sem("cond_ready")
        sq_ready, stat_done, rstd_ready = sem("sq_ready"), sem("stat_done"), sem("rstd_ready")
        smp_ready, t_ready, hhi_ready, h_ready = sem("smp_ready"), sem("t_ready"), sem("hhi_ready"), sem("h_ready")
        x_ready = sem("x_ready")
        act_steps, dve_steps = sem("act_steps"), sem("dve_steps")
        dt_done, dt_x, dt_e, dA_ready = sem("dt_done"), sem("dt_x"), sem("dt_e"), sem("dA_ready")
        conv_done, xbc_ready = sem("conv_done"), sem("xbc_ready")
        yahi_ready, ya_ready = sem("yahi_ready"), sem("ya_ready")
        cum_done, cum_x, cum_e, cum_ready = sem("cum_done"), sem("cum_x"), sem("cum_e"), sem("cum_ready")
        smp_pe, smp_seg, smp_act, smp_G, smp_y, smp_done = (sem("smp_pe"), sem("smp_seg"), sem("smp_act"),
                                                            sem("smp_G"), sem("smp_y"), sem("smp_done"))
        chunk_pe, chunk_seg, chunk_act, chunk_G, chunk_Ce = (sem("chunk_pe"), sem("chunk_seg"), sem("chunk_act"),
                                                             sem("chunk_G"), sem("chunk_Ce"))
        chunk_y, seq_pe, seq_new = sem("chunk_y"), sem("seq_pe"), sem("seq_new")
        seq_in = [sem("seq_in0"), sem("seq_in1")]
        seq_out = [sem("seq_out0"), sem("seq_out1")]
        gz_ready, gy_ready, ybf_ready, ybhi_ready, yb_ready = (sem("gz_ready"), sem("gy_ready"), sem("ybf_ready"),
                                                               sem("ybhi_ready"), sem("yb_ready"))
        windows_in, windows_out, state_out, x_back, spill_out = (sem("windows_in"), sem("windows_out"),
                                                                 sem("state_out"), sem("x_back"), sem("spill_out"))
        hidhi_ready, hid_ready = sem("hidhi_ready"), sem("hid_ready")
        logits_done, router_x, router_e, comb_ready = (sem("logits_done"), sem("router_x"), sem("router_e"),
                                                       sem("comb_ready"))
        combb_done, cbr_ready = sem("combb_done"), sem("cbr_ready")
        y_out, staged, units_free, diag_ready = sem("y_out"), sem("staged"), sem("units_free"), sem("diag_ready")

        FIRST, USES = [], []
        pair = 0
        for L in range(DEPTH):
            FIRST.append({"xbc": pair, "mix": pair + N_XBC // 2, "outA": pair + (N_XBC + N_MIX) // 2,
                          "outB": pair + (N_XBC + N_MIX + KT) // 2, "exp": pair + (N_XBC + N_MIX) // 2 + KT})
            pair += LAYER_PAIRS[L]
        PAIRS = pair

        def bank(s):
            return ps[:, 2 * s:2 * s + 2, 0:HALF]

        NORMS = 6
        PRE_MIX, GATE, POST_MIX, PRE_FFN, POST_FFN = 0, 1, 3, 4, 5
        SQ = {PRE_MIX: 0, GATE: 8, POST_MIX: 16, PRE_FFN: 24, POST_FFN: 32}

        def mod_bank(place, n):
            return {"cum": 6, "gate": 4, "post_ffn": 4 + n % 2}.get(place, 6 + n % 2)

        def sums(idx):
            b = 4 + 2 * (idx % 2)
            return ps[:, b:b + 2, 0:HALF]

        block = ctx.enter_context(nc.Block())

        @block.sync
        def _(sp):
            sp.dma_start(cond[:, :, :].rearrange("p k b -> p (k b)"), cT).then_inc(params_in, 16)
            sp.dma_start(cst[:, :], const).then_inc(params_in, 16)
            sp.dma_start(par[:, :, :].rearrange("p l n -> p (l n)"), pack).then_inc(params_in, 16)
            sp.dma_start(router[:, :], w_router).then_inc(params_in, 16)
            sp.dma_start(xreg[:, :], xT).then_inc(x_in, 16)

            def load_pair(m, src, cols):
                for s in range(2):
                    sp.wait_ge(lo_split, m * 2 + s + 1)
                    sp.dma_start(raw[:, s, 0:cols], src(s)).then_inc(raw_landed[s], 16)

            for L in range(DEPTH):
                first = FIRST[L]
                with sp.Fori(0, N_XBC // 2) as i:
                    load_pair(i + first["xbc"], lambda s: w_xbc[L, i * 2 + s], SLAB)
                with sp.Fori(0, N_MIX // 2) as i:
                    load_pair(i + first["mix"], lambda s: w_mix[L, i * 2 + s], SLAB)
                with sp.Fori(0, KT) as i:
                    load_pair(i + first["outA"], lambda s: w_out[L, i * 2 + s], SLAB)
                with sp.Fori(0, NEXP[L]) as e:
                    with sp.Fori(0, FT) as j:
                        load_pair(e * EP + j + first["exp"], lambda s: w_gu[L][e, j * 2 + s], SLAB)
                    with sp.Fori(0, N_DOWN // 2) as j:
                        load_pair(e * EP + j + (FT + first["exp"]), lambda s: w_dn[L][e, j * 2 + s], SLABMAX)
            sp.wait_ge(x_ready, DEPTH * 2 * KT)
            sp.dma_start(yT, xreg[:, :]).then_inc(y_out, 16)
            sp.wait_ge(y_out, 16)

        @block.gpsimd
        def _(pool):
            def ada_load(n):
                for q in range(4):
                    pool.wait_ge(ada_used, n * 4 + (q + 1))
                    pool.dma_start(adaw[:, q % 2, :], w_ada[n, q]).then_inc(ada_landed[q % 2], 16)

            def ada_loads(L, place):
                for n in MOD_AT.get((L, place), ()):
                    ada_load(n)

            with pool.Fori(0, 4) as n:
                ada_load(n)
            for L in range(DEPTH):
                if L:
                    pool.wait_ge(x_ready, 2 * KT * L)
                    pool.dma_start(x_spill, xreg[:, :]).then_inc(spill_out, 16)
                pool.dma_start(usb[:, :, :, 0:3], s_convb[L].rearrange("p (k b t) -> p k b t", k=XBC, b=NB)
                               ).then_inc(windows_in, 16)
                pool.dma_start(usa[:, :, :, 0:2], s_conva[L].rearrange("p (k b t) -> p k b t", k=KT, b=NB)
                               ).then_inc(windows_in, 16)
                ada_loads(L, "pre_mix")
                ada_loads(L, "cum")
                pool.wait_ge(h_ready, (2 * L + 1) * KT)
                for g in range(GROUPS):
                    pool.dma_start(S0[:, g, :], s_ssm[L, 0, g]).then_inc(seq_in[g], 16)
                pool.wait_ge(xbc_ready, XBC * (L + 1) + 1)
                pool.wait_ge(dA_ready, L + 1)
                with pool.Fori(0, KT) as i:
                    pool.wait_ge(chunk_pe, i + (KT * L + 1))
                    for j in range(GT):
                        nc.gpsimd.tensor_copy(x_st[j], mix[:, (i % 2) * GT + j, bass.ds((i // 2) * CH, CH)])
                    nc.gpsimd.tensor_copy(B_st, mix[:, i % 2 + B0, bass.ds((i // 2) * CH, CH)])
                    nc.gpsimd.tensor_copy(dA_st, dA[:, i // 2, bass.ds((i % 2) * GH, GH)]).then_inc(staged, 1)
                    pool.wait_ge(chunk_act, i * 2 + (1 + 2 * KT * L))
                    nc.gpsimd.tensor_tensor(Ce, Ce, mix[:, i % 2 + C0, bass.ds((i // 2) * CH, CH)].unsqueeze(
                        1).broadcast_to([P, GH, CH]), ALU.mult).then_inc(chunk_Ce, 1)
                    for g in range(GROUPS):
                        pool.wait_ge(seq_new, i * 2 + (g + 1 + 2 * NB * L))
                        pool.dma_start(o_ss[L, i, g], S0[:, g, :]).then_inc(seq_out[g], 16)
                    for g in range(GROUPS):
                        pool.wait_ge(seq_out[g], i * 16 + (16 + 16 * NB * L))
                        pool.dma_start(S0[:, g, :], s_ssm[L, (i + 1) % NB, g]).then_inc(seq_in[g], 16)
                ada_loads(L, "gate")
                pool.wait_ge(ya_ready, KT * (L + 1))
                pool.wait_ge(units_free, (KT + 1) * (L + 1))
                pool.dma_start(o_sp[L], xreg[:, 2048:3072]).then_inc(state_out, 16)
                pool.dma_start(o_as[L].rearrange("p (k b t) -> p k b t", k=KT, b=NB), usa[:, :, :, TS:TS + 2]
                               ).then_inc(windows_out, 16)
                pool.dma_start(o_bs[L].rearrange("p (k b t) -> p k b t", k=XBC, b=NB), usb[:, :, :, TS:TS + 3]
                               ).then_inc(windows_out, 16)
                pool.dma_start(o_ap[L], nap.rearrange("p k t -> p (k t)")).then_inc(windows_out, 16)
                pool.dma_start(o_bp[L], nbp.rearrange("p k t -> p (k t)")).then_inc(windows_out, 16)
                pool.wait_ge(stat_done, NORMS * L + GATE + 2)
                if L:
                    pool.wait_ge(spill_out, 16 * L)
                pool.dma_start(z.rearrange("p k t -> p (k t)"), x_spill if L else xT).then_inc(x_back, 16)
                ada_loads(L, "post_mix")
                ada_loads(L, "pre_ffn")
                pool.wait_ge(windows_out, 64 * (L + 1))
                if L == 0:
                    with pool.Fori(0, N_DOWN) as n:
                        ada_load(n + NG // 2)
                ada_loads(L, "post_ffn")

        @block.scalar
        def _(act):
            st = Tally(act_steps, act)

            def hi(m, s, cols):
                act.wait_ge(raw_landed[s], m * 16 + 16)
                act.wait_ge(slabs_used, m * 2 + (s + 1))
                nc.scalar.copy(whi[:, s, 0:cols], raw[:, s, 0:cols]).then_inc(hi_split, 1)

            def used(m, s):
                act.wait_ge(slabs_used, m * 2 + (s + 1 + PRIME))

            def make_rstd(idx, n, to):
                act.wait_ge(stat_done, idx + 1)
                st.step(nc.scalar.activation(halves(to), sums(idx % NORMS), ACT.Ln, scale=1.0 / n, bias=con("eps")))
                st.settle()
                nc.scalar.activation(to, to, ACT.Exp, scale=-0.5).then_inc(rstd_ready, 1)

            def modulate(L, nth, shift):
                act.wait_ge(smp_ready, 2 * L + nth + 1)
                nc.scalar.copy(h_hi[:, :, SEQ:T], smp).then_inc(hhi_ready, 1)
                base = (2 * L + nth) * KT
                outer = None
                with act.Fori(0, KT) as k:
                    outer = st.enter(k, 1)
                    act.wait_ge(t_ready, k + (base + 1))
                    st.step(nc.scalar.activation(sq[:, k, 0:SEQ], sq[:, k, 0:SEQ], ACT.Identity,
                                                 scale=coef[:, k, 0:1], bias=mod[:, L, k + shift, 0:1]))
                    st.settle()
                    nc.scalar.copy(h_hi[:, k, 0:SEQ], sq[:, k, 0:SEQ]).then_inc(hhi_ready, 1)
                st.leave(outer, KT)

            act.wait_ge(params_in, 64)
            nc.scalar.activation(cond[:, :, :], cond[:, :, :], ACT.Silu).then_inc(cond_ready, 1)
            for s in range(2):
                hi(0, s, SLAB)
            act.wait_ge(x_in, 16)
            for L in range(DEPTH):
                first = FIRST[L]
                with act.Fori(0, KT) as k:
                    if L:
                        act.wait_ge(x_ready, k + (2 * KT * L - KT + 1))
                    nc.scalar.activation(sq[:, k, :], x[:, k, :], ACT.Square).then_inc(sq_ready, 1)
                make_rstd(NORMS * L + PRE_MIX, D, rstd)
                modulate(L, 0, 0)
                act.wait_ge(dt_x, 2 * L + 1)
                st.step(nc.scalar.activation(expA, prm(L, "a_log"), ACT.Exp))
                st.settle()
                nc.scalar.activation(sp_e, sp_e, ACT.Exp).then_inc(dt_e, 1)
                act.wait_ge(dt_x, 2 * L + 2)
                nc.scalar.activation(sp_l, sp_t, ACT.Ln).then_inc(dt_e, 1)
                with act.Fori(0, N_XBC // 2) as i:
                    for s in range(2):
                        t = i * 2 + s
                        used(i + first["xbc"], s)
                        act.wait_ge(conv_done, t + (1 + (XBC + KT) * L))
                        nc.scalar.copy(halves(ub[:, 3:3 + T]), bank(s)).then_inc(taken[s], 1)
                        hi(i + (first["xbc"] + 1), s, SLAB)
                        act.wait_ge(conv_done, t + (2 + (XBC + KT) * L))
                        nc.scalar.activation(mix[:, t, :], acc, ACT.Silu).then_inc(xbc_ready, 1)
                act.wait_ge(cum_done, L + 1)
                act.wait_ge(cum_x, L + 1)
                st.step(nc.scalar.activation(dec, ps[:, 7, 64:128].rearrange("p (c h) -> p c h", c=NCH), ACT.Exp))
                st.step(nc.scalar.activation(dec_s, ps[:, 7, 160:288].rearrange("p (c h) -> p c h", c=NB), ACT.Exp))
                nc.scalar.activation(wend, wend, ACT.Exp).then_inc(cum_e, 1)
                act.wait_ge(smp_seg, L + 1)
                nc.scalar.activation(ecum_s, ps[:, 7, :].rearrange("p (h t) -> p h t", h=HEADS), ACT.Exp
                                     ).then_inc(smp_act, 1)
                nc.scalar.activation(E_s[0:NS], E_s[0:NS], ACT.Exp).then_inc(smp_act, 1)
                with act.Fori(0, KT) as i:
                    mA, mB = i * 2 + first["mix"], i * 2 + (first["mix"] + 1)
                    used(mA, 0)
                    nc.scalar.copy(halves(gc_s), bank(0)).then_inc(taken[0], 1)
                    hi(mB, 0, SLAB)
                    act.wait_ge(chunk_seg, i + (KT * L + 1))
                    nc.scalar.activation(Ce, ps[:, 4:6, :].rearrange("p a (h t) -> p (a h) t", h=4), ACT.Exp
                                         ).then_inc(chunk_act, 1)
                    nc.scalar.activation(E, E, ACT.Exp).then_inc(chunk_act, 1)
                    used(mA, 1)
                    hi(mB, 1, SLAB)
                    act.wait_ge(taken[0], mB + 2)
                    nc.scalar.copy(ya_hi[:, i, :], ya_f).then_inc(yahi_ready, 1)
                    hi(mB + 1, 0, SLAB)
                    used(mB, 1)
                    nc.scalar.copy(halves(mix[:, i + XBC, :]), bank(1)).then_inc(taken[1], 1)
                    hi(mB + 1, 1, SLAB)
                act.wait_ge(taken[1], first["outA"] + 1)
                with act.Fori(0, KT) as k:
                    nc.scalar.activation(mix[:, k + XBC, :], mix[:, k + XBC, :], ACT.Silu).then_inc(gz_ready, 1)
                with act.Fori(0, KT) as k:
                    act.wait_ge(gy_ready, k + (KT * L + 1))
                    nc.scalar.activation(mix[:, k + XBC, :], mix[:, k, :], ACT.Square).then_inc(sq_ready, 1)
                for g in range(GROUPS):
                    make_rstd(NORMS * L + GATE + g, D // GROUPS, rg[g])
                act.wait_ge(state_out, 16 * (L + 1))
                with act.Fori(0, KT // 2) as i:
                    for s in range(2):
                        used(i + first["outA"], s)
                        nc.scalar.copy(halves(x[:, i * 2 + s, :]), bank(s)).then_inc(taken[s], 1)
                        hi(i + (first["outA"] + 1), s, SLAB)
                        act.wait_ge(ybf_ready, i * 2 + (s + 1 + KT * L))
                        nc.scalar.copy(h_hi[:, i * 2 + s, :], yb_t[s]).then_inc(ybhi_ready, 1)
                for g in range(GROUPS):
                    act.wait_ge(seq_in[g], 16 * (NB + 1) * (L + 1))
                act.wait_ge(windows_out, 64 * (L + 1))
                act.wait_ge(yb_ready, KT * (L + 1))
                with act.Fori(0, KT // 2) as i:
                    for s in range(2):
                        used(i + first["outB"], s)
                        hi(i + (first["outB"] + 1), s, SLAB)
                        act.wait_ge(taken[s], i + (first["outB"] + 2))
                        nc.scalar.activation(sq[:, i * 2 + s, :], x[:, i * 2 + s, :], ACT.Square).then_inc(sq_ready, 1)
                make_rstd(NORMS * L + POST_MIX, D, rstd)
                with act.Fori(0, KT) as k:
                    act.wait_ge(x_ready, k + (2 * KT * L + 1))
                    nc.scalar.activation(sq[:, k, :], x[:, k, :], ACT.Square).then_inc(sq_ready, 1)
                make_rstd(NORMS * L + PRE_FFN, D, rstd)
                modulate(L, 1, 3 * KT)
                if L:
                    act.wait_ge(router_x, 1)
                    nc.scalar.activation(pr, pr, ACT.Exp).then_inc(router_e, 1)

                def expert(e, last):
                    m0 = e * EP + first["exp"]

                    def gate_up(j, cols):
                        m = m0 + j
                        used(m, 0)
                        nc.scalar.activation(halves(ta), bank(0), ACT.Silu).then_inc(taken[0], 1)
                        hi(m + 1, 0, cols)
                        used(m, 1)
                        hi(m + 1, 1, cols)
                        act.wait_ge(taken[1], m + 2)
                        nc.scalar.copy(hid_hi[:, j, :], tb).then_inc(hidhi_ready, 1)

                    if L:
                        act.wait_ge(combb_done, e + 1)
                        nc.scalar.copy(cbr[:, 0:SEQ], ps[:, 4, :]).then_inc(cbr_ready, 1)
                        nc.scalar.copy(cbr[:, SEQ:T], ps[:, 5, 0:NS]).then_inc(cbr_ready, 1)
                    with act.Fori(0, FT - 1) as j:
                        gate_up(j, SLAB)
                    gate_up(FT - 1, SLABMAX)
                    with act.Fori(0, N_DOWN // 2 - 1) as j:
                        for s in range(2):
                            used(m0 + FT + j, s)
                            hi(m0 + FT + 1 + j, s, SLABMAX)
                    for s in range(2):
                        if not last:
                            used(m0 + (EP - 1), s)
                            hi(m0 + EP, s, SLAB)

                with act.Fori(0, NEXP[L] - 1) as e:
                    expert(e, False)
                expert(NEXP[L] - 1, L == DEPTH - 1)
                for k in range(KT):
                    act.wait_ge(taken[k % 2], first["exp"] + EP * NEXP[L] - (N_DOWN // 2) + k // 2 + 2)
                    nc.scalar.activation(sq[:, k, :], f[:, k, :], ACT.Square).then_inc(sq_ready, 1)
                make_rstd(NORMS * L + POST_FFN, D, rstd)

        @block.vector
        def _(dve):
            st = Tally(dve_steps, dve)
            v = nc.vector

            def lo(m, s, cols):
                dve.wait_ge(hi_split, m * 2 + (s + 1))
                v.tensor_tensor(wlo[:, s, 0:cols], raw[:, s, 0:cols], whi[:, s, 0:cols].bitcast(F32), ALU.subtract
                                ).then_inc(lo_split, 1)

            def used(m, s):
                dve.wait_ge(slabs_used, m * 2 + (s + 1 + PRIME))

            def link(ins):
                st.step(ins)
                st.settle()

            def coefficients(L, gain, which, one):
                m = mod[:, L, which * KT:(which + 1) * KT, :]
                if one:
                    link(v.tensor_scalar(coef[:, :, :], m, 1.0, None, ALU.add))
                    link(v.tensor_tensor(coef[:, :, :], coef[:, :, :], over(prm(L, gain), NM), ALU.mult))
                else:
                    link(v.tensor_tensor(coef[:, :, :], m, over(prm(L, gain), NM), ALU.mult))

            def by_seq(v4):
                return v4.rearrange("p k (b t) -> p k b t", b=NB)

            def times_rstd_samples(src):
                link(v.tensor_tensor(smp, src[:, :, SEQ:T], rstd[:, SEQ:T].unsqueeze(1).broadcast_to([P, KT, NS]),
                                     ALU.mult))
                link(v.tensor_tensor(by_seq(smp), by_seq(smp), over(coef[:, :, 1:NM], TS), ALU.mult))

            def modulate(L, nth, idx, gain, shift, scale):
                if nth or L:
                    dve.wait_ge(x_ready, (2 * L + nth) * KT)
                coefficients(L, gain, scale, True)
                dve.wait_ge(rstd_ready, NORMS * L + idx + 1)
                times_rstd_samples(x)
                v.tensor_tensor(by_seq(smp), by_seq(smp), over(mod[:, L, shift * KT:(shift + 1) * KT, 1:NM], TS),
                                ALU.add).then_inc(smp_ready, 1)
                base = (2 * L + nth)
                with dve.Fori(0, KT) as k:
                    v.tensor_tensor(sq[:, k, 0:SEQ], x[:, k, 0:SEQ], rstd[:, 0:SEQ], ALU.mult).then_inc(t_ready, 1)
                dve.wait_ge(hhi_ready, base * (KT + 1) + 1)
                link(v.tensor_tensor(h_lo[:, :, SEQ:T], smp, h_hi[:, :, SEQ:T].bitcast(F32), ALU.subtract))
                with dve.Fori(0, KT) as k:
                    dve.wait_ge(hhi_ready, k + (base * (KT + 1) + 2))
                    v.tensor_tensor(h_lo[:, k, 0:SEQ], sq[:, k, 0:SEQ], h_hi[:, k, 0:SEQ].bitcast(F32), ALU.subtract
                                    ).then_inc(h_ready, 1)

            def residual(L, idx, gain, gate, src, old):
                coefficients(L, gain, gate, False)
                dve.wait_ge(rstd_ready, NORMS * L + idx + 1)
                times_rstd_samples(src)
                link(v.tensor_tensor(x[:, :, SEQ:T], smp, old[:, :, SEQ:T], ALU.add))
                with dve.Fori(0, KT) as k:
                    outer = st.enter(k, 1)
                    link(v.tensor_tensor(sq[:, k, 0:SEQ], src[:, k, 0:SEQ], rstd[:, 0:SEQ], ALU.mult))
                    v.scalar_tensor_tensor(x[:, k, 0:SEQ], sq[:, k, 0:SEQ], coef[:, k, 0:1], old[:, k, 0:SEQ],
                                           ALU.mult, ALU.add).then_inc(x_ready, 1)
                st.leave(outer, KT)

            def convolve(weights, taps, i, windows, tails, bias, before):
                n = weights.shape[-1] // taps
                o = 4 - taps
                st.step(v.tensor_copy(windows[:, i, :, taps - 1:taps - 1 + TS], seqs(ub[:, 3 + SEQ:3 + T])))
                st.step(v.tensor_copy(tails[:, i, :], ub[:, 3 + SEQ - (taps - 1):3 + SEQ]))
                before()
                st.settle()
                for j in range(taps):
                    w = weights[:, bass.ds(i + j * n, 1)]
                    a_p, a_s = ub[:, o + j:o + j + SEQ], windows[:, i, :, j:j + TS]
                    if j == 0:
                        st.step(v.tensor_scalar(acc[:, 0:SEQ], a_p, w, bias, ALU.mult, ALU.add))
                        st.step(v.tensor_scalar(seqs(acc[:, SEQ:T]), a_s, w, bias, ALU.mult, ALU.add))
                    else:
                        st.settle()
                        st.step(v.scalar_tensor_tensor(acc[:, 0:SEQ], a_p, w, acc[:, 0:SEQ], ALU.mult, ALU.add))
                        last = v.scalar_tensor_tensor(seqs(acc[:, SEQ:T]), a_s, w, seqs(acc[:, SEQ:T]), ALU.mult,
                                                      ALU.add)
                        if j < taps - 1:
                            st.step(last)
                last.then_inc(conv_done, 1)

            dve.sem_inc(lo_split, PRIME)
            dve.sem_inc(taken[0], 1)
            dve.sem_inc(taken[1], 1)
            dve.sem_inc(conv_done, 1)
            dve.sem_inc(xbc_ready, 1)
            dve.sem_inc(hid_ready, 1)
            for s in range(2):
                lo(0, s, SLAB)
            dve.wait_ge(params_in, 64)

            def ada_take(L, n, g, b):
                dve.wait_ge(ada_used, n * 4 + (4 + PRIME))
                dve.wait_ge(ada_out, n + 1)
                rows = ps[0:32, b, :].rearrange("p (t r b) -> p t r b", t=4, r=4)
                for r in range(4):
                    st.step(v.transpose(modT[32 * r:32 * r + 32, :, :], rows[:, :, r, :]))
                st.settle()
                v.tensor_tensor(mod[:, L, bass.ds(g * 4, 4), :], modT[:, :, 0:NM],
                                over(prm(L, "ada_b")[:, bass.ds(g * 4, 4)], NM), ALU.add).then_inc(ada_out, 1)

            def ada_takes(L, place):
                for n in MOD_AT.get((L, place), ()):
                    ada_take(n // (NG // 2), n, n % (NG // 2), mod_bank(place, n))
                    dve.wait_ge(ada_out, n + 2)

            with dve.Fori(0, 4) as n:
                outer = st.enter(n, 4)
                ada_take(0, n, n, 6)
            st.leave(outer, 4)
            for L in range(DEPTH):
                first = FIRST[L]
                if L == 0:
                    dve.wait_ge(ada_out, 4 + 1)
                    dve.wait_ge(x_in, 16)
                else:
                    dve.wait_ge(ada_out, 22 + 1)
                modulate(L, 0, PRE_MIX, "pre_mix", 0, 1)
                ada_takes(L, "pre_mix")
                dve.wait_ge(h_ready, (2 * L + 1) * KT)
                link(v.memset(ub[:, 0:3], 0.0))
                link(v.memset(sp_x, 0.0))
                dve.wait_ge(dt_done, L + 1)
                bias = prm(L, "dt_bias").unsqueeze(1).broadcast_to([P, NCH, HEADS])
                st.step(v.tensor_tensor(sp_x[:, 0:NCH, :], ps[:, 5, 0:64].rearrange("p (c h) -> p c h", c=NCH), bias,
                                        ALU.add))
                link(v.tensor_tensor(sp_x[0:NS, NCH, :], ps[0:NS, 5, 64:80], prm(L, "dt_bias")[0:NS], ALU.add))
                v.scalar_tensor_tensor(sp_e, sp_x, -1.0, sp_x, ALU.mult, ALU.min).then_inc(dt_x, 1)
                dve.wait_ge(dt_e, 2 * L + 1)
                v.tensor_scalar(sp_t, sp_e, 1.0, None, ALU.add).then_inc(dt_x, 1)
                dve.wait_ge(dt_x, 2 * L + 2)
                link(v.tensor_scalar(sp_r, sp_t, -1.0, None, ALU.add))
                link(v.tensor_tensor(sp_e, sp_e, sp_r, ALU.subtract))
                link(v.reciprocal(sp_r, sp_t))
                link(v.tensor_tensor(sp_e, sp_e, sp_r, ALU.mult))
                dve.wait_ge(dt_e, 2 * L + 2)
                link(v.tensor_tensor(sp_e, sp_e, sp_l, ALU.add))
                link(v.scalar_tensor_tensor(dt_t, sp_x, 0.0, sp_e, ALU.max, ALU.add))
                link(v.scalar_tensor_tensor(dA, dt_t, -1.0, expA.unsqueeze(1).broadcast_to([P, 5, HEADS]), ALU.mult,
                                            ALU.mult))
                v.tensor_tensor(dA_s[0:NS], dA[0:NS, NCH:NCH + 1, :].broadcast_to([NS, NB, HEADS]),
                                over(con("in_seq")[0:NS], HEADS), ALU.mult).then_inc(dA_ready, 1)
                dve.wait_ge(windows_in, 32 * (L + 1))
                with dve.Fori(0, N_XBC // 2) as i:
                    outer = st.enter(i, 2 * 9)
                    for s in range(2):
                        t = i * 2 + s
                        dve.wait_ge(taken[s], i + (first["xbc"] + 2))
                        convolve(prm(L, "convb"), 4, t, usb, nbp, prm(L, "convb_b")[:, bass.ds(t, 1)],
                                 lambda: dve.wait_ge(xbc_ready, t + (XBC * L + 1)))
                        lo(i + (first["xbc"] + 1), s, SLAB)
                st.leave(outer, N_XBC // 2)
                if L:
                    dve.wait_ge(spill_out, 16 * L)
                link(v.memset(wend, 0.0))
                dve.wait_ge(cum_done, L + 1)
                st.step(v.tensor_copy(cum[:, 0:NCH, :], ps[:, 7, 0:64].rearrange("p (c h) -> p c h", c=NCH)))
                link(v.tensor_copy(cum[0:NS, NCH, :], ps[0:NS, 7, 128:144]))
                st.step(v.tensor_tensor(wend[:, 0:NCH, :], ps[:, 7, 64:128].rearrange("p (c h) -> p c h", c=NCH),
                                        cum[:, 0:NCH, :], ALU.subtract))
                v.tensor_tensor(wend[0:NS, NCH, :], ps[0:NS, 7, 144:160], cum[0:NS, NCH, :], ALU.subtract
                                ).then_inc(cum_x, 1)
                dve.wait_ge(cum_e, L + 1)
                link(v.tensor_tensor(wend, wend, dt_t, ALU.mult))
                ada_takes(L, "cum")
                dve.wait_ge(smp_pe, L + 1)
                st.step(v.tensor_copy(Bt_s[0:NS], ps[0:NS, 6, 0:256]))
                st.step(v.tensor_tensor(cbm_s[0:NS], ps[0:NS, 6, 256:320].rearrange("p (g t) -> p g t", g=GROUPS),
                                        con("tri_seq")[0:NS].unsqueeze(1).broadcast_to([NS, GROUPS, NS]), ALU.mult))
                xT_s = ps[0:NS, 4:6, :].rearrange("p a (h d) -> p (a h) d", d=HD)
                st.step(v.tensor_tensor(xdt_s[0:NS].rearrange("p (h d) -> p h d", h=HEADS), xT_s,
                                        over(dt_t[0:NS, NCH, :], HD), ALU.mult))
                st.step(v.tensor_tensor(xe_s[0:NS].rearrange("p (h d) -> p h d", h=HEADS), xT_s,
                                        over(wend[0:NS, NCH, :], HD), ALU.mult))
                link(v.tensor_tensor(E_s[0:NS], ps[0:NS, 7, :].rearrange("p (h t) -> p h t", h=HEADS),
                                     over(cum[0:NS, NCH, :], NS), ALU.subtract))
                v.tensor_scalar(E_s[0:NS], E_s[0:NS], 0.0, None, ALU.min).then_inc(smp_seg, 1)
                dve.wait_ge(smp_act, 2 * (L + 1))
                Eg = E_s[0:NS].rearrange("p (g h) t -> p g h t", g=GROUPS)
                v.tensor_tensor(Eg, Eg, cbm_s[0:NS].unsqueeze(2).broadcast_to([NS, GROUPS, GH, NS]), ALU.mult
                                ).then_inc(smp_G, 1)
                dve.wait_ge(smp_y, L + 1)
                st.step(v.tensor_copy(yd_s, ps[:, 6, 0:KT * NS].rearrange("p (k t) -> p k t", k=KT)))
                v.memset(S, 0.0).then_inc(units_free, 1)
                dve.wait_ge(units_free, (KT + 1) * L + 1)
                with dve.Fori(0, KT) as i:
                    outer = st.enter(i, 7 + 7 + 2 + 2 + 3)
                    c, h0 = i // 2, (i % 2) * GH
                    mA, mB = i * 2 + first["mix"], i * 2 + (first["mix"] + 1)
                    lo(mB, 0, SLAB)
                    dve.wait_ge(chunk_pe, i + (KT * L + 2))
                    st.step(v.tensor_scalar(Bm[0:NS], Bt_s[0:NS], con("in_seq")[0:NS, bass.ds(i, 1)], None, ALU.mult))
                    st.step(v.tensor_copy(Bt, ps[:, 7, 0:NST]))
                    st.step(v.tensor_copy(yo_s[:, :, bass.ds(i * TS, TS)],
                                          ps[:, 7, 256:288].rearrange("p (k t) -> p k t", k=KT)))
                    st.step(v.tensor_tensor(cbm, ps[:, 7, NST:2 * NST], tri, ALU.mult))
                    xT_c = ps[:, 6, :].rearrange("p (h d) -> p h d", h=GH)
                    st.step(v.tensor_tensor(xdt.rearrange("p (h d) -> p h d", h=GH), xT_c,
                                            over(dt_t[:, c, bass.ds(h0, GH)], HD), ALU.mult))
                    st.step(v.tensor_tensor(xe.rearrange("p (h d) -> p h d", h=GH), xT_c,
                                            over(wend[:, c, bass.ds(h0, GH)], HD), ALU.mult))
                    link(v.tensor_tensor(E, ps[:, 4:6, :].rearrange("p a (h t) -> p (a h) t", h=4),
                                         over(cum[:, c, bass.ds(h0, GH)], CH), ALU.subtract))
                    v.tensor_scalar(E, E, 0.0, None, ALU.min).then_inc(chunk_seg, 1)
                    dve.wait_ge(chunk_act, i * 2 + (2 + 2 * KT * L))
                    v.tensor_tensor(E, E, cbm.unsqueeze(1).broadcast_to([P, GH, CH]), ALU.mult).then_inc(chunk_G, 1)
                    used(mA, 1)
                    dve.wait_ge(taken[0], mA + 2)
                    v.tensor_tensor(halves(ub[:, 3:3 + T]), bank(1), halves(gc_s), ALU.mult).then_inc(taken[1], 1)
                    dve.wait_ge(taken[1], mA + 2)
                    convolve(prm(L, "conva"), 3, i, usa, nap, 0.0, lambda: None)
                    lo(mB, 1, SLAB)
                    used(mB, 0)
                    dve.wait_ge(conv_done, i + (XBC + 2 + (XBC + KT) * L))
                    v.tensor_tensor(halves(ya_f), bank(0), halves(acc), ALU.mult).then_inc(taken[0], 1)
                    dve.wait_ge(yahi_ready, i + (KT * L + 1))
                    v.tensor_tensor(ya_lo[:, i, :], ya_f, ya_hi[:, i, :].bitcast(F32), ALU.subtract
                                    ).then_inc(ya_ready, 1)
                    lo(mB + 1, 0, SLAB)
                    dve.wait_ge(seq_pe, i + (KT * L + 1))
                    for g in range(GROUPS):
                        S0g = S0[:, g, :].rearrange("p (h d) -> p h d", h=GH)
                        st.step(v.tensor_tensor(S0g, S0g, over(dec_s[:, i, g * GH:(g + 1) * GH], HD), ALU.mult))
                    st.settle()
                    for g in range(GROUPS):
                        v.tensor_tensor(S0[:, g, :], S0[:, g, :], ps[:, 4 + g, :], ALU.add).then_inc(seq_new, 1)
                    Sg = S[:, i % 2, :].rearrange("p (h d) -> p h d", h=GH)
                    link(v.tensor_tensor(Sg, Sg, over(dec[:, c, bass.ds(h0, GH)], HD), ALU.mult))
                    st.step(v.tensor_tensor(S[:, i % 2, :], S[:, i % 2, :], ps[:, 6, :], ALU.add))
                    for j in range(GT):
                        y = mix[:, (i % 2) * GT + j, bass.ds(c * CH, CH)]
                        ins = v.scalar_tensor_tensor(y, y, prm(L, "d_skip")[:, bass.ds((i % 2) * GT + j, 1)],
                                                     ps[:, 7, j * CH:(j + 1) * CH], ALU.mult, ALU.add)
                        if j < GT - 1:
                            st.step(ins)
                    ins.then_inc(units_free, 1)
                    lo(mB + 1, 1, SLAB)
                st.leave(outer, KT)
                dve.wait_ge(units_free, (KT + 1) * (L + 1))
                ec = ecum_s.rearrange("p (k a) t -> p k a t", a=2)
                st.step(v.tensor_tensor(yt[0:HD], yo_s[0:HD], ec[0:HD, :, 0, :], ALU.mult))
                st.step(v.tensor_tensor(yt[HD:P], yo_s[HD:P], ec[HD:P, :, 1, :], ALU.mult))
                link(v.tensor_tensor(xs[:, :, SEQ:T], xs[:, :, SEQ:T], over(prm(L, "d_skip"), NS), ALU.mult))
                link(v.tensor_tensor(yt, yt, yd_s, ALU.add))
                link(v.tensor_tensor(xs[:, :, SEQ:T], xs[:, :, SEQ:T], yt, ALU.add))
                with dve.Fori(0, KT) as k:
                    dve.wait_ge(gz_ready, k + (KT * L + 1))
                    v.tensor_tensor(mix[:, k, :], mix[:, k, :], mix[:, k + XBC, :], ALU.mult).then_inc(gy_ready, 1)
                dve.wait_ge(gy_ready, KT * (L + 1))
                ada_takes(L, "gate")
                for g in range(GROUPS):
                    dve.wait_ge(rstd_ready, NORMS * L + GATE + 1 + g)
                    with dve.Fori(0, GT // 2) as i:
                        for s in range(2):
                            k = i * 2 + s + GT * g
                            v.scalar_tensor_tensor(yb_t[s], mix[:, k, :], prm(L, "ssd_norm")[:, bass.ds(k, 1)], rg[g],
                                                   ALU.mult, ALU.mult).then_inc(ybf_ready, 1)
                            dve.wait_ge(ybhi_ready, k + (KT * L + 1))
                            v.tensor_tensor(h_lo[:, k, :], yb_t[s], h_hi[:, k, :].bitcast(F32), ALU.subtract
                                            ).then_inc(yb_ready, 1)
                            lo(i + (first["outA"] + 1 + GT // 2 * g), s, SLAB)
                for s in range(2):
                    dve.wait_ge(taken[s], first["outB"] + 1)
                with dve.Fori(0, KT // 2) as i:
                    for s in range(2):
                        used(i + first["outB"], s)
                        m_k = halves(x[:, i * 2 + s, :])
                        v.tensor_tensor(m_k, m_k, bank(s), ALU.add).then_inc(taken[s], 1)
                        lo(i + (first["outB"] + 1), s, SLAB)
                dve.wait_ge(x_back, 16 * (L + 1))
                residual(L, POST_MIX, "post_mix", 2, x, z)
                ada_takes(L, "post_mix")
                modulate(L, 1, PRE_FFN, "pre_ffn", 3, 4)
                ada_takes(L, "pre_ffn")
                if L:
                    dve.wait_ge(h_ready, (2 * L + 2) * KT)
                    link(v.memset(pr, 0.0))
                    dve.wait_ge(logits_done, 1)
                    st.step(v.tensor_copy(pr[:, 0:NCH, :], ps[:, 7, 0:32].rearrange("p (c e) -> p c e", c=NCH)))
                    link(v.tensor_copy(pr[0:NS, NCH, :], ps[0:NS, 7, 32:40]))
                    link(v.tensor_reduce(pm, pr, axis=AX_X, op=ALU.max))
                    v.tensor_tensor(pr, pr, over(pm, NE), ALU.subtract).then_inc(router_x, 1)
                    dve.wait_ge(router_e, 1)
                    link(v.tensor_reduce(pm, pr, axis=AX_X, op=ALU.add))
                    link(v.reciprocal(pm, pm))
                    link(v.tensor_tensor(pr, pr, over(pm, NE), ALU.mult))
                    before = con("before").rearrange("p (e j) -> p e j", e=NE)
                    with dve.Fori(0, NCH + 1) as c:
                        outer = st.enter(c, 5)
                        other = pr[:, bass.ds(c, 1), :].broadcast_to([P, NE, NE])
                        own = pr[:, c, :].unsqueeze(2).broadcast_to([P, NE, NE])
                        st.step(v.tensor_tensor(cmp, other, own, ALU.is_gt))
                        link(v.tensor_tensor(cmq, other, own, ALU.is_equal))
                        link(v.tensor_tensor(cmq, cmq, before, ALU.mult))
                        link(v.tensor_tensor(cmp, cmp, cmq, ALU.add))
                        link(v.tensor_reduce(rank[:, c, :], cmp, axis=AX_X, op=ALU.add))
                    st.leave(outer, NCH + 1)
                    link(v.tensor_scalar(rank, rank, 2.0, None, ALU.is_lt))
                    link(v.tensor_tensor(comb[:, :, :], rank, pr, ALU.mult))
                    link(v.tensor_reduce(pm, comb[:, :, :], axis=AX_X, op=ALU.add))
                    link(v.reciprocal(pm, pm))
                    link(v.tensor_tensor(comb[:, :, :], comb[:, :, :], over(pm, NE), ALU.mult))
                link(v.memset(f[:, :, :], 0.0))

                def expert(e, last):
                    m0 = e * EP + first["exp"]
                    tiles = (e + sum(NEXP[:L])) * FT

                    def gate_up(j, cols):
                        m = m0 + j
                        dve.wait_ge(taken[0], m + 2)
                        if L:
                            dve.wait_ge(cbr_ready, e * 2 + 2)
                            link(v.tensor_tensor(ta, ta, cbr, ALU.mult))
                        lo(m + 1, 0, cols)
                        used(m, 1)
                        dve.wait_ge(hid_ready, tiles + j + 1)
                        v.tensor_tensor(halves(tb), bank(1), halves(ta), ALU.mult).then_inc(taken[1], 1)
                        lo(m + 1, 1, cols)
                        dve.wait_ge(hidhi_ready, tiles + j + 1)
                        v.tensor_tensor(hid_lo[:, j, :], tb, hid_hi[:, j, :].bitcast(F32), ALU.subtract
                                        ).then_inc(hid_ready, 1)

                    if L:
                        v.tensor_tensor(diag, ident.unsqueeze(1).broadcast_to([P, 5, P]),
                                        comb[:, :, bass.ds(e, 1)].broadcast_to([P, 5, P]), ALU.mult
                                        ).then_inc(diag_ready, 1)
                    with dve.Fori(0, FT - 1) as j:
                        outer = st.enter(j, 1 if L else 0)
                        gate_up(j, SLAB)
                    st.leave(outer, FT - 1)
                    gate_up(FT - 1, SLABMAX)

                    def down(j, cols):
                        for s in range(2):
                            dve.wait_ge(hid_ready, tiles + (FT + 1))
                            used(m0 + FT + j, s)
                            f_k = halves(f[:, j * 2 + s, :])
                            v.tensor_tensor(f_k, f_k, bank(s), ALU.add).then_inc(taken[s], 1)
                            if cols:
                                lo(m0 + FT + 1 + j, s, cols)
                        if L == 0:
                            ada_take(1, e * (N_DOWN // 2) + j + NG // 2, e * (N_DOWN // 2) + j, 6)

                    with dve.Fori(0, N_DOWN // 2 - 1) as j:
                        outer = st.enter(j, 0 if L else 4)
                        down(j, SLABMAX)
                    st.leave(outer, N_DOWN // 2 - 1)
                    down(N_DOWN // 2 - 1, 0 if last else SLAB)

                with dve.Fori(0, NEXP[L] - 1) as e:
                    outer2 = st.enter(e, FT if L else 4 * N_DOWN // 2)
                    expert(e, False)
                st.leave(outer2, NEXP[L] - 1)
                expert(NEXP[L] - 1, L == DEPTH - 1)
                residual(L, POST_FFN, "post_ffn", 5, f[:, :, :], x)
                ada_takes(L, "post_ffn")

        @block.tensor
        def _(pe):
            mm = nc.tensor.matmul

            def slab(m, s, kt, a_hi, a_lo):
                pe.wait_ge(lo_split, m * 2 + (s + 1 + PRIME))
                pe.wait_ge(taken[s], m + 1)
                n = 0
                for k in range(kt):
                    for w, a in ((whi, a_hi), (whi, a_lo), (wlo, a_hi)):
                        for half in range(2):
                            ins = mm(ps[:, 2 * s + half, 0:HALF], w[:, s, k * P:(k + 1) * P],
                                     a[:, k, half * HALF:(half + 1) * HALF], start=(n < 2), stop=(n >= 6 * kt - 2))
                            n += 1
                ins.then_inc(slabs_used, 1)

            def ada_group(n, b, strict=True):
                pe.wait_ge(ada_out, n + (1 if strict else 0))
                for q in range(4):
                    pe.wait_ge(ada_landed[q % 2], n * 32 + (16 * (q // 2) + 16))
                    for k in range(2):
                        ins = mm(ps[0:32, b, :], cond[:, 2 * q + k, :], adaw[:, q % 2, 512 * k:512 * (k + 1)],
                                 start=(q + k == 0), stop=(q + k == 4))
                    ins.then_inc(ada_used, 1)

            def ada_groups(L, place):
                for n in MOD_AT.get((L, place), ()):
                    ada_group(n, mod_bank(place, n), n % 2 == 0)

            def sums_of(L, idx, src, ks, base):
                to = sums(idx)
                for n, k in enumerate(ks):
                    pe.wait_ge(sq_ready, 5 * KT * L + base + n + 1)
                    for half in range(2):
                        ins = mm(to[:, half, :], ones, src(k)[:, half * HALF:(half + 1) * HALF], start=(n == 0),
                                 stop=(n == len(ks) - 1))
                ins.then_inc(stat_done, 1)

            def by_token(to, n, weights):
                for c in range(NCH + 1):
                    rows = CH if c < NCH else NS
                    for part in range(2):
                        h = (h_hi, h_lo)[part]
                        for k in range(KT):
                            ins = mm(to[0:rows, n * c:n * (c + 1)], h[:, k, c * CH:c * CH + rows].bitcast(F32),
                                     weights[:, n * k:n * (k + 1)], start=(part + k == 0),
                                     stop=(part == 1 and k == KT - 1))
                return ins

            pe.sem_inc(slabs_used, PRIME)
            pe.sem_inc(ada_used, PRIME)
            pe.sem_inc(ada_out, 1)
            pe.wait_ge(cond_ready, 1)
            with pe.Fori(0, 4) as n:
                ada_group(n, 6)
            for L in range(DEPTH):
                first = FIRST[L]
                if L:
                    pe.wait_ge(ada_out, 21 + 2)
                sums_of(L, PRE_MIX, lambda k: sq[:, k, :], range(KT), SQ[PRE_MIX])
                ada_groups(L, "pre_mix")
                pe.wait_ge(h_ready, (2 * L + 1) * KT)
                by_token(ps[:, 5, :], HEADS, prm(L, "w_dt")).then_inc(dt_done, 1)
                with pe.Fori(0, N_XBC // 2) as i:
                    for s in range(2):
                        slab(i + first["xbc"], s, KT, h_hi, h_lo)
                pe.wait_ge(dA_ready, L + 1)
                dA_p = dA[:, 0:NCH, :].rearrange("p c h -> p (c h)")
                mm(ps[:, 7, 0:64], tri, dA_p, start=True, stop=True)
                mm(ps[:, 7, 64:128], ones, dA_p, start=True, stop=True)
                mm(ps[0:NS, 7, 128:144], con("tri_seq")[0:NS], dA[0:NS, NCH, :], start=True, stop=True)
                mm(ps[0:NS, 7, 144:160], con("same_seq")[0:NS], dA[0:NS, NCH, :], start=True, stop=True)
                mm(ps[:, 7, 160:288], con("ones")[0:NS].to_broadcast([NS, P]), dA_s[0:NS].rearrange("p b h -> p (b h)"), start=True, stop=True
                   ).then_inc(cum_done, 1)
                ada_groups(L, "cum")
                pe.wait_ge(xbc_ready, XBC * (L + 1) + 1)
                pe.wait_ge(cum_e, L + 1)
                if L == 0:
                    pe.wait_ge(ada_out, 6 + 2)
                for k in range(KT):
                    nc.tensor.transpose(ps[0:NS, 4 + k // GT, (k % GT) * P:(k % GT + 1) * P], mix[:, k, SEQ:T], ident)
                for g in range(GROUPS):
                    nc.tensor.transpose(ps[0:NS, 6, g * P:(g + 1) * P], mix[:, B0 + g, SEQ:T], ident)
                for g in range(GROUPS):
                    mm(ps[0:NS, 6, 256 + NS * g:256 + NS * (g + 1)], mix[:, B0 + g, SEQ:T], mix[:, C0 + g, SEQ:T],
                       start=True, stop=True)
                for h in range(HEADS):
                    ins = mm(ps[:, 7, NS * h:NS * (h + 1)], dA[0:NS, NCH, h:h + 1].to_broadcast([NS, P]),
                             con("tri_seq")[0:NS], start=True, stop=True)
                ins.then_inc(smp_pe, 1)
                pe.wait_ge(smp_G, L + 1)
                for h in range(HEADS):
                    a = HD * (h % 2)
                    ins = mm(ps[a:a + HD, 6, (h // 2) * NS:(h // 2 + 1) * NS], xdt_s[0:NS, h * HD:(h + 1) * HD],
                             E_s[0:NS, h, :], start=True, stop=True)
                ins.then_inc(smp_y, 1)
                if L == 0:
                    pe.sem_inc(chunk_pe, 1)
                with pe.Fori(0, NCH) as c:
                    for g in range(GROUPS):
                        i = c * 2 + g
                        mA, mB = i * 2 + first["mix"], i * 2 + (first["mix"] + 1)
                        slab(mA, 0, KT, h_hi, h_lo)
                        pe.wait_ge(staged, i + (KT * L + 1))
                        pe.wait_ge(units_free, i + ((KT + 1) * L + 1))
                        for j in range(GT):
                            nc.tensor.transpose(ps[:, 6, j * P:(j + 1) * P], x_st[j], ident)
                        nc.tensor.transpose(ps[:, 7, 0:NST], B_st, ident)
                        for gg in range(GROUPS):
                            pe.wait_ge(seq_in[gg], i * 16 + (16 + 16 * (NB + 1) * L))
                        for k in range(KT):
                            mm(ps[:, 7, 256 + TS * k:256 + TS * (k + 1)], S0[:, k // GT, (k % GT) * P:(k % GT + 1) * P],
                               mix[:, C0 + k // GT, bass.ds(i * TS + SEQ, TS)], start=True, stop=True)
                        mm(ps[:, 7, NST:2 * NST], B_st, mix[:, C0 + g, bass.ds(c * CH, CH)], start=True, stop=True)
                        for h in range(GH):
                            ins = mm(ps[:, 4 + h // 4, (h % 4) * CH:(h % 4 + 1) * CH],
                                     dA_st[:, h:h + 1].to_broadcast([P, P]), tri, start=True, stop=True)
                        ins.then_inc(chunk_pe, 1)
                        slab(mA, 1, KT, h_hi, h_lo)
                        slab(mB, 0, KT, h_hi, h_lo)
                        pe.wait_ge(chunk_G, i + (KT * L + 1))
                        pe.wait_ge(chunk_Ce, i + (KT * L + 1))
                        for h in range(GH):
                            a = HD * (h % 2)
                            to = ps[a:a + HD, 7, (h // 2) * CH:(h // 2 + 1) * CH]
                            mm(to, xdt[:, h * HD:(h + 1) * HD], E[:, h, :], start=True, stop=False)
                            mm(to, S[:, g, h * HD:(h + 1) * HD], Ce[:, h, :], start=False, stop=True)
                        mm(ps[:, 6, :], Bt, xe, start=True, stop=True).then_inc(chunk_y, 1)
                        for gg in range(GROUPS):
                            ins = mm(ps[:, 4 + gg, :], Bm[0:NS, gg * NST:(gg + 1) * NST],
                                     xe_s[0:NS, gg * GH * HD:(gg + 1) * GH * HD], start=True, stop=True)
                        ins.then_inc(seq_pe, 1)
                        slab(mB, 1, KT, h_hi, h_lo)
                pe.wait_ge(ya_ready, KT * (L + 1))
                for s in range(2):
                    slab(first["outA"], s, KT, ya_hi, ya_lo)
                ada_groups(L, "gate")
                for g in range(GROUPS):
                    if L == 0 and g == 1:
                        pe.wait_ge(ada_out, 7 + 2)
                    sums_of(L, GATE + g, lambda k: z[:, k, :], range(GT * g, GT * (g + 1)), SQ[GATE] + GT * g)
                with pe.Fori(1, KT // 2) as i:
                    for s in range(2):
                        slab(i + first["outA"], s, KT, ya_hi, ya_lo)
                pe.wait_ge(yb_ready, KT * (L + 1))
                with pe.Fori(0, KT // 2) as i:
                    for s in range(2):
                        slab(i + first["outB"], s, KT, h_hi, h_lo)
                sums_of(L, POST_MIX, lambda k: sq[:, k, :], range(KT), SQ[POST_MIX])
                pe.wait_ge(rstd_ready, NORMS * L + POST_MIX + 1)
                ada_groups(L, "post_mix")
                sums_of(L, PRE_FFN, lambda k: sq[:, k, :], range(KT), SQ[PRE_FFN])
                ada_groups(L, "pre_ffn")
                pe.wait_ge(h_ready, (2 * L + 2) * KT)
                if L:
                    by_token(ps[:, 7, :], NE, router).then_inc(logits_done, 1)

                def expert(e):
                    m0 = e * EP + first["exp"]
                    if L:
                        pe.wait_ge(diag_ready, e + 1)
                        mm(ps[:, 4, :], ones, diag[:, 0:NCH, :].rearrange("p c t -> p (c t)"), start=True, stop=True)
                        mm(ps[:, 5, 0:NS], ones, diag[:, NCH, 0:NS], start=True, stop=True
                           ).then_inc(combb_done, 1)
                    with pe.Fori(0, FT) as j:
                        slab(m0 + j, 0, KT, h_hi, h_lo)
                        slab(m0 + j, 1, KT, h_hi, h_lo)
                    with pe.Fori(0, N_DOWN // 2) as j:
                        for s in range(2):
                            pe.wait_ge(hid_ready, (e + (sum(NEXP[:L]) + 1)) * FT + 1)
                            slab(m0 + FT + j, s, FT, hid_hi, hid_lo)
                        if L == 0:
                            ada_group(e * (N_DOWN // 2) + j + NG // 2, 6)

                with pe.Fori(0, NEXP[L]) as e:
                    expert(e)
                if L == 0:
                    pe.wait_ge(ada_out, 19 + 2)
                sums_of(L, POST_FFN, lambda k: sq[:, k, :], range(KT), SQ[POST_FFN])
                ada_groups(L, "post_ffn")


def kernel(**inputs):
    import concourse.bacc as _bacc
    from concourse.bass_utils import run_bass_kernel_spmd as _run

    a = {k: np.asarray(v) for k, v in inputs.items()}

    def tiles(w):
        *lead, k, n = w.shape
        w = w.reshape(*lead, k // P, P, n // P, P)
        d = len(lead)
        return np.ascontiguousarray(np.moveaxis(w, (d + 2, d + 1, d, d + 3), (d, d + 1, d + 2, d + 3))).reshape(
            *lead, n // P, P, k)

    def by_feature(v):
        v = v.reshape(*v.shape[:-1], v.shape[-1] // P, P)
        return np.ascontiguousarray(np.moveaxis(v, (-1, -2), (0, 1)))

    xall = np.concatenate([a["x_prompt"].reshape(SEQ, D), a["x_sample"].reshape(NS, D)])
    call = np.concatenate([a["c_prompt"], a["c_sample"], np.zeros((32 - NM, D), np.float32)])
    pack = []
    w_dt0 = a["w_in"].shape[-1] - HEADS
    for L in range(DEPTH):
        cols = [by_feature(a["ada_b"][L]), by_feature(a["norm_pre_mix"][L]), by_feature(a["norm_post_mix"][L]),
                by_feature(a["norm_pre_ffn"][L]), by_feature(a["norm_post_ffn"][L]),
                np.moveaxis(by_feature(a["conva_w"][L]), 2, 1), np.moveaxis(by_feature(a["convb_w"][L]), 2, 1),
                by_feature(a["convb_b"][L]), by_feature(a["ssd_norm"][L]),
                by_feature(np.broadcast_to(a["d_skip"][L][:, None], (HEADS, HD)).reshape(-1)),
                a["w_in"][L][:, w_dt0:].reshape(KT, P, HEADS).transpose(1, 0, 2),
                np.broadcast_to(a["dt_bias"][L], (P, HEADS)), np.broadcast_to(a["a_log"][L], (P, HEADS))]
        pack += [c.reshape(P, -1) for c in cols]
    s, q = np.arange(P)[:, None], np.arange(P)[None, :]
    s2, q2 = s, np.arange(NS)[None, :]
    e2 = np.arange(NE)
    const = [(s <= q), (s == q), np.ones((P, 1)), (s2 // TS == q2 // TS) & (s2 <= q2), (s2 // TS == q2 // TS),
             (s // TS == np.arange(NB)[None, :]), np.full((P, 1), EPS),
             np.broadcast_to((e2[None, :] < e2[:, None]).reshape(1, -1), (P, NE * NE))]
    w_in = tiles(a["w_in"][:, :, :w_dt0])
    c = KT
    ff = a["ffd_w_gate"].shape[-1] // 2

    def gate_up(wg, wu):
        g, u = tiles(wg), tiles(wu)
        return np.stack([g, u], 2).reshape(g.shape[0], -1, P, D)

    def states(v):
        v = v.reshape(DEPTH, NB, v.shape[2], -1, P)
        return np.ascontiguousarray(v.transpose(0, 4, 3, 1, 2)).reshape(DEPTH, P, -1)

    split = a["ffd_w_gate"][0].reshape(D, 2, ff).transpose(1, 0, 2)
    splitu = a["ffd_w_up"][0].reshape(D, 2, ff).transpose(1, 0, 2)
    w_out = tiles(a["w_out"]).reshape(DEPTH, KT, P, 2, D).transpose(0, 3, 1, 2, 4)
    arrays = {
        "xT": by_feature(xall).reshape(P, -1),
        "cT": by_feature(call).reshape(P, -1),
        "pack": np.concatenate(pack, 1),
        "const": np.concatenate([v.astype(np.float32) for v in const], 1),
        "w_router": a["moe_router"][0].reshape(KT, P, NE).transpose(1, 0, 2).reshape(P, -1),
        "s_conva": states(a["state_conva"]),
        "s_convb": states(a["state_convb"]),
        "s_ssm": a["state_ssm"].reshape(DEPTH, NB, GROUPS, GH * HD, NST).transpose(0, 1, 2, 4, 3),
        "w_ada": a["ada_w"].reshape(DEPTH, 4, 2, P, NG // 2, 512).transpose(0, 4, 1, 3, 2, 5).reshape(NG, 4, P, 2 * 512),
        "w_xbc": w_in[:, 4 * c:],
        "w_mix": np.stack([w_in[:, c:2 * c], w_in[:, 2 * c:3 * c], w_in[:, 0:c], w_in[:, 3 * c:4 * c]], 2).reshape(
            DEPTH, 4 * c, P, D),
        "w_out": w_out.reshape(DEPTH, 2 * KT, P, D),
        "w_gu0": gate_up(split, splitu),
        "w_dn0": tiles(a["ffd_w_down"][0].reshape(2, ff, D)),
        "w_gu1": gate_up(a["moe_w_gate"][0], a["moe_w_up"][0]),
        "w_dn1": tiles(a["moe_w_down"][0]),
    }
    arrays = {k: np.ascontiguousarray(v) for k, v in arrays.items()}
    outs = {"yT": (P, KT * T), "o_ap": (DEPTH, P, KT * 2), "o_bp": (DEPTH, P, XBC * 3),
            "o_sp": (DEPTH, P, HEADS * HD), "o_as": (DEPTH, P, KT * NB * 2), "o_bs": (DEPTH, P, XBC * NB * 3),
            "o_ss": (DEPTH, NB, GROUPS, P, GH * HD)}
    nc = _bacc.Bacc("TRN2", target_bir_lowering=False, num_devices=1)
    args = [nc.dram_tensor(k, v.shape, mybir.dt.from_np(v.dtype), kind="ExternalInput").ap() for k, v in arrays.items()]
    args += [nc.dram_tensor(k, v, F32, kind="ExternalOutput").ap() for k, v in outs.items()]
    hybrid_decoder(nc, *args)
    r = _run(nc, [arrays], core_ids=[0]).results[0]
    y = r["yT"].reshape(P, KT, T).transpose(2, 1, 0).reshape(T, D)

    def rows(v, n, tile):
        v = v.reshape(DEPTH, P, tile, *n)
        return np.ascontiguousarray(np.moveaxis(v, (2, 1), (-2, -1))).reshape(DEPTH, *n, tile * P)

    return (y[:SEQ].reshape(1, SEQ, D), y[SEQ:].reshape(NB, TS, D),
            rows(r["o_ap"], (1, 2), KT), rows(r["o_bp"], (1, 3), XBC),
            np.ascontiguousarray(r["o_sp"].reshape(DEPTH, 1, P, HEADS, HD).transpose(0, 1, 3, 4, 2)),
            rows(r["o_as"], (NB, 2), KT), rows(r["o_bs"], (NB, 3), XBC),
            np.ascontiguousarray(r["o_ss"].reshape(DEPTH, NB, GROUPS, P, GH, HD).transpose(0, 1, 2, 4, 5, 3)).reshape(
                DEPTH, NB, HEADS, HD, NST))
```

```python
from contextlib import ExitStack

import numpy as np

import concourse.bass as bass
from concourse import mybir

ALU = mybir.AluOpType
ACT = mybir.ActivationFunctionType
F32 = mybir.dt.float32
F32R = mybir.dt.float32r
AX_X = mybir.AxisListType.X

P = 128
D = 1024
KT = D // P
SEQ = 512
NB, TS = 8, 4
NS = NB * TS
T = SEQ + NS
HALF = T // 2
DEPTH = 2
HEADS, HD, NST = 16, 64, 128
GROUPS = 2
GH = HEADS // GROUPS
GT = KT // GROUPS
CH = 128
NCH = SEQ // CH
XBC = 12
FT = 11
NE = 8
NEXP = (2, NE)
CAP = 256
CAPT = CAP // P
MAXU = (2 * T + NE * (CAP - 1)) // CAP
SLAB = KT * P
SLABMAX = FT * P
EPS = 1e-6
MODS = 6 * KT
NM = 1 + NB
NG = 2 * MODS // 4
MOD_AT = {(0, "pre_mix"): (4, 5), (0, "cum"): (6,), (0, "gate"): (7,), (0, "post_mix"): (8, 9), (0, "pre_ffn"): (10, 11),
          (0, "post_ffn"): (20, 21), (1, "pre_mix"): (22, 23)}


def columns(*fields):
    at, out = 0, {}
    for name, n in fields:
        out[name] = (at, at + n)
        at += n
    return out, at


PACK, NPACK = columns(("ada_b", MODS), ("pre_mix", KT), ("post_mix", KT), ("pre_ffn", KT), ("post_ffn", KT),
                      ("conva", 3 * KT), ("convb", 4 * XBC), ("convb_b", XBC), ("ssd_norm", KT), ("d_skip", KT),
                      ("w_dt", KT * HEADS), ("dt_bias", HEADS), ("a_log", HEADS))
CONST, NCONST = columns(("tri", P), ("ident", P), ("ones", 1), ("tri_seq", NS), ("same_seq", NS), ("in_seq", NB),
                        ("eps", 1), ("before", NE * NE))

N_XBC, N_MIX, N_GU, N_DOWN = XBC, 4 * KT, 2 * FT, KT
EP = (N_GU + N_DOWN) // 2
LAYER_PAIRS = (N_XBC + N_MIX + 2 * KT) // 2 + NEXP[0] * EP


class Tally:

    def __init__(self, sem, engine):
        self.sem, self.engine, self.base, self.n = sem, engine, 0, 0

    def step(self, ins):
        ins.then_inc(self.sem, 1)
        self.n += 1

    def settle(self):
        self.engine.wait_ge(self.sem, self.base + self.n)

    def enter(self, i, each):
        outer = (self.base, self.n, each)
        self.base, self.n = self.base + self.n + i * each, 0
        return outer

    def leave(self, outer, times):
        base, n, each = outer
        assert self.n == each, (self.n, each)
        self.base, self.n = base, n + times * each


def hybrid_decoder(nc, xT, cT, pack, const, count, w_router, s_conva, s_convb, s_ssm, w_ada, w_xbc, w_mix, w_out, w_gu0, w_dn0, w_gu1,
                   w_dn1, yT, o_ap, o_bp, o_sp, o_as, o_bs, o_ss):
    x_spill = nc.dram_tensor("x_spill", [P, KT * T], F32).ap()
    w_gu, w_dn = (w_gu0, w_gu1), (w_dn0, w_dn1)
    with ExitStack() as ctx:
        def sb(name, shape, dt=F32, where=ctx):
            return where.enter_context(nc.sbuf_tensor(name, shape, dt))

        def sem(name):
            return ctx.enter_context(nc.semaphore(name))

        raw = sb("raw", [P, 2, SLABMAX])
        whi = sb("whi", [P, 2, SLABMAX], F32R)
        wlo = sb("wlo", [P, 2, SLABMAX], F32R)
        adaw = sb("adaw", [P, 2, SLAB])
        cst = sb("cst", [P, NCONST])
        par = sb("par", [P, DEPTH, NPACK])
        cond = sb("cond", [P, KT, 32])
        modT = sb("modT", [P, 4, 32])
        router = sb("router", [P, KT * NE])
        mod = sb("mod", [P, DEPTH, MODS, NM])
        coef = sb("coef", [P, KT, NM])
        comb = sb("comb", [P, 5, NE])
        usb = sb("usb", [P, XBC, NB, 3 + TS])
        h_hi = sb("h_hi", [P, KT, T], F32R)
        h_lo = sb("h_lo", [P, KT, T], F32R)
        xreg = sb("xreg", [P, KT * T])
        wreg = sb("wreg", [P, 6480])
        with ExitStack() as mixer:
            ya_hi = sb("ya_hi", [P, KT, T], F32R, mixer)
            ya_lo = sb("ya_lo", [P, KT, T], F32R, mixer)
            mix = sb("mix", [P, XBC + KT, T], F32, mixer)
            usa = sb("usa", [P, KT, NB, 2 + TS], F32, mixer)
        with ExitStack() as experts:
            hid_hi = sb("hid_hi", [P, FT, T], F32R, experts)
            hid_lo = sb("hid_lo", [P, FT, T], F32R, experts)
            f = sb("f", [P, KT, T], F32, experts)
        with ExitStack() as routed:
            htok_hi = sb("htok_hi", [P, NCH + 1, D], F32R, routed)
            htok_lo = sb("htok_lo", [P, NCH + 1, D], F32R, routed)
            G = sb("G", [P, NCH + 1, CAP], F32R, routed)
            Gt = sb("Gt", [P, CAPT, T], F32R, routed)
            hidu_hi = sb("hidu_hi", [P, FT, CAP], F32R, routed)
            hidu_lo = sb("hidu_lo", [P, FT, CAP], F32R, routed)
            place = sb("place", [P, NCH + 1, NE], F32, routed)
            before_c = sb("before_c", [P, NCH + 2, NE], F32, routed)
            n_units = sb("n_units", [P, NE], F32, routed)
            end_unit = sb("end_unit", [P, NE], F32, routed)
            is_expert = sb("is_expert", [P, MAXU + 1, NE], F32, routed)
            of_unit = sb("of_unit", [P, MAXU + 1], F32, routed)
            first_of = sb("first_of", [P, MAXU + 1], F32, routed)
            own8 = sb("own8", [P, NCH + 1, NE], F32, routed)
            own_place = sb("own_place", [P, NCH + 1], F32, routed)
            own_comb = sb("own_comb", [P, NCH + 1], F32, routed)
            cj = sb("cj", [P, CAPT], F32, routed)
            units = sb("units", [P, MAXU + 2], mybir.dt.int32, routed)
            iota = sb("iota", [P, CAP], F32, routed)
        ps = ctx.enter_context(nc.psum_tensor("ps", [P, 8, 512], F32))

        def con(name):
            a, b = CONST[name]
            return cst[:, a:b]

        def prm(layer, name):
            a, b = PACK[name]
            return par[:, layer, a:b]

        def view(buf, at, *shape):
            v = buf[:, at:at + int(np.prod(shape))]
            if len(shape) == 2:
                v = v.rearrange("p (a b) -> p a b", a=shape[0])
            if len(shape) == 3:
                v = v.rearrange("p (a b c) -> p a b c", a=shape[0], b=shape[1])
            return v

        def halves(v):
            return v.rearrange("p (a b) -> p a b", a=2)

        def seqs(v):
            return v.rearrange("p (b t) -> p b t", b=NB)

        def over(v, n):
            return v.unsqueeze(len(v.shape)).broadcast_to([*v.shape, n])

        ident, tri, ones = con("ident"), con("tri"), con("ones").to_broadcast([P, P])
        x = view(xreg, 0, KT, T)
        xs = mix[:, 0:KT, :]
        z = mix[:, XBC:XBC + KT, :]
        B0, C0 = KT, KT + GROUPS
        E = view(xreg, 0, GH, CH)
        Ce = view(xreg, 1024, GH, CH)
        S = view(xreg, 2048, GROUPS, GH * HD)
        xdt = view(xreg, 3072, GH * HD)
        xe = view(xreg, 3584, GH * HD)
        Bt = view(xreg, 4096, NST)
        cbm = view(xreg, 4224, CH)
        x_st = [raw[:, j // 2, SLAB + CH * (j % 2):SLAB + CH * (j % 2 + 1)] for j in range(GT)]
        B_st = raw[:, 0, SLAB + 2 * CH:SLAB + 3 * CH]
        dA_st = raw[:, 1, SLAB + 2 * CH:SLAB + 2 * CH + GH]
        yt = view(xreg, 0, KT, NS)
        E_s = view(xreg, 0, HEADS, NS)
        xdt_s = view(xreg, 1024, D)
        cbm_s = view(xreg, 4224, GROUPS, NS)
        S0 = view(wreg, 0, GROUPS, GH * HD)
        xe_s = view(wreg, 1024, D)
        Bt_s = view(wreg, 2048, 2 * NST)
        Bm = view(wreg, 2304, 2 * NST)
        ecum_s = view(wreg, 2560, HEADS, NS)
        yo_s = view(wreg, 3072, KT, NS)
        yd_s = view(wreg, 3328, KT, NS)
        ub = view(wreg, 3584, 3 + T)
        acc = view(wreg, 4131, T)
        gc_s = view(wreg, 4675, T)
        ya_f = view(wreg, 5219, T)
        dt_t = view(wreg, 5763, 5, HEADS)
        dA = view(wreg, 5843, 5, HEADS)
        cum = view(wreg, 5923, 5, HEADS)
        wend = view(wreg, 6003, 5, HEADS)
        dec = view(wreg, 6083, NCH, HEADS)
        dec_s = view(wreg, 6147, NB, HEADS)
        dA_s = view(wreg, 6275, NB, HEADS)
        nap = view(wreg, 6403, KT, 2)
        nbp = view(wreg, 6419, XBC, 3)
        expA = view(wreg, 6455, HEADS)
        sp_x = view(wreg, 4131, 5, HEADS)
        sp_e = view(wreg, 4211, 5, HEADS)
        sp_t = view(wreg, 4291, 5, HEADS)
        sp_l = view(wreg, 4371, 5, HEADS)
        sp_r = view(wreg, 4451, 5, HEADS)
        yb_t = (acc, ub[:, 0:T])
        rg = (gc_s, ya_f)
        sq = view(wreg, 0, KT, T)
        rstd = view(wreg, KT * T, T)
        ta = view(wreg, KT * T + T, T)
        tb = view(wreg, KT * T + 2 * T, T)
        smp = view(wreg, KT * T + 3 * T, KT, NS)
        f_routed = sq
        ta_u = view(wreg, KT * T, CAP)
        tb_u = view(wreg, KT * T + CAP, CAP)
        yu = view(wreg, KT * T + 2 * CAP, 2, CAP)
        hu_hi, hu_lo = h_hi[:, :, 0:CAP], h_lo[:, :, 0:CAP]
        ye_hi, ye_lo = h_hi[:, 0:2, HALF:HALF + CAP], h_lo[:, 0:2, HALF:HALF + CAP]
        pr = view(wreg, 1024, 5, NE)
        pm = view(wreg, 1064, 5)
        rank = view(wreg, 1072, 5, NE)
        cmp = view(wreg, 1152, NE, NE)
        cmq = view(wreg, 1216, NE, NE)

        PRIME = 2
        params_in, x_in = sem("params_in"), sem("x_in")
        raw_landed = [sem("raw_landed0"), sem("raw_landed1")]
        hi_split = sem("hi_split")
        lo_split = sem("lo_split")
        slabs_used = sem("slabs_used")
        taken = [sem("taken0"), sem("taken1")]
        ada_landed = [sem("ada_landed0"), sem("ada_landed1")]
        ada_used = sem("ada_used")
        ada_out = sem("ada_out")
        cond_ready = sem("cond_ready")
        sq_ready, stat_done, rstd_ready = sem("sq_ready"), sem("stat_done"), sem("rstd_ready")
        smp_ready, t_ready, hhi_ready, h_ready = sem("smp_ready"), sem("t_ready"), sem("hhi_ready"), sem("h_ready")
        x_ready = sem("x_ready")
        act_steps, dve_steps = sem("act_steps"), sem("dve_steps")
        dt_done, dt_x, dt_e, dA_ready = sem("dt_done"), sem("dt_x"), sem("dt_e"), sem("dA_ready")
        conv_done, xbc_ready = sem("conv_done"), sem("xbc_ready")
        yahi_ready, ya_ready = sem("yahi_ready"), sem("ya_ready")
        cum_done, cum_x, cum_e, cum_ready = sem("cum_done"), sem("cum_x"), sem("cum_e"), sem("cum_ready")
        smp_pe, smp_seg, smp_act, smp_G, smp_y, smp_done = (sem("smp_pe"), sem("smp_seg"), sem("smp_act"),
                                                            sem("smp_G"), sem("smp_y"), sem("smp_done"))
        chunk_pe, chunk_seg, chunk_act, chunk_G, chunk_Ce = (sem("chunk_pe"), sem("chunk_seg"), sem("chunk_act"),
                                                             sem("chunk_G"), sem("chunk_Ce"))
        chunk_y, seq_pe, seq_new = sem("chunk_y"), sem("seq_pe"), sem("seq_new")
        seq_in = [sem("seq_in0"), sem("seq_in1")]
        seq_out = [sem("seq_out0"), sem("seq_out1")]
        gz_ready, gy_ready, ybf_ready, ybhi_ready, yb_ready = (sem("gz_ready"), sem("gy_ready"), sem("ybf_ready"),
                                                               sem("ybhi_ready"), sem("yb_ready"))
        windows_in, windows_out, state_out, x_back, spill_out = (sem("windows_in"), sem("windows_out"),
                                                                 sem("state_out"), sem("x_back"), sem("spill_out"))
        hidhi_ready, hid_ready = sem("hidhi_ready"), sem("hid_ready")
        logits_done, router_x, router_e, comb_ready = (sem("logits_done"), sem("router_x"), sem("router_e"),
                                                       sem("comb_ready"))
        y_out, staged, units_free = sem("y_out"), sem("staged"), sem("units_free")
        iota_in, chosen, counted, table_ready = sem("iota_in"), sem("chosen"), sem("counted"), sem("table_ready")
        tok_turned, tok_taken = sem("tok_turned"), sem("tok_taken")
        unit_steps, G_ready, G_turned, Gt_ready = sem("unit_steps"), sem("G_ready"), sem("G_turned"), sem("Gt_ready")
        hi_gathered, lo_gathered = sem("hi_gathered"), sem("lo_gathered")
        hi_taken, lo_taken = sem("hi_taken"), sem("lo_taken")
        cj_done, cj_ready, y_turned = sem("cj_done"), sem("cj_ready"), sem("y_turned")
        yehi_ready, ye_ready, scattered = sem("yehi_ready"), sem("ye_ready"), sem("scattered")
        f_added, units_over = sem("f_added"), sem("units_over")

        FIRST, USES = [], []
        pair = 0
        for L in range(DEPTH):
            FIRST.append({"xbc": pair, "mix": pair + N_XBC // 2, "outA": pair + (N_XBC + N_MIX) // 2,
                          "outB": pair + (N_XBC + N_MIX + KT) // 2, "exp": pair + (N_XBC + N_MIX) // 2 + KT})
            pair += LAYER_PAIRS

        def bank(s):
            return ps[:, 2 * s:2 * s + 2, 0:HALF]

        NORMS = 6
        PRE_MIX, GATE, POST_MIX, PRE_FFN, POST_FFN = 0, 1, 3, 4, 5
        SQ = {PRE_MIX: 0, GATE: 8, POST_MIX: 16, PRE_FFN: 24, POST_FFN: 32}

        def mod_bank(place, n):
            return {"cum": 6, "gate": 4, "post_ffn": 4 + n % 2}.get(place, 6 + n % 2)

        def sums(idx):
            b = 4 + 2 * (idx % 2)
            return ps[:, b:b + 2, 0:HALF]

        block = ctx.enter_context(nc.Block())

        @block.sync
        def _(sp):
            sp.dma_start(cond[:, :, :].rearrange("p k b -> p (k b)"), cT).then_inc(params_in, 16)
            sp.dma_start(cst[:, :], const).then_inc(params_in, 16)
            sp.dma_start(par[:, :, :].rearrange("p l n -> p (l n)"), pack).then_inc(params_in, 16)
            sp.dma_start(router[:, :], w_router).then_inc(params_in, 16)
            sp.dma_start(xreg[:, :], xT).then_inc(x_in, 16)

            def load_pair(m, src, cols):
                for s in range(2):
                    sp.wait_ge(lo_split, m * 2 + s + 1)
                    sp.dma_start(raw[:, s, 0:cols], src(s)).then_inc(raw_landed[s], 16)

            for L in range(DEPTH):
                first = FIRST[L]
                with sp.Fori(0, N_XBC // 2) as i:
                    load_pair(i + first["xbc"], lambda s: w_xbc[L, i * 2 + s], SLAB)
                with sp.Fori(0, N_MIX // 2) as i:
                    load_pair(i + first["mix"], lambda s: w_mix[L, i * 2 + s], SLAB)
                with sp.Fori(0, KT) as i:
                    load_pair(i + first["outA"], lambda s: w_out[L, i * 2 + s], SLAB)

                def expert(u, e):
                    with sp.Fori(0, FT) as j:
                        load_pair(u * EP + j + first["exp"], lambda s: w_gu[L][e, j * 2 + s], SLAB)
                    with sp.Fori(0, N_DOWN // 2) as j:
                        load_pair(u * EP + j + (FT + first["exp"]), lambda s: w_dn[L][e, j * 2 + s], SLABMAX)

                if L == 0:
                    with sp.Fori(0, NEXP[0]) as e:
                        expert(e, e)
                else:
                    sp.wait_ge(table_ready, 1)
                    n = sp.value_load(units[0:1, 0:1], min_val=1, max_val=MAXU)
                    with sp.Fori(0, n) as u:
                        expert(u, sp.value_load(units[0:1, bass.ds(u + 1, 1)], min_val=0, max_val=NE - 1))
            sp.wait_ge(x_ready, DEPTH * 2 * KT)
            sp.dma_start(yT, xreg[:, :]).then_inc(y_out, 16)
            sp.wait_ge(y_out, 16)

        @block.gpsimd
        def _(pool):
            def ada_load(n):
                for q in range(4):
                    pool.wait_ge(ada_used, n * 4 + (q + 1))
                    pool.dma_start(adaw[:, q % 2, :], w_ada[n, q]).then_inc(ada_landed[q % 2], 16)

            def ada_loads(L, place):
                for n in MOD_AT.get((L, place), ()):
                    ada_load(n)

            with pool.Fori(0, 4) as n:
                ada_load(n)
            for L in range(DEPTH):
                if L:
                    pool.wait_ge(x_ready, 2 * KT * L)
                    pool.dma_start(x_spill, xreg[:, :]).then_inc(spill_out, 16)
                pool.dma_start(usb[:, :, :, 0:3], s_convb[L].rearrange("p (k b t) -> p k b t", k=XBC, b=NB)
                               ).then_inc(windows_in, 16)
                pool.dma_start(usa[:, :, :, 0:2], s_conva[L].rearrange("p (k b t) -> p k b t", k=KT, b=NB)
                               ).then_inc(windows_in, 16)
                ada_loads(L, "pre_mix")
                ada_loads(L, "cum")
                pool.wait_ge(h_ready, (2 * L + 1) * KT)
                for g in range(GROUPS):
                    pool.dma_start(S0[:, g, :], s_ssm[L, 0, g]).then_inc(seq_in[g], 16)
                pool.wait_ge(xbc_ready, XBC * (L + 1) + 1)
                pool.wait_ge(dA_ready, L + 1)
                with pool.Fori(0, KT) as i:
                    pool.wait_ge(chunk_pe, i + (KT * L + 1))
                    for j in range(GT):
                        nc.gpsimd.tensor_copy(x_st[j], mix[:, (i % 2) * GT + j, bass.ds((i // 2) * CH, CH)])
                    nc.gpsimd.tensor_copy(B_st, mix[:, i % 2 + B0, bass.ds((i // 2) * CH, CH)])
                    nc.gpsimd.tensor_copy(dA_st, dA[:, i // 2, bass.ds((i % 2) * GH, GH)]).then_inc(staged, 1)
                    pool.wait_ge(chunk_act, i * 2 + (1 + 2 * KT * L))
                    nc.gpsimd.tensor_tensor(Ce, Ce, mix[:, i % 2 + C0, bass.ds((i // 2) * CH, CH)].unsqueeze(
                        1).broadcast_to([P, GH, CH]), ALU.mult).then_inc(chunk_Ce, 1)
                    for g in range(GROUPS):
                        pool.wait_ge(seq_new, i * 2 + (g + 1 + 2 * NB * L))
                        pool.dma_start(o_ss[L, i, g], S0[:, g, :]).then_inc(seq_out[g], 16)
                    for g in range(GROUPS):
                        pool.wait_ge(seq_out[g], i * 16 + (16 + 16 * NB * L))
                        pool.dma_start(S0[:, g, :], s_ssm[L, (i + 1) % NB, g]).then_inc(seq_in[g], 16)
                ada_loads(L, "gate")
                pool.wait_ge(ya_ready, KT * (L + 1))
                pool.wait_ge(units_free, (KT + 1) * (L + 1))
                pool.dma_start(o_sp[L], xreg[:, 2048:3072]).then_inc(state_out, 16)
                pool.dma_start(o_as[L].rearrange("p (k b t) -> p k b t", k=KT, b=NB), usa[:, :, :, TS:TS + 2]
                               ).then_inc(windows_out, 16)
                pool.dma_start(o_bs[L].rearrange("p (k b t) -> p k b t", k=XBC, b=NB), usb[:, :, :, TS:TS + 3]
                               ).then_inc(windows_out, 16)
                pool.dma_start(o_ap[L], nap.rearrange("p k t -> p (k t)")).then_inc(windows_out, 16)
                pool.dma_start(o_bp[L], nbp.rearrange("p k t -> p (k t)")).then_inc(windows_out, 16)
                pool.wait_ge(stat_done, NORMS * L + GATE + 2)
                if L:
                    pool.wait_ge(spill_out, 16 * L)
                pool.dma_start(z.rearrange("p k t -> p (k t)"), x_spill if L else xT).then_inc(x_back, 16)
                ada_loads(L, "post_mix")
                ada_loads(L, "pre_ffn")
                pool.wait_ge(windows_out, 64 * (L + 1))
                if L:
                    pool.wait_ge(x_ready, (2 * L + 1) * KT)
                    pool.dma_start(iota[:, :], count).then_inc(iota_in, 16)
                if L == 0:
                    with pool.Fori(0, N_DOWN) as n:
                        ada_load(n + NG // 2)
                ada_loads(L, "post_ffn")

        @block.scalar
        def _(act):
            st = Tally(act_steps, act)

            def hi(m, s, cols):
                act.wait_ge(raw_landed[s], m * 16 + 16)
                act.wait_ge(slabs_used, m * 2 + (s + 1))
                nc.scalar.copy(whi[:, s, 0:cols], raw[:, s, 0:cols]).then_inc(hi_split, 1)

            def used(m, s):
                act.wait_ge(slabs_used, m * 2 + (s + 1 + PRIME))

            def make_rstd(idx, n, to):
                act.wait_ge(stat_done, idx + 1)
                st.step(nc.scalar.activation(halves(to), sums(idx % NORMS), ACT.Ln, scale=1.0 / n, bias=con("eps")))
                st.settle()
                nc.scalar.activation(to, to, ACT.Exp, scale=-0.5).then_inc(rstd_ready, 1)

            def modulate(L, nth, shift):
                act.wait_ge(smp_ready, 2 * L + nth + 1)
                nc.scalar.copy(h_hi[:, :, SEQ:T], smp).then_inc(hhi_ready, 1)
                base = (2 * L + nth) * KT
                outer = None
                with act.Fori(0, KT) as k:
                    outer = st.enter(k, 1)
                    act.wait_ge(t_ready, k + (base + 1))
                    st.step(nc.scalar.activation(sq[:, k, 0:SEQ], sq[:, k, 0:SEQ], ACT.Identity,
                                                 scale=coef[:, k, 0:1], bias=mod[:, L, k + shift, 0:1]))
                    st.settle()
                    nc.scalar.copy(h_hi[:, k, 0:SEQ], sq[:, k, 0:SEQ]).then_inc(hhi_ready, 1)
                st.leave(outer, KT)

            act.wait_ge(params_in, 64)
            nc.scalar.activation(cond[:, :, :], cond[:, :, :], ACT.Silu).then_inc(cond_ready, 1)
            for s in range(2):
                hi(0, s, SLAB)
            act.wait_ge(x_in, 16)
            for L in range(DEPTH):
                first = FIRST[L]
                with act.Fori(0, KT) as k:
                    if L:
                        act.wait_ge(x_ready, k + (2 * KT * L - KT + 1))
                    nc.scalar.activation(sq[:, k, :], x[:, k, :], ACT.Square).then_inc(sq_ready, 1)
                make_rstd(NORMS * L + PRE_MIX, D, rstd)
                modulate(L, 0, 0)
                act.wait_ge(dt_x, 2 * L + 1)
                st.step(nc.scalar.activation(expA, prm(L, "a_log"), ACT.Exp))
                st.settle()
                nc.scalar.activation(sp_e, sp_e, ACT.Exp).then_inc(dt_e, 1)
                act.wait_ge(dt_x, 2 * L + 2)
                nc.scalar.activation(sp_l, sp_t, ACT.Ln).then_inc(dt_e, 1)
                with act.Fori(0, N_XBC // 2) as i:
                    for s in range(2):
                        t = i * 2 + s
                        used(i + first["xbc"], s)
                        act.wait_ge(conv_done, t + (1 + (XBC + KT) * L))
                        nc.scalar.copy(halves(ub[:, 3:3 + T]), bank(s)).then_inc(taken[s], 1)
                        hi(i + (first["xbc"] + 1), s, SLAB)
                        act.wait_ge(conv_done, t + (2 + (XBC + KT) * L))
                        nc.scalar.activation(mix[:, t, :], acc, ACT.Silu).then_inc(xbc_ready, 1)
                act.wait_ge(cum_done, L + 1)
                act.wait_ge(cum_x, L + 1)
                st.step(nc.scalar.activation(dec, ps[:, 7, 64:128].rearrange("p (c h) -> p c h", c=NCH), ACT.Exp))
                st.step(nc.scalar.activation(dec_s, ps[:, 7, 160:288].rearrange("p (c h) -> p c h", c=NB), ACT.Exp))
                nc.scalar.activation(wend, wend, ACT.Exp).then_inc(cum_e, 1)
                act.wait_ge(smp_seg, L + 1)
                nc.scalar.activation(ecum_s, ps[:, 7, :].rearrange("p (h t) -> p h t", h=HEADS), ACT.Exp
                                     ).then_inc(smp_act, 1)
                nc.scalar.activation(E_s[0:NS], E_s[0:NS], ACT.Exp).then_inc(smp_act, 1)
                with act.Fori(0, KT) as i:
                    mA, mB = i * 2 + first["mix"], i * 2 + (first["mix"] + 1)
                    used(mA, 0)
                    nc.scalar.copy(halves(gc_s), bank(0)).then_inc(taken[0], 1)
                    hi(mB, 0, SLAB)
                    act.wait_ge(chunk_seg, i + (KT * L + 1))
                    nc.scalar.activation(Ce, ps[:, 4:6, :].rearrange("p a (h t) -> p (a h) t", h=4), ACT.Exp
                                         ).then_inc(chunk_act, 1)
                    nc.scalar.activation(E, E, ACT.Exp).then_inc(chunk_act, 1)
                    used(mA, 1)
                    hi(mB, 1, SLAB)
                    act.wait_ge(taken[0], mB + 2)
                    nc.scalar.copy(ya_hi[:, i, :], ya_f).then_inc(yahi_ready, 1)
                    hi(mB + 1, 0, SLAB)
                    used(mB, 1)
                    nc.scalar.copy(halves(mix[:, i + XBC, :]), bank(1)).then_inc(taken[1], 1)
                    hi(mB + 1, 1, SLAB)
                act.wait_ge(taken[1], first["outA"] + 1)
                with act.Fori(0, KT) as k:
                    nc.scalar.activation(mix[:, k + XBC, :], mix[:, k + XBC, :], ACT.Silu).then_inc(gz_ready, 1)
                with act.Fori(0, KT) as k:
                    act.wait_ge(gy_ready, k + (KT * L + 1))
                    nc.scalar.activation(mix[:, k + XBC, :], mix[:, k, :], ACT.Square).then_inc(sq_ready, 1)
                for g in range(GROUPS):
                    make_rstd(NORMS * L + GATE + g, D // GROUPS, rg[g])
                act.wait_ge(state_out, 16 * (L + 1))
                with act.Fori(0, KT // 2) as i:
                    for s in range(2):
                        used(i + first["outA"], s)
                        nc.scalar.copy(halves(x[:, i * 2 + s, :]), bank(s)).then_inc(taken[s], 1)
                        hi(i + (first["outA"] + 1), s, SLAB)
                        act.wait_ge(ybf_ready, i * 2 + (s + 1 + KT * L))
                        nc.scalar.copy(h_hi[:, i * 2 + s, :], yb_t[s]).then_inc(ybhi_ready, 1)
                for g in range(GROUPS):
                    act.wait_ge(seq_in[g], 16 * (NB + 1) * (L + 1))
                act.wait_ge(windows_out, 64 * (L + 1))
                act.wait_ge(yb_ready, KT * (L + 1))

                def second_half(i, ahead):
                    for s in range(2):
                        used(i + first["outB"], s)
                        if ahead:
                            hi(i + (first["outB"] + 1), s, SLAB)
                        act.wait_ge(taken[s], i + (first["outB"] + 2))
                        nc.scalar.activation(sq[:, i * 2 + s, :], x[:, i * 2 + s, :], ACT.Square).then_inc(sq_ready, 1)

                with act.Fori(0, KT // 2 - 1) as i:
                    second_half(i, True)
                second_half(KT // 2 - 1, L == 0)
                make_rstd(NORMS * L + POST_MIX, D, rstd)
                with act.Fori(0, KT) as k:
                    act.wait_ge(x_ready, k + (2 * KT * L + 1))
                    nc.scalar.activation(sq[:, k, :], x[:, k, :], ACT.Square).then_inc(sq_ready, 1)
                make_rstd(NORMS * L + PRE_FFN, D, rstd)
                modulate(L, 1, 3 * KT)
                if L:
                    act.wait_ge(router_x, 1)
                    nc.scalar.activation(pr, pr, ACT.Exp).then_inc(router_e, 1)

                def gate_up(m0, j, cols, ta, tb, gate, hid):
                    m = m0 + j
                    used(m, 0)
                    nc.scalar.activation(ta, gate, ACT.Silu).then_inc(taken[0], 1)
                    hi(m + 1, 0, cols)
                    used(m, 1)
                    hi(m + 1, 1, cols)
                    act.wait_ge(taken[1], m + 2)
                    nc.scalar.copy(hid[:, j, :], tb).then_inc(hidhi_ready, 1)

                if L == 0:
                    with act.Fori(0, NEXP[0]) as e:
                        m0 = e * EP + first["exp"]
                        with act.Fori(0, FT - 1) as j:
                            gate_up(m0, j, SLAB, halves(ta), tb, bank(0), hid_hi)
                        gate_up(m0, FT - 1, SLABMAX, halves(ta), tb, bank(0), hid_hi)
                        with act.Fori(0, N_DOWN // 2 - 1) as j:
                            for s in range(2):
                                used(m0 + FT + j, s)
                                hi(m0 + FT + 1 + j, s, SLABMAX)
                        for s in range(2):
                            used(m0 + (EP - 1), s)
                            hi(m0 + EP, s, SLAB)
                else:
                    for c in range(NCH + 1):
                        rows = CH if c < NCH else NS
                        for part, to in enumerate((htok_hi, htok_lo)):
                            act.wait_ge(tok_turned, 2 * c + part + 1)
                            nc.scalar.copy(to[0:rows, c, :].rearrange("p (a b) -> p a b", a=2),
                                           ps[0:rows, 2 * part:2 * part + 2, :]).then_inc(tok_taken, 1)
                    act.wait_ge(table_ready, 1)
                    n = act.value_load(units[0:1, 0:1], min_val=1, max_val=MAXU)

                    def ye_upper(u, k, s):
                        act.wait_ge(y_turned, u * KT + (k + 1))
                        nc.scalar.activation(ye_hi[:, s, :].rearrange("p (c f) -> p c f", c=CAPT)[:, 0, :],
                                             ps[:, 2 * s + 1, 0:P], ACT.Copy, scale=cj[:, 0:1])
                        nc.scalar.activation(ye_hi[:, s, :].rearrange("p (c f) -> p c f", c=CAPT)[:, 1, :],
                                             ps[:, 2 * s + 1, P:2 * P], ACT.Copy, scale=cj[:, 1:2]
                                             ).then_inc(yehi_ready, 1)

                    with act.Fori(0, n) as u:
                        m0 = u * EP + first["exp"]
                        for q in range(KT // 2):
                            act.wait_ge(hi_gathered, u * (KT // 2) + (q + 1))
                            nc.scalar.copy(hu_hi[:, 2 * q:2 * q + 2, :],
                                           ps[:, 4 + q % 2, :].rearrange("p (k t) -> p k t", k=2)
                                           ).then_inc(hi_taken, 1)
                            if q < 2:
                                hi(m0, q, SLAB)
                        act.wait_ge(G_turned, u + 1)
                        for c in range(CAPT):
                            nc.scalar.copy(Gt[:, c, 0:SEQ], ps[:, 2 * c + 1, :]).then_inc(Gt_ready, 1)
                        with act.Fori(0, FT - 1) as j:
                            gate_up(m0, j, SLAB, ta_u, tb_u, ps[:, 0, 0:CAP], hidu_hi)
                        gate_up(m0, FT - 1, SLABMAX, ta_u, tb_u, ps[:, 0, 0:CAP], hidu_hi)

                        def down(j, head, ahead):
                            for s in range(2):
                                m = m0 + FT + j
                                used(m, s)
                                nc.scalar.copy(yu[:, s, :], ps[:, 2 * s, 0:CAP]).then_inc(taken[s], 1)
                                if ahead:
                                    hi(m + 1, s, SLABMAX)
                                if s or not head:
                                    ye_upper(u, j * 2 + s - 1, 1 - s)

                        act.wait_ge(cj_ready, u + 1)
                        down(0, True, True)
                        with act.Fori(1, N_DOWN // 2 - 1) as j:
                            down(j, False, True)
                        down(N_DOWN // 2 - 1, False, False)
                        ye_upper(u, KT - 1, 1)
                if L:
                    act.wait_ge(units_over, 1)
                for k in range(KT):
                    if L == 0:
                        act.wait_ge(taken[k % 2], first["exp"] + EP * NEXP[0] - (N_DOWN // 2) + k // 2 + 2)
                        nc.scalar.activation(sq[:, k, :], f[:, k, :], ACT.Square).then_inc(sq_ready, 1)
                    else:
                        nc.scalar.activation(f[:, k, :], f_routed[:, k, :], ACT.Square).then_inc(sq_ready, 1)
                make_rstd(NORMS * L + POST_FFN, D, rstd)

        @block.vector
        def _(dve):
            st = Tally(dve_steps, dve)
            v = nc.vector

            def lo(m, s, cols):
                dve.wait_ge(hi_split, m * 2 + (s + 1))
                v.tensor_tensor(wlo[:, s, 0:cols], raw[:, s, 0:cols], whi[:, s, 0:cols].bitcast(F32), ALU.subtract
                                ).then_inc(lo_split, 1)

            def used(m, s):
                dve.wait_ge(slabs_used, m * 2 + (s + 1 + PRIME))

            def link(ins):
                st.step(ins)
                st.settle()

            def coefficients(L, gain, which, one):
                m = mod[:, L, which * KT:(which + 1) * KT, :]
                if one:
                    link(v.tensor_scalar(coef[:, :, :], m, 1.0, None, ALU.add))
                    link(v.tensor_tensor(coef[:, :, :], coef[:, :, :], over(prm(L, gain), NM), ALU.mult))
                else:
                    link(v.tensor_tensor(coef[:, :, :], m, over(prm(L, gain), NM), ALU.mult))

            def by_seq(v4):
                return v4.rearrange("p k (b t) -> p k b t", b=NB)

            def times_rstd_samples(src):
                link(v.tensor_tensor(smp, src[:, :, SEQ:T], rstd[:, SEQ:T].unsqueeze(1).broadcast_to([P, KT, NS]),
                                     ALU.mult))
                link(v.tensor_tensor(by_seq(smp), by_seq(smp), over(coef[:, :, 1:NM], TS), ALU.mult))

            def modulate(L, nth, idx, gain, shift, scale):
                if nth or L:
                    dve.wait_ge(x_ready, (2 * L + nth) * KT)
                coefficients(L, gain, scale, True)
                dve.wait_ge(rstd_ready, NORMS * L + idx + 1)
                times_rstd_samples(x)
                v.tensor_tensor(by_seq(smp), by_seq(smp), over(mod[:, L, shift * KT:(shift + 1) * KT, 1:NM], TS),
                                ALU.add).then_inc(smp_ready, 1)
                base = (2 * L + nth)
                with dve.Fori(0, KT) as k:
                    v.tensor_tensor(sq[:, k, 0:SEQ], x[:, k, 0:SEQ], rstd[:, 0:SEQ], ALU.mult).then_inc(t_ready, 1)
                dve.wait_ge(hhi_ready, base * (KT + 1) + 1)
                link(v.tensor_tensor(h_lo[:, :, SEQ:T], smp, h_hi[:, :, SEQ:T].bitcast(F32), ALU.subtract))
                with dve.Fori(0, KT) as k:
                    dve.wait_ge(hhi_ready, k + (base * (KT + 1) + 2))
                    v.tensor_tensor(h_lo[:, k, 0:SEQ], sq[:, k, 0:SEQ], h_hi[:, k, 0:SEQ].bitcast(F32), ALU.subtract
                                    ).then_inc(h_ready, 1)

            def residual(L, idx, gain, gate, src, old, scaled):
                coefficients(L, gain, gate, False)
                dve.wait_ge(rstd_ready, NORMS * L + idx + 1)
                times_rstd_samples(src)
                link(v.tensor_tensor(x[:, :, SEQ:T], smp, old[:, :, SEQ:T], ALU.add))
                with dve.Fori(0, KT) as k:
                    outer = st.enter(k, 1)
                    link(v.tensor_tensor(scaled[:, k, 0:SEQ], src[:, k, 0:SEQ], rstd[:, 0:SEQ], ALU.mult))
                    v.scalar_tensor_tensor(x[:, k, 0:SEQ], scaled[:, k, 0:SEQ], coef[:, k, 0:1], old[:, k, 0:SEQ],
                                           ALU.mult, ALU.add).then_inc(x_ready, 1)
                st.leave(outer, KT)

            def convolve(weights, taps, i, windows, tails, bias, before):
                n = weights.shape[-1] // taps
                o = 4 - taps
                st.step(v.tensor_copy(windows[:, i, :, taps - 1:taps - 1 + TS], seqs(ub[:, 3 + SEQ:3 + T])))
                st.step(v.tensor_copy(tails[:, i, :], ub[:, 3 + SEQ - (taps - 1):3 + SEQ]))
                before()
                st.settle()
                for j in range(taps):
                    w = weights[:, bass.ds(i + j * n, 1)]
                    a_p, a_s = ub[:, o + j:o + j + SEQ], windows[:, i, :, j:j + TS]
                    if j == 0:
                        st.step(v.tensor_scalar(acc[:, 0:SEQ], a_p, w, bias, ALU.mult, ALU.add))
                        st.step(v.tensor_scalar(seqs(acc[:, SEQ:T]), a_s, w, bias, ALU.mult, ALU.add))
                    else:
                        st.settle()
                        st.step(v.scalar_tensor_tensor(acc[:, 0:SEQ], a_p, w, acc[:, 0:SEQ], ALU.mult, ALU.add))
                        last = v.scalar_tensor_tensor(seqs(acc[:, SEQ:T]), a_s, w, seqs(acc[:, SEQ:T]), ALU.mult,
                                                      ALU.add)
                        if j < taps - 1:
                            st.step(last)
                last.then_inc(conv_done, 1)

            dve.sem_inc(lo_split, PRIME)
            dve.sem_inc(taken[0], 1)
            dve.sem_inc(taken[1], 1)
            dve.sem_inc(conv_done, 1)
            dve.sem_inc(xbc_ready, 1)
            dve.sem_inc(hid_ready, 1)
            for s in range(2):
                lo(0, s, SLAB)
            dve.wait_ge(params_in, 64)

            def ada_take(L, n, g, b):
                dve.wait_ge(ada_used, n * 4 + (4 + PRIME))
                dve.wait_ge(ada_out, n + 1)
                rows = ps[0:32, b, :].rearrange("p (t r b) -> p t r b", t=4, r=4)
                for r in range(4):
                    st.step(v.transpose(modT[32 * r:32 * r + 32, :, :], rows[:, :, r, :]))
                st.settle()
                v.tensor_tensor(mod[:, L, bass.ds(g * 4, 4), :], modT[:, :, 0:NM],
                                over(prm(L, "ada_b")[:, bass.ds(g * 4, 4)], NM), ALU.add).then_inc(ada_out, 1)

            def ada_takes(L, place):
                for n in MOD_AT.get((L, place), ()):
                    ada_take(n // (NG // 2), n, n % (NG // 2), mod_bank(place, n))
                    dve.wait_ge(ada_out, n + 2)

            with dve.Fori(0, 4) as n:
                outer = st.enter(n, 4)
                ada_take(0, n, n, 6)
            st.leave(outer, 4)
            for L in range(DEPTH):
                first = FIRST[L]
                if L == 0:
                    dve.wait_ge(ada_out, 4 + 1)
                    dve.wait_ge(x_in, 16)
                else:
                    dve.wait_ge(ada_out, 22 + 1)
                modulate(L, 0, PRE_MIX, "pre_mix", 0, 1)
                ada_takes(L, "pre_mix")
                dve.wait_ge(h_ready, (2 * L + 1) * KT)
                link(v.memset(ub[:, 0:3], 0.0))
                link(v.memset(sp_x, 0.0))
                dve.wait_ge(dt_done, L + 1)
                bias = prm(L, "dt_bias").unsqueeze(1).broadcast_to([P, NCH, HEADS])
                st.step(v.tensor_tensor(sp_x[:, 0:NCH, :], ps[:, 5, 0:64].rearrange("p (c h) -> p c h", c=NCH), bias,
                                        ALU.add))
                link(v.tensor_tensor(sp_x[0:NS, NCH, :], ps[0:NS, 5, 64:80], prm(L, "dt_bias")[0:NS], ALU.add))
                v.scalar_tensor_tensor(sp_e, sp_x, -1.0, sp_x, ALU.mult, ALU.min).then_inc(dt_x, 1)
                dve.wait_ge(dt_e, 2 * L + 1)
                v.tensor_scalar(sp_t, sp_e, 1.0, None, ALU.add).then_inc(dt_x, 1)
                dve.wait_ge(dt_x, 2 * L + 2)
                link(v.tensor_scalar(sp_r, sp_t, -1.0, None, ALU.add))
                link(v.tensor_tensor(sp_e, sp_e, sp_r, ALU.subtract))
                link(v.reciprocal(sp_r, sp_t))
                link(v.tensor_tensor(sp_e, sp_e, sp_r, ALU.mult))
                dve.wait_ge(dt_e, 2 * L + 2)
                link(v.tensor_tensor(sp_e, sp_e, sp_l, ALU.add))
                link(v.scalar_tensor_tensor(dt_t, sp_x, 0.0, sp_e, ALU.max, ALU.add))
                link(v.scalar_tensor_tensor(dA, dt_t, -1.0, expA.unsqueeze(1).broadcast_to([P, 5, HEADS]), ALU.mult,
                                            ALU.mult))
                v.tensor_tensor(dA_s[0:NS], dA[0:NS, NCH:NCH + 1, :].broadcast_to([NS, NB, HEADS]),
                                over(con("in_seq")[0:NS], HEADS), ALU.mult).then_inc(dA_ready, 1)
                dve.wait_ge(windows_in, 32 * (L + 1))
                with dve.Fori(0, N_XBC // 2) as i:
                    outer = st.enter(i, 2 * 9)
                    for s in range(2):
                        t = i * 2 + s
                        dve.wait_ge(taken[s], i + (first["xbc"] + 2))
                        convolve(prm(L, "convb"), 4, t, usb, nbp, prm(L, "convb_b")[:, bass.ds(t, 1)],
                                 lambda: dve.wait_ge(xbc_ready, t + (XBC * L + 1)))
                        lo(i + (first["xbc"] + 1), s, SLAB)
                st.leave(outer, N_XBC // 2)
                if L:
                    dve.wait_ge(spill_out, 16 * L)
                link(v.memset(wend, 0.0))
                dve.wait_ge(cum_done, L + 1)
                st.step(v.tensor_copy(cum[:, 0:NCH, :], ps[:, 7, 0:64].rearrange("p (c h) -> p c h", c=NCH)))
                link(v.tensor_copy(cum[0:NS, NCH, :], ps[0:NS, 7, 128:144]))
                st.step(v.tensor_tensor(wend[:, 0:NCH, :], ps[:, 7, 64:128].rearrange("p (c h) -> p c h", c=NCH),
                                        cum[:, 0:NCH, :], ALU.subtract))
                v.tensor_tensor(wend[0:NS, NCH, :], ps[0:NS, 7, 144:160], cum[0:NS, NCH, :], ALU.subtract
                                ).then_inc(cum_x, 1)
                dve.wait_ge(cum_e, L + 1)
                link(v.tensor_tensor(wend, wend, dt_t, ALU.mult))
                ada_takes(L, "cum")
                dve.wait_ge(smp_pe, L + 1)
                st.step(v.tensor_copy(Bt_s[0:NS], ps[0:NS, 6, 0:256]))
                st.step(v.tensor_tensor(cbm_s[0:NS], ps[0:NS, 6, 256:320].rearrange("p (g t) -> p g t", g=GROUPS),
                                        con("tri_seq")[0:NS].unsqueeze(1).broadcast_to([NS, GROUPS, NS]), ALU.mult))
                xT_s = ps[0:NS, 4:6, :].rearrange("p a (h d) -> p (a h) d", d=HD)
                st.step(v.tensor_tensor(xdt_s[0:NS].rearrange("p (h d) -> p h d", h=HEADS), xT_s,
                                        over(dt_t[0:NS, NCH, :], HD), ALU.mult))
                st.step(v.tensor_tensor(xe_s[0:NS].rearrange("p (h d) -> p h d", h=HEADS), xT_s,
                                        over(wend[0:NS, NCH, :], HD), ALU.mult))
                link(v.tensor_tensor(E_s[0:NS], ps[0:NS, 7, :].rearrange("p (h t) -> p h t", h=HEADS),
                                     over(cum[0:NS, NCH, :], NS), ALU.subtract))
                v.tensor_scalar(E_s[0:NS], E_s[0:NS], 0.0, None, ALU.min).then_inc(smp_seg, 1)
                dve.wait_ge(smp_act, 2 * (L + 1))
                Eg = E_s[0:NS].rearrange("p (g h) t -> p g h t", g=GROUPS)
                v.tensor_tensor(Eg, Eg, cbm_s[0:NS].unsqueeze(2).broadcast_to([NS, GROUPS, GH, NS]), ALU.mult
                                ).then_inc(smp_G, 1)
                dve.wait_ge(smp_y, L + 1)
                st.step(v.tensor_copy(yd_s, ps[:, 6, 0:KT * NS].rearrange("p (k t) -> p k t", k=KT)))
                v.memset(S, 0.0).then_inc(units_free, 1)
                dve.wait_ge(units_free, (KT + 1) * L + 1)
                with dve.Fori(0, KT) as i:
                    outer = st.enter(i, 7 + 7 + 2 + 2 + 3)
                    c, h0 = i // 2, (i % 2) * GH
                    mA, mB = i * 2 + first["mix"], i * 2 + (first["mix"] + 1)
                    lo(mB, 0, SLAB)
                    dve.wait_ge(chunk_pe, i + (KT * L + 2))
                    st.step(v.tensor_scalar(Bm[0:NS], Bt_s[0:NS], con("in_seq")[0:NS, bass.ds(i, 1)], None, ALU.mult))
                    st.step(v.tensor_copy(Bt, ps[:, 7, 0:NST]))
                    st.step(v.tensor_copy(yo_s[:, :, bass.ds(i * TS, TS)],
                                          ps[:, 7, 256:288].rearrange("p (k t) -> p k t", k=KT)))
                    st.step(v.tensor_tensor(cbm, ps[:, 7, NST:2 * NST], tri, ALU.mult))
                    xT_c = ps[:, 6, :].rearrange("p (h d) -> p h d", h=GH)
                    st.step(v.tensor_tensor(xdt.rearrange("p (h d) -> p h d", h=GH), xT_c,
                                            over(dt_t[:, c, bass.ds(h0, GH)], HD), ALU.mult))
                    st.step(v.tensor_tensor(xe.rearrange("p (h d) -> p h d", h=GH), xT_c,
                                            over(wend[:, c, bass.ds(h0, GH)], HD), ALU.mult))
                    link(v.tensor_tensor(E, ps[:, 4:6, :].rearrange("p a (h t) -> p (a h) t", h=4),
                                         over(cum[:, c, bass.ds(h0, GH)], CH), ALU.subtract))
                    v.tensor_scalar(E, E, 0.0, None, ALU.min).then_inc(chunk_seg, 1)
                    dve.wait_ge(chunk_act, i * 2 + (2 + 2 * KT * L))
                    v.tensor_tensor(E, E, cbm.unsqueeze(1).broadcast_to([P, GH, CH]), ALU.mult).then_inc(chunk_G, 1)
                    used(mA, 1)
                    dve.wait_ge(taken[0], mA + 2)
                    v.tensor_tensor(halves(ub[:, 3:3 + T]), bank(1), halves(gc_s), ALU.mult).then_inc(taken[1], 1)
                    dve.wait_ge(taken[1], mA + 2)
                    convolve(prm(L, "conva"), 3, i, usa, nap, 0.0, lambda: None)
                    lo(mB, 1, SLAB)
                    used(mB, 0)
                    dve.wait_ge(conv_done, i + (XBC + 2 + (XBC + KT) * L))
                    v.tensor_tensor(halves(ya_f), bank(0), halves(acc), ALU.mult).then_inc(taken[0], 1)
                    dve.wait_ge(yahi_ready, i + (KT * L + 1))
                    v.tensor_tensor(ya_lo[:, i, :], ya_f, ya_hi[:, i, :].bitcast(F32), ALU.subtract
                                    ).then_inc(ya_ready, 1)
                    lo(mB + 1, 0, SLAB)
                    dve.wait_ge(seq_pe, i + (KT * L + 1))
                    for g in range(GROUPS):
                        S0g = S0[:, g, :].rearrange("p (h d) -> p h d", h=GH)
                        st.step(v.tensor_tensor(S0g, S0g, over(dec_s[:, i, g * GH:(g + 1) * GH], HD), ALU.mult))
                    st.settle()
                    for g in range(GROUPS):
                        v.tensor_tensor(S0[:, g, :], S0[:, g, :], ps[:, 4 + g, :], ALU.add).then_inc(seq_new, 1)
                    Sg = S[:, i % 2, :].rearrange("p (h d) -> p h d", h=GH)
                    link(v.tensor_tensor(Sg, Sg, over(dec[:, c, bass.ds(h0, GH)], HD), ALU.mult))
                    st.step(v.tensor_tensor(S[:, i % 2, :], S[:, i % 2, :], ps[:, 6, :], ALU.add))
                    for j in range(GT):
                        y = mix[:, (i % 2) * GT + j, bass.ds(c * CH, CH)]
                        ins = v.scalar_tensor_tensor(y, y, prm(L, "d_skip")[:, bass.ds((i % 2) * GT + j, 1)],
                                                     ps[:, 7, j * CH:(j + 1) * CH], ALU.mult, ALU.add)
                        if j < GT - 1:
                            st.step(ins)
                    ins.then_inc(units_free, 1)
                    lo(mB + 1, 1, SLAB)
                st.leave(outer, KT)
                dve.wait_ge(units_free, (KT + 1) * (L + 1))
                ec = ecum_s.rearrange("p (k a) t -> p k a t", a=2)
                st.step(v.tensor_tensor(yt[0:HD], yo_s[0:HD], ec[0:HD, :, 0, :], ALU.mult))
                st.step(v.tensor_tensor(yt[HD:P], yo_s[HD:P], ec[HD:P, :, 1, :], ALU.mult))
                link(v.tensor_tensor(xs[:, :, SEQ:T], xs[:, :, SEQ:T], over(prm(L, "d_skip"), NS), ALU.mult))
                link(v.tensor_tensor(yt, yt, yd_s, ALU.add))
                link(v.tensor_tensor(xs[:, :, SEQ:T], xs[:, :, SEQ:T], yt, ALU.add))
                with dve.Fori(0, KT) as k:
                    dve.wait_ge(gz_ready, k + (KT * L + 1))
                    v.tensor_tensor(mix[:, k, :], mix[:, k, :], mix[:, k + XBC, :], ALU.mult).then_inc(gy_ready, 1)
                dve.wait_ge(gy_ready, KT * (L + 1))
                ada_takes(L, "gate")
                for g in range(GROUPS):
                    dve.wait_ge(rstd_ready, NORMS * L + GATE + 1 + g)
                    with dve.Fori(0, GT // 2) as i:
                        for s in range(2):
                            k = i * 2 + s + GT * g
                            v.scalar_tensor_tensor(yb_t[s], mix[:, k, :], prm(L, "ssd_norm")[:, bass.ds(k, 1)], rg[g],
                                                   ALU.mult, ALU.mult).then_inc(ybf_ready, 1)
                            dve.wait_ge(ybhi_ready, k + (KT * L + 1))
                            v.tensor_tensor(h_lo[:, k, :], yb_t[s], h_hi[:, k, :].bitcast(F32), ALU.subtract
                                            ).then_inc(yb_ready, 1)
                            lo(i + (first["outA"] + 1 + GT // 2 * g), s, SLAB)
                for s in range(2):
                    dve.wait_ge(taken[s], first["outB"] + 1)

                def second_half(i, ahead):
                    for s in range(2):
                        used(i + first["outB"], s)
                        m_k = halves(x[:, i * 2 + s, :])
                        v.tensor_tensor(m_k, m_k, bank(s), ALU.add).then_inc(taken[s], 1)
                        if ahead:
                            lo(i + (first["outB"] + 1), s, SLAB)

                with dve.Fori(0, KT // 2 - 1) as i:
                    second_half(i, True)
                second_half(KT // 2 - 1, L == 0)
                dve.wait_ge(x_back, 16 * (L + 1))
                residual(L, POST_MIX, "post_mix", 2, x, z, sq)
                ada_takes(L, "post_mix")
                modulate(L, 1, PRE_FFN, "pre_ffn", 3, 4)
                ada_takes(L, "pre_ffn")
                if L:
                    dve.wait_ge(h_ready, (2 * L + 2) * KT)
                    link(v.memset(pr, 0.0))
                    dve.wait_ge(logits_done, 1)
                    st.step(v.tensor_copy(pr[:, 0:NCH, :], ps[:, 7, 0:32].rearrange("p (c e) -> p c e", c=NCH)))
                    link(v.tensor_copy(pr[0:NS, NCH, :], ps[0:NS, 7, 32:40]))
                    link(v.tensor_reduce(pm, pr, axis=AX_X, op=ALU.max))
                    v.tensor_tensor(pr, pr, over(pm, NE), ALU.subtract).then_inc(router_x, 1)
                    dve.wait_ge(router_e, 1)
                    link(v.tensor_reduce(pm, pr, axis=AX_X, op=ALU.add))
                    link(v.reciprocal(pm, pm))
                    link(v.tensor_tensor(pr, pr, over(pm, NE), ALU.mult))
                    before = con("before").rearrange("p (e j) -> p e j", e=NE)
                    with dve.Fori(0, NCH + 1) as c:
                        outer = st.enter(c, 5)
                        other = pr[:, bass.ds(c, 1), :].broadcast_to([P, NE, NE])
                        own = pr[:, c, :].unsqueeze(2).broadcast_to([P, NE, NE])
                        st.step(v.tensor_tensor(cmp, other, own, ALU.is_gt))
                        link(v.tensor_tensor(cmq, other, own, ALU.is_equal))
                        link(v.tensor_tensor(cmq, cmq, before, ALU.mult))
                        link(v.tensor_tensor(cmp, cmp, cmq, ALU.add))
                        link(v.tensor_reduce(rank[:, c, :], cmp, axis=AX_X, op=ALU.add))
                    st.leave(outer, NCH + 1)
                    link(v.tensor_scalar(rank, rank, 2.0, None, ALU.is_lt))
                    link(v.tensor_tensor(comb[:, :, :], rank, pr, ALU.mult))
                    link(v.tensor_reduce(pm, comb[:, :, :], axis=AX_X, op=ALU.add))
                    link(v.reciprocal(pm, pm))
                    link(v.tensor_tensor(comb[:, :, :], comb[:, :, :], over(pm, NE), ALU.mult))
                    v.tensor_scalar(rank, rank, 1.0, None, ALU.mult).then_inc(chosen, 1)
                    dve.wait_ge(chosen, 1)
                    dve.wait_ge(iota_in, 16)
                    st.step(v.memset(place[:, :, :], 0.0))
                    link(v.memset(before_c[:, :, :], 0.0))
                    dve.wait_ge(counted, 1)
                    st.step(v.tensor_copy(place[:, 0:NCH, :], ps[:, 7, 64:96].rearrange("p (c e) -> p c e", c=NCH)))
                    st.step(v.tensor_copy(place[0:NS, NCH, :], ps[0:NS, 7, 96:104]))
                    for c in range(NCH + 1):
                        link(v.tensor_tensor(before_c[:, c + 1, :], before_c[:, c, :],
                                             ps[:, 7, 128 + NE * c:128 + NE * (c + 1)], ALU.add))
                    total = before_c[:, NCH + 1, :]
                    link(v.tensor_scalar(n_units[:, :], total, 0.0, None, ALU.is_gt))
                    for c in range(1, -(-T // CAP)):
                        link(v.tensor_scalar(end_unit[:, :], total, float(c * CAP), None, ALU.is_gt))
                        link(v.tensor_tensor(n_units[:, :], n_units[:, :], end_unit[:, :], ALU.add))
                    link(v.tensor_tensor(cmp, before, n_units[:, :].unsqueeze(1).broadcast_to([P, NE, NE]), ALU.mult))
                    link(v.tensor_reduce(end_unit[:, :], cmp, axis=AX_X, op=ALU.add))
                    link(v.tensor_scalar(own8[:, 0, :], end_unit[:, :], float(CAP), None, ALU.mult))
                    link(v.tensor_tensor(before_c[:, 0:NCH + 1, :], before_c[:, 0:NCH + 1, :],
                                         own8[:, 0:1, :].broadcast_to([P, NCH + 1, NE]), ALU.add))
                    link(v.tensor_tensor(place[:, :, :], place[:, :, :], before_c[:, 0:NCH + 1, :], ALU.add))
                    link(v.tensor_tensor(place[:, :, :], place[:, :, :], rank, ALU.mult))
                    link(v.tensor_scalar(place[:, :, :], place[:, :, :], -1.0, None, ALU.add))
                    link(v.tensor_tensor(end_unit[:, :], end_unit[:, :], n_units[:, :], ALU.add))
                    link(v.tensor_tensor(is_expert[:, :, :], end_unit[:, :].unsqueeze(1).broadcast_to([P, MAXU + 1, NE]),
                                         over(iota[:, 0:MAXU + 1], NE), ALU.is_gt))
                    link(v.tensor_reduce(of_unit[:, :], is_expert[:, :, :], axis=AX_X, op=ALU.add))
                    link(v.tensor_scalar(of_unit[:, :], of_unit[:, :], -1.0, float(NE), ALU.mult, ALU.add))
                    link(v.tensor_tensor(is_expert[:, :, :], over(of_unit[:, :], NE),
                                         iota[:, 0:NE].unsqueeze(1).broadcast_to([P, MAXU + 1, NE]), ALU.is_equal))
                    link(v.tensor_scalar(first_of[:, :], iota[:, 0:MAXU + 1], -float(CAP), None, ALU.mult))
                    st.step(v.tensor_copy(units[:, 0:1], end_unit[:, NE - 1:NE]))
                    v.tensor_copy(units[:, 1:MAXU + 2], of_unit[:, :]).then_inc(table_ready, 1)
                    link(v.memset(f_routed, 0.0))
                else:
                    link(v.memset(f[:, :, :], 0.0))

                def gate_up(m0, tiles, j, cols, ta, tb, up, hi_of, lo_of):
                    m = m0 + j
                    dve.wait_ge(taken[0], m + 2)
                    lo(m + 1, 0, cols)
                    used(m, 1)
                    dve.wait_ge(hid_ready, tiles + j + 1)
                    v.tensor_tensor(tb, up, ta, ALU.mult).then_inc(taken[1], 1)
                    lo(m + 1, 1, cols)
                    dve.wait_ge(hidhi_ready, tiles + j + 1)
                    v.tensor_tensor(lo_of[:, j, :], tb if len(tb.shape) == 2 else tb.rearrange("p a b -> p (a b)"),
                                    hi_of[:, j, :].bitcast(F32), ALU.subtract).then_inc(hid_ready, 1)

                if L == 0:
                    with dve.Fori(0, NEXP[0]) as e:
                        outer2 = st.enter(e, 4 * N_DOWN // 2)
                        m0, tiles = e * EP + first["exp"], e * FT
                        with dve.Fori(0, FT - 1) as j:
                            gate_up(m0, tiles, j, SLAB, halves(ta), halves(tb), bank(1), hid_hi, hid_lo)
                        gate_up(m0, tiles, FT - 1, SLABMAX, halves(ta), halves(tb), bank(1), hid_hi, hid_lo)

                        def down(j, cols):
                            for s in range(2):
                                dve.wait_ge(hid_ready, tiles + (FT + 1))
                                used(m0 + FT + j, s)
                                f_k = halves(f[:, j * 2 + s, :])
                                v.tensor_tensor(f_k, f_k, bank(s), ALU.add).then_inc(taken[s], 1)
                                lo(m0 + FT + 1 + j, s, cols)
                            ada_take(1, e * (N_DOWN // 2) + j + NG // 2, e * (N_DOWN // 2) + j, 6)

                        with dve.Fori(0, N_DOWN // 2 - 1) as j:
                            outer = st.enter(j, 4)
                            down(j, SLABMAX)
                        st.leave(outer, N_DOWN // 2 - 1)
                        down(N_DOWN // 2 - 1, SLAB)
                    st.leave(outer2, NEXP[0])
                    residual(L, POST_FFN, "post_ffn", 5, f[:, :, :], x, sq)
                else:
                    ut = Tally(unit_steps, dve)

                    def make_places(u):
                        for src, to in ((comb, own_comb), (place, own_place)):
                            ut.step(v.tensor_tensor(own8[:, :, :], src[:, :, :],
                                                    is_expert[:, bass.ds(u, 1), :].broadcast_to([P, NCH + 1, NE]),
                                                    ALU.mult))
                            ut.settle()
                            ut.step(v.tensor_reduce(to[:, :], own8[:, :, :], axis=AX_X, op=ALU.add))
                            ut.settle()
                        ut.step(v.tensor_scalar(own_place[:, :], own_place[:, :], first_of[:, bass.ds(u, 1)], None,
                                                ALU.add))
                        ut.settle()
                        v.tensor_tensor(G[:, :, :], iota[:, :].unsqueeze(1).broadcast_to([P, NCH + 1, CAP]),
                                        over(own_place[:, :], CAP), ALU.is_equal).then_inc(G_ready, 1)

                    def ye_rest(u, k, s):
                        dve.wait_ge(yehi_ready, u * KT + (k + 1))
                        for c in range(CAPT):
                            ins = v.scalar_tensor_tensor(ye_lo[:, s, c * P:(c + 1) * P], ps[:, 2 * s + 1, c * P:(c + 1) * P],
                                                         cj[:, c:c + 1], ye_hi[:, s, c * P:(c + 1) * P].bitcast(F32),
                                                         ALU.mult, ALU.subtract)
                        ins.then_inc(ye_ready, 1)

                    def add(u, k, s):
                        dve.wait_ge(scattered, u * KT + (k + 1))
                        dve.wait_ge(f_added, u * KT + PRIME)
                        f_k = halves(f_routed[:, k, :])
                        v.tensor_tensor(f_k, f_k, ps[:, 4 + 2 * s:6 + 2 * s, 0:HALF], ALU.add).then_inc(f_added, 1)

                    dve.sem_inc(f_added, PRIME)
                    make_places(0)
                    dve.wait_ge(table_ready, 1)
                    n = dve.value_load(units[0:1, 0:1], min_val=1, max_val=MAXU)
                    with dve.Fori(0, n) as u:
                        outer = ut.enter(u, 5)
                        m0, tiles = u * EP + first["exp"], (u + NEXP[0]) * FT
                        for q in range(KT // 2):
                            dve.wait_ge(lo_gathered, u * (KT // 2) + (q + 1))
                            v.tensor_copy(hu_lo[:, 2 * q:2 * q + 2, :],
                                          ps[:, 6 + q % 2, :].rearrange("p (k t) -> p k t", k=2)).then_inc(lo_taken, 1)
                            if q < 2:
                                lo(m0, q, SLAB)
                        dve.wait_ge(cj_done, u + 1)
                        v.tensor_copy(Gt[:, :, SEQ:T], ps[:, 6, 0:CAPT * NS].rearrange("p (c t) -> p c t", c=CAPT))
                        v.tensor_copy(cj[:, :], ps[:, 6, 128:128 + CAPT]).then_inc(cj_ready, 1)
                        with dve.Fori(0, FT - 1) as j:
                            gate_up(m0, tiles, j, SLAB, ta_u, tb_u, ps[:, 2, 0:CAP], hidu_hi, hidu_lo)
                        gate_up(m0, tiles, FT - 1, SLABMAX, ta_u, tb_u, ps[:, 2, 0:CAP], hidu_hi, hidu_lo)
                        dve.wait_ge(G_ready, u + 1)
                        make_places(u + 1)

                        def down(j, head, ahead):
                            for s in range(2):
                                if ahead:
                                    lo(m0 + FT + 1 + j, s, SLABMAX)
                                if s or not head:
                                    ye_rest(u, j * 2 + s - 1, 1 - s)
                                if not head:
                                    add(u, j * 2 + s - 2, s)

                        dve.wait_ge(cj_ready, u + 1)
                        down(0, True, True)
                        with dve.Fori(1, N_DOWN // 2 - 1) as j:
                            down(j, False, True)
                        down(N_DOWN // 2 - 1, False, False)
                        ye_rest(u, KT - 1, 1)
                        for s in range(2):
                            add(u, KT - 2 + s, s)
                    v.memset(own8[:, :, :], 0.0).then_inc(units_over, 1)
                    dve.wait_ge(units_over, 1)
                    residual(L, POST_FFN, "post_ffn", 5, f_routed, x, f[:, :, :])
                ada_takes(L, "post_ffn")

        @block.tensor
        def _(pe):
            mm = nc.tensor.matmul

            def slab(m, s, kt, a_hi, a_lo):
                pe.wait_ge(lo_split, m * 2 + (s + 1 + PRIME))
                pe.wait_ge(taken[s], m + 1)
                n = 0
                for k in range(kt):
                    for w, a in ((whi, a_hi), (whi, a_lo), (wlo, a_hi)):
                        for half in range(2):
                            ins = mm(ps[:, 2 * s + half, 0:HALF], w[:, s, k * P:(k + 1) * P],
                                     a[:, k, half * HALF:(half + 1) * HALF], start=(n < 2), stop=(n >= 6 * kt - 2))
                            n += 1
                ins.then_inc(slabs_used, 1)

            def ada_group(n, b, strict=True):
                pe.wait_ge(ada_out, n + (1 if strict else 0))
                for q in range(4):
                    pe.wait_ge(ada_landed[q % 2], n * 32 + (16 * (q // 2) + 16))
                    for k in range(2):
                        ins = mm(ps[0:32, b, :], cond[:, 2 * q + k, :], adaw[:, q % 2, 512 * k:512 * (k + 1)],
                                 start=(q + k == 0), stop=(q + k == 4))
                    ins.then_inc(ada_used, 1)

            def ada_groups(L, place):
                for n in MOD_AT.get((L, place), ()):
                    ada_group(n, mod_bank(place, n), n % 2 == 0)

            def sums_of(L, idx, src, ks, base):
                to = sums(idx)
                for n, k in enumerate(ks):
                    pe.wait_ge(sq_ready, 5 * KT * L + base + n + 1)
                    for half in range(2):
                        ins = mm(to[:, half, :], ones, src(k)[:, half * HALF:(half + 1) * HALF], start=(n == 0),
                                 stop=(n == len(ks) - 1))
                ins.then_inc(stat_done, 1)

            def by_token(to, n, weights):
                for c in range(NCH + 1):
                    rows = CH if c < NCH else NS
                    for part in range(2):
                        h = (h_hi, h_lo)[part]
                        for k in range(KT):
                            ins = mm(to[0:rows, n * c:n * (c + 1)], h[:, k, c * CH:c * CH + rows].bitcast(F32),
                                     weights[:, n * k:n * (k + 1)], start=(part + k == 0),
                                     stop=(part == 1 and k == KT - 1))
                return ins

            pe.sem_inc(slabs_used, PRIME)
            pe.sem_inc(ada_used, PRIME)
            pe.sem_inc(ada_out, 1)
            pe.wait_ge(cond_ready, 1)
            with pe.Fori(0, 4) as n:
                ada_group(n, 6)
            for L in range(DEPTH):
                first = FIRST[L]
                if L:
                    pe.wait_ge(ada_out, 21 + 2)
                sums_of(L, PRE_MIX, lambda k: sq[:, k, :], range(KT), SQ[PRE_MIX])
                ada_groups(L, "pre_mix")
                pe.wait_ge(h_ready, (2 * L + 1) * KT)
                by_token(ps[:, 5, :], HEADS, prm(L, "w_dt")).then_inc(dt_done, 1)
                with pe.Fori(0, N_XBC // 2) as i:
                    for s in range(2):
                        slab(i + first["xbc"], s, KT, h_hi, h_lo)
                pe.wait_ge(dA_ready, L + 1)
                dA_p = dA[:, 0:NCH, :].rearrange("p c h -> p (c h)")
                mm(ps[:, 7, 0:64], tri, dA_p, start=True, stop=True)
                mm(ps[:, 7, 64:128], ones, dA_p, start=True, stop=True)
                mm(ps[0:NS, 7, 128:144], con("tri_seq")[0:NS], dA[0:NS, NCH, :], start=True, stop=True)
                mm(ps[0:NS, 7, 144:160], con("same_seq")[0:NS], dA[0:NS, NCH, :], start=True, stop=True)
                mm(ps[:, 7, 160:288], con("ones")[0:NS].to_broadcast([NS, P]), dA_s[0:NS].rearrange("p b h -> p (b h)"), start=True, stop=True
                   ).then_inc(cum_done, 1)
                ada_groups(L, "cum")
                pe.wait_ge(xbc_ready, XBC * (L + 1) + 1)
                pe.wait_ge(cum_e, L + 1)
                if L == 0:
                    pe.wait_ge(ada_out, 6 + 2)
                for k in range(KT):
                    nc.tensor.transpose(ps[0:NS, 4 + k // GT, (k % GT) * P:(k % GT + 1) * P], mix[:, k, SEQ:T], ident)
                for g in range(GROUPS):
                    nc.tensor.transpose(ps[0:NS, 6, g * P:(g + 1) * P], mix[:, B0 + g, SEQ:T], ident)
                for g in range(GROUPS):
                    mm(ps[0:NS, 6, 256 + NS * g:256 + NS * (g + 1)], mix[:, B0 + g, SEQ:T], mix[:, C0 + g, SEQ:T],
                       start=True, stop=True)
                for h in range(HEADS):
                    ins = mm(ps[:, 7, NS * h:NS * (h + 1)], dA[0:NS, NCH, h:h + 1].to_broadcast([NS, P]),
                             con("tri_seq")[0:NS], start=True, stop=True)
                ins.then_inc(smp_pe, 1)
                pe.wait_ge(smp_G, L + 1)
                for h in range(HEADS):
                    a = HD * (h % 2)
                    ins = mm(ps[a:a + HD, 6, (h // 2) * NS:(h // 2 + 1) * NS], xdt_s[0:NS, h * HD:(h + 1) * HD],
                             E_s[0:NS, h, :], start=True, stop=True)
                ins.then_inc(smp_y, 1)
                if L == 0:
                    pe.sem_inc(chunk_pe, 1)
                with pe.Fori(0, NCH) as c:
                    for g in range(GROUPS):
                        i = c * 2 + g
                        mA, mB = i * 2 + first["mix"], i * 2 + (first["mix"] + 1)
                        slab(mA, 0, KT, h_hi, h_lo)
                        pe.wait_ge(staged, i + (KT * L + 1))
                        pe.wait_ge(units_free, i + ((KT + 1) * L + 1))
                        for j in range(GT):
                            nc.tensor.transpose(ps[:, 6, j * P:(j + 1) * P], x_st[j], ident)
                        nc.tensor.transpose(ps[:, 7, 0:NST], B_st, ident)
                        for gg in range(GROUPS):
                            pe.wait_ge(seq_in[gg], i * 16 + (16 + 16 * (NB + 1) * L))
                        for k in range(KT):
                            mm(ps[:, 7, 256 + TS * k:256 + TS * (k + 1)], S0[:, k // GT, (k % GT) * P:(k % GT + 1) * P],
                               mix[:, C0 + k // GT, bass.ds(i * TS + SEQ, TS)], start=True, stop=True)
                        mm(ps[:, 7, NST:2 * NST], B_st, mix[:, C0 + g, bass.ds(c * CH, CH)], start=True, stop=True)
                        for h in range(GH):
                            ins = mm(ps[:, 4 + h // 4, (h % 4) * CH:(h % 4 + 1) * CH],
                                     dA_st[:, h:h + 1].to_broadcast([P, P]), tri, start=True, stop=True)
                        ins.then_inc(chunk_pe, 1)
                        slab(mA, 1, KT, h_hi, h_lo)
                        slab(mB, 0, KT, h_hi, h_lo)
                        pe.wait_ge(chunk_G, i + (KT * L + 1))
                        pe.wait_ge(chunk_Ce, i + (KT * L + 1))
                        for h in range(GH):
                            a = HD * (h % 2)
                            to = ps[a:a + HD, 7, (h // 2) * CH:(h // 2 + 1) * CH]
                            mm(to, xdt[:, h * HD:(h + 1) * HD], E[:, h, :], start=True, stop=False)
                            mm(to, S[:, g, h * HD:(h + 1) * HD], Ce[:, h, :], start=False, stop=True)
                        mm(ps[:, 6, :], Bt, xe, start=True, stop=True).then_inc(chunk_y, 1)
                        for gg in range(GROUPS):
                            ins = mm(ps[:, 4 + gg, :], Bm[0:NS, gg * NST:(gg + 1) * NST],
                                     xe_s[0:NS, gg * GH * HD:(gg + 1) * GH * HD], start=True, stop=True)
                        ins.then_inc(seq_pe, 1)
                        slab(mB, 1, KT, h_hi, h_lo)
                pe.wait_ge(ya_ready, KT * (L + 1))
                for s in range(2):
                    slab(first["outA"], s, KT, ya_hi, ya_lo)
                ada_groups(L, "gate")
                for g in range(GROUPS):
                    if L == 0 and g == 1:
                        pe.wait_ge(ada_out, 7 + 2)
                    sums_of(L, GATE + g, lambda k: z[:, k, :], range(GT * g, GT * (g + 1)), SQ[GATE] + GT * g)
                with pe.Fori(1, KT // 2) as i:
                    for s in range(2):
                        slab(i + first["outA"], s, KT, ya_hi, ya_lo)
                pe.wait_ge(yb_ready, KT * (L + 1))
                with pe.Fori(0, KT // 2) as i:
                    for s in range(2):
                        slab(i + first["outB"], s, KT, h_hi, h_lo)
                sums_of(L, POST_MIX, lambda k: sq[:, k, :], range(KT), SQ[POST_MIX])
                pe.wait_ge(rstd_ready, NORMS * L + POST_MIX + 1)
                ada_groups(L, "post_mix")
                sums_of(L, PRE_FFN, lambda k: sq[:, k, :], range(KT), SQ[PRE_FFN])
                ada_groups(L, "pre_ffn")
                pe.wait_ge(h_ready, (2 * L + 2) * KT)
                if L == 0:
                    with pe.Fori(0, NEXP[0]) as e:
                        m0 = e * EP + first["exp"]
                        with pe.Fori(0, FT) as j:
                            slab(m0 + j, 0, KT, h_hi, h_lo)
                            slab(m0 + j, 1, KT, h_hi, h_lo)
                        with pe.Fori(0, N_DOWN // 2) as j:
                            for s in range(2):
                                pe.wait_ge(hid_ready, e * FT + (FT + 1))
                                slab(m0 + FT + j, s, FT, hid_hi, hid_lo)
                            ada_group(e * (N_DOWN // 2) + j + NG // 2, 6)
                    pe.wait_ge(ada_out, 19 + 2)
                    sums_of(L, POST_FFN, lambda k: sq[:, k, :], range(KT), SQ[POST_FFN])
                    ada_groups(L, "post_ffn")
                    continue
                by_token(ps[:, 7, :], NE, router).then_inc(logits_done, 1)
                for c in range(NCH + 1):
                    rows = CH if c < NCH else NS
                    for part, h in enumerate((h_hi, h_lo)):
                        if c:
                            pe.wait_ge(tok_taken, 2 * c - 1 + part)
                        for k in range(KT):
                            ins = nc.tensor.transpose(ps[0:rows, 2 * part + k // 4, (k % 4) * P:(k % 4 + 1) * P],
                                                      h[:, k, c * CH:c * CH + rows].bitcast(F32), ident)
                        ins.then_inc(tok_turned, 1)
                pe.wait_ge(chosen, 1)
                rank_p = rank[:, 0:NCH, :].rearrange("p c e -> p (c e)")
                mm(ps[:, 7, 64:96], tri, rank_p, start=True, stop=True)
                mm(ps[0:NS, 7, 96:104], tri[0:NS, 0:NS], rank[0:NS, NCH, :], start=True, stop=True)
                mm(ps[:, 7, 128:160], ones, rank_p, start=True, stop=True)
                mm(ps[:, 7, 160:168], con("ones")[0:NS].to_broadcast([NS, P]), rank[0:NS, NCH, :], start=True, stop=True
                   ).then_inc(counted, 1)
                pe.wait_ge(tok_taken, 2 * (NCH + 1))
                pe.wait_ge(table_ready, 1)
                n_of = pe.value_load(units[0:1, 0:1], min_val=1, max_val=MAXU)

                def unit_slab(m, s, kt, a_hi, a_lo):
                    pe.wait_ge(lo_split, m * 2 + (s + 1 + PRIME))
                    pe.wait_ge(taken[s], m + 1)
                    n = 0
                    for k in range(kt):
                        for w, a in ((whi, a_hi), (whi, a_lo), (wlo, a_hi)):
                            ins = mm(ps[:, 2 * s, 0:CAP], w[:, s, k * P:(k + 1) * P], a[:, k, 0:CAP], start=(n == 0),
                                     stop=(n == 3 * kt - 1))
                            n += 1
                    ins.then_inc(slabs_used, 1)

                with pe.Fori(0, n_of) as u:
                    m0 = u * EP + first["exp"]
                    pe.wait_ge(G_ready, u + 1)
                    for c in range(CAPT):
                        for q in range(NCH):
                            ins = nc.tensor.transpose(ps[:, 2 * c + 1, q * P:(q + 1) * P],
                                                      G[:, q, c * P:(c + 1) * P].bitcast(F32), ident)
                    ins.then_inc(G_turned, 1)
                    for q in range(KT // 2):
                        for part, (tok, gathered, gone) in enumerate(((htok_hi, hi_gathered, hi_taken),
                                                                      (htok_lo, lo_gathered, lo_taken))):
                            if q < 2:
                                pe.wait_ge(f_added, u * KT + PRIME)
                            else:
                                pe.wait_ge(gone, u * (KT // 2) + (q - 1))
                            for k in (2 * q, 2 * q + 1):
                                for c in range(NCH + 1):
                                    rows = CH if c < NCH else NS
                                    ins = mm(ps[:, 4 + 2 * part + q % 2, (k % 2) * CAP:(k % 2 + 1) * CAP],
                                             tok[0:rows, c, k * P:(k + 1) * P], G[0:rows, c, :], start=(c == 0),
                                             stop=(c == NCH))
                            ins.then_inc(gathered, 1)
                    pe.wait_ge(lo_taken, u * (KT // 2) + (KT // 2 - 1))
                    for c in range(CAPT):
                        mm(ps[:, 6, c * NS:(c + 1) * NS], G[0:NS, NCH, c * P:(c + 1) * P].bitcast(F32),
                           ident[0:NS, 0:NS], start=True, stop=True)
                    for c in range(CAPT):
                        for q in range(NCH + 1):
                            rows = CH if q < NCH else NS
                            ins = mm(ps[:, 6, 128 + c:129 + c], G[0:rows, q, c * P:(c + 1) * P].bitcast(F32),
                                     own_comb[0:rows, q:q + 1], start=(q == 0), stop=(q == NCH))
                    ins.then_inc(cj_done, 1)
                    with pe.Fori(0, FT) as j:
                        pe.wait_ge(hi_taken, u * (KT // 2) + KT // 2)
                        pe.wait_ge(lo_taken, u * (KT // 2) + KT // 2)
                        unit_slab(m0 + j, 0, KT, hu_hi, hu_lo)
                        unit_slab(m0 + j, 1, KT, hu_hi, hu_lo)

                    def turn(j, s):
                        pe.wait_ge(taken[s], m0 + FT + j + 2)
                        for c in range(CAPT):
                            ins = nc.tensor.transpose(ps[:, 2 * s + 1, c * P:(c + 1) * P], yu[:, s, c * P:(c + 1) * P],
                                                      ident)
                        ins.then_inc(y_turned, 1)

                    def scatter(j, s):
                        pe.wait_ge(ye_ready, u * KT + j * 2 + (s + 1))
                        pe.wait_ge(f_added, u * KT + j * 2 + (s + 1))
                        n = 0
                        for c in range(CAPT):
                            for ye in (ye_hi, ye_lo):
                                for half in range(2):
                                    ins = mm(ps[:, 4 + 2 * s + half, 0:HALF], ye[:, s, c * P:(c + 1) * P],
                                             Gt[:, c, half * HALF:(half + 1) * HALF], start=(n < 2), stop=(n >= 6))
                                    n += 1
                        ins.then_inc(scattered, 1)

                    def down(j, s):
                        pe.wait_ge(hid_ready, (u + (NEXP[0] + 1)) * FT + 1)
                        unit_slab(m0 + FT + j, s, FT, hidu_hi, hidu_lo)

                    down(0, 0)
                    down(0, 1)
                    turn(0, 0)
                    with pe.Fori(1, N_DOWN // 2) as j:
                        down(j, 0)
                        turn(j - 1, 1)
                        scatter(j - 1, 0)
                        down(j, 1)
                        turn(j, 0)
                        scatter(j - 1, 1)
                    turn(N_DOWN // 2 - 1, 1)
                    scatter(N_DOWN // 2 - 1, 0)
                    scatter(N_DOWN // 2 - 1, 1)
                sums_of(L, POST_FFN, lambda k: f[:, k, :], range(KT), SQ[POST_FFN])


def kernel(**inputs):
    import concourse.bacc as _bacc
    from concourse.bass_utils import run_bass_kernel_spmd as _run

    a = {k: np.asarray(v) for k, v in inputs.items()}

    def tiles(w):
        *lead, k, n = w.shape
        w = w.reshape(*lead, k // P, P, n // P, P)
        d = len(lead)
        return np.ascontiguousarray(np.moveaxis(w, (d + 2, d + 1, d, d + 3), (d, d + 1, d + 2, d + 3))).reshape(
            *lead, n // P, P, k)

    def by_feature(v):
        v = v.reshape(*v.shape[:-1], v.shape[-1] // P, P)
        return np.ascontiguousarray(np.moveaxis(v, (-1, -2), (0, 1)))

    xall = np.concatenate([a["x_prompt"].reshape(SEQ, D), a["x_sample"].reshape(NS, D)])
    call = np.concatenate([a["c_prompt"], a["c_sample"], np.zeros((32 - NM, D), np.float32)])
    pack = []
    w_dt0 = a["w_in"].shape[-1] - HEADS
    for L in range(DEPTH):
        cols = [by_feature(a["ada_b"][L]), by_feature(a["norm_pre_mix"][L]), by_feature(a["norm_post_mix"][L]),
                by_feature(a["norm_pre_ffn"][L]), by_feature(a["norm_post_ffn"][L]),
                np.moveaxis(by_feature(a["conva_w"][L]), 2, 1), np.moveaxis(by_feature(a["convb_w"][L]), 2, 1),
                by_feature(a["convb_b"][L]), by_feature(a["ssd_norm"][L]),
                by_feature(np.broadcast_to(a["d_skip"][L][:, None], (HEADS, HD)).reshape(-1)),
                a["w_in"][L][:, w_dt0:].reshape(KT, P, HEADS).transpose(1, 0, 2),
                np.broadcast_to(a["dt_bias"][L], (P, HEADS)), np.broadcast_to(a["a_log"][L], (P, HEADS))]
        pack += [c.reshape(P, -1) for c in cols]
    s, q = np.arange(P)[:, None], np.arange(P)[None, :]
    s2, q2 = s, np.arange(NS)[None, :]
    e2 = np.arange(NE)
    const = [(s <= q), (s == q), np.ones((P, 1)), (s2 // TS == q2 // TS) & (s2 <= q2), (s2 // TS == q2 // TS),
             (s // TS == np.arange(NB)[None, :]), np.full((P, 1), EPS),
             np.broadcast_to((e2[None, :] < e2[:, None]).reshape(1, -1), (P, NE * NE))]
    count = np.ascontiguousarray(np.broadcast_to(np.arange(CAP, dtype=np.float32), (P, CAP)))
    w_in = tiles(a["w_in"][:, :, :w_dt0])
    c = KT
    ff = a["ffd_w_gate"].shape[-1] // 2

    def gate_up(wg, wu):
        g, u = tiles(wg), tiles(wu)
        return np.stack([g, u], 2).reshape(g.shape[0], -1, P, D)

    def states(v):
        v = v.reshape(DEPTH, NB, v.shape[2], -1, P)
        return np.ascontiguousarray(v.transpose(0, 4, 3, 1, 2)).reshape(DEPTH, P, -1)

    split = a["ffd_w_gate"][0].reshape(D, 2, ff).transpose(1, 0, 2)
    splitu = a["ffd_w_up"][0].reshape(D, 2, ff).transpose(1, 0, 2)
    w_out = tiles(a["w_out"]).reshape(DEPTH, KT, P, 2, D).transpose(0, 3, 1, 2, 4)
    arrays = {
        "xT": by_feature(xall).reshape(P, -1),
        "cT": by_feature(call).reshape(P, -1),
        "pack": np.concatenate(pack, 1),
        "const": np.concatenate([v.astype(np.float32) for v in const], 1),
        "count": count,
        "w_router": a["moe_router"][0].reshape(KT, P, NE).transpose(1, 0, 2).reshape(P, -1),
        "s_conva": states(a["state_conva"]),
        "s_convb": states(a["state_convb"]),
        "s_ssm": a["state_ssm"].reshape(DEPTH, NB, GROUPS, GH * HD, NST).transpose(0, 1, 2, 4, 3),
        "w_ada": a["ada_w"].reshape(DEPTH, 4, 2, P, NG // 2, 512).transpose(0, 4, 1, 3, 2, 5).reshape(NG, 4, P, 2 * 512),
        "w_xbc": w_in[:, 4 * c:],
        "w_mix": np.stack([w_in[:, c:2 * c], w_in[:, 2 * c:3 * c], w_in[:, 0:c], w_in[:, 3 * c:4 * c]], 2).reshape(
            DEPTH, 4 * c, P, D),
        "w_out": w_out.reshape(DEPTH, 2 * KT, P, D),
        "w_gu0": gate_up(split, splitu),
        "w_dn0": tiles(a["ffd_w_down"][0].reshape(2, ff, D)),
        "w_gu1": gate_up(a["moe_w_gate"][0], a["moe_w_up"][0]),
        "w_dn1": tiles(a["moe_w_down"][0]),
    }
    arrays = {k: np.ascontiguousarray(v) for k, v in arrays.items()}
    outs = {"yT": (P, KT * T), "o_ap": (DEPTH, P, KT * 2), "o_bp": (DEPTH, P, XBC * 3),
            "o_sp": (DEPTH, P, HEADS * HD), "o_as": (DEPTH, P, KT * NB * 2), "o_bs": (DEPTH, P, XBC * NB * 3),
            "o_ss": (DEPTH, NB, GROUPS, P, GH * HD)}
    nc = _bacc.Bacc("TRN2", target_bir_lowering=False, num_devices=1)
    args = [nc.dram_tensor(k, v.shape, mybir.dt.from_np(v.dtype), kind="ExternalInput").ap() for k, v in arrays.items()]
    args += [nc.dram_tensor(k, v, F32, kind="ExternalOutput").ap() for k, v in outs.items()]
    hybrid_decoder(nc, *args)
    r = _run(nc, [arrays], core_ids=[0]).results[0]
    y = r["yT"].reshape(P, KT, T).transpose(2, 1, 0).reshape(T, D)

    def rows(v, n, tile):
        v = v.reshape(DEPTH, P, tile, *n)
        return np.ascontiguousarray(np.moveaxis(v, (2, 1), (-2, -1))).reshape(DEPTH, *n, tile * P)

    return (y[:SEQ].reshape(1, SEQ, D), y[SEQ:].reshape(NB, TS, D),
            rows(r["o_ap"], (1, 2), KT), rows(r["o_bp"], (1, 3), XBC),
            np.ascontiguousarray(r["o_sp"].reshape(DEPTH, 1, P, HEADS, HD).transpose(0, 1, 3, 4, 2)),
            rows(r["o_as"], (NB, 2), KT), rows(r["o_bs"], (NB, 3), XBC),
            np.ascontiguousarray(r["o_ss"].reshape(DEPTH, NB, GROUPS, P, GH, HD).transpose(0, 1, 2, 4, 5, 3)).reshape(
                DEPTH, NB, HEADS, HD, NST))
```

```python
from contextlib import ExitStack

import numpy as np

import concourse.bass as bass
from concourse import mybir

ALU = mybir.AluOpType
ACT = mybir.ActivationFunctionType
F32 = mybir.dt.float32
F32R = mybir.dt.float32r
AX_X = mybir.AxisListType.X

P = 128
D = 1024
KT = D // P
SEQ = 512
NB, TS = 8, 4
NS = NB * TS
T = SEQ + NS
HALF = T // 2
DEPTH = 2
HEADS, HD, NST = 16, 64, 128
GROUPS = 2
GH = HEADS // GROUPS
GT = KT // GROUPS
CH = 128
NCH = SEQ // CH
XBC = 12
FT = 11
NE = 8
NEXP = (2, NE)
CAP = 256
CAPT = CAP // P
MAXU = (2 * T + NE * (CAP - 1)) // CAP
SLAB = KT * P
SLABMAX = FT * P
EPS = 1e-6
MODS = 6 * KT
ADA_SLOTS = 4
NM = 1 + NB
NG = 2 * MODS // 4
MOD_AT = {(0, "pre_mix"): (4, 5), (0, "cum"): (6,), (0, "gate"): (7,), (0, "post_mix"): (8, 9), (0, "pre_ffn"): (10, 11),
          (0, "post_ffn"): (20, 21), (1, "pre_mix"): (22, 23)}


def columns(*fields):
    at, out = 0, {}
    for name, n in fields:
        out[name] = (at, at + n)
        at += n
    return out, at


PACK, NPACK = columns(("ada_b", MODS), ("pre_mix", KT), ("post_mix", KT), ("pre_ffn", KT), ("post_ffn", KT),
                      ("conva", 3 * KT), ("convb", 4 * XBC), ("convb_b", XBC), ("ssd_norm", KT), ("d_skip", KT),
                      ("w_dt", KT * HEADS), ("dt_bias", HEADS), ("a_log", HEADS))
CONST, NCONST = columns(("tri", P), ("ident", P), ("ones", 1), ("tri_seq", NS), ("same_seq", NS), ("in_seq", NB),
                        ("eps", 1), ("before", NE * NE))

N_XBC, N_MIX, N_GU, N_DOWN = XBC, 4 * KT, 2 * FT, KT
EP = (N_GU + N_DOWN) // 2
LAYER_PAIRS = (N_XBC + N_MIX + 2 * KT) // 2 + NEXP[0] * EP


class Tally:

    def __init__(self, sem, engine):
        self.sem, self.engine, self.base, self.n = sem, engine, 0, 0

    def step(self, ins):
        ins.then_inc(self.sem, 1)
        self.n += 1

    def settle(self):
        self.engine.wait_ge(self.sem, self.base + self.n)

    def enter(self, i, each):
        outer = (self.base, self.n, each)
        self.base, self.n = self.base + self.n + i * each, 0
        return outer

    def leave(self, outer, times):
        base, n, each = outer
        assert self.n == each, (self.n, each)
        self.base, self.n = base, n + times * each


def hybrid_decoder(nc, xT, cT, pack, const, count, w_router, s_conva, s_convb, s_ssm, w_ada, w_xbc, w_mix, w_out, w_gu0, w_dn0, w_gu1,
                   w_dn1, yT, o_ap, o_bp, o_sp, o_as, o_bs, o_ss):
    x_spill = nc.dram_tensor("x_spill", [P, KT * T], F32).ap()
    w_gu, w_dn = (w_gu0, w_gu1), (w_dn0, w_dn1)
    with ExitStack() as ctx:
        def sb(name, shape, dt=F32, where=ctx):
            return where.enter_context(nc.sbuf_tensor(name, shape, dt))

        def sem(name):
            return ctx.enter_context(nc.semaphore(name))

        raw = sb("raw", [P, 2, SLABMAX])
        whi = sb("whi", [P, 2, SLABMAX], F32R)
        wlo = sb("wlo", [P, 2, SLABMAX], F32R)
        with ExitStack() as conditioning:
            adaw = sb("adaw", [P, ADA_SLOTS, 512], F32, conditioning)
        raw_b0 = sb("raw_b0", [P, 2 * SLAB])
        cst = sb("cst", [P, NCONST])
        par = sb("par", [P, DEPTH, NPACK])
        cond = sb("cond", [P, KT, 32])
        modT = sb("modT", [P, 4, 32])
        router = sb("router", [P, KT * NE])
        mod = sb("mod", [P, DEPTH, MODS, NM])
        warm = sb("warm", [P, 1])
        coef = sb("coef", [P, KT, NM])
        comb = sb("comb", [P, 5, NE])
        usb = sb("usb", [P, XBC, NB, 3 + TS])
        h_hi = sb("h_hi", [P, KT, T], F32R)
        h_lo = sb("h_lo", [P, KT, T], F32R)
        xreg = sb("xreg", [P, KT * T])
        wreg = sb("wreg", [P, 6480])
        with ExitStack() as mixer:
            ya_hi = sb("ya_hi", [P, KT, T], F32R, mixer)
            ya_lo = sb("ya_lo", [P, KT, T], F32R, mixer)
            mix = sb("mix", [P, XBC + KT, T], F32, mixer)
            usa = sb("usa", [P, KT, NB, 2 + TS], F32, mixer)
        with ExitStack() as narrow:
            nar_hi = sb("nar_hi", [P, KT * HEADS], F32R, narrow)
            nar_lo = sb("nar_lo", [P, KT * HEADS], F32R, narrow)
        with ExitStack() as experts:
            hid_hi = sb("hid_hi", [P, FT, T], F32R, experts)
            hid_lo = sb("hid_lo", [P, FT, T], F32R, experts)
            f = sb("f", [P, KT, T], F32, experts)
        with ExitStack() as routed:
            htok_hi = sb("htok_hi", [P, NCH + 1, D], F32R, routed)
            htok_lo = sb("htok_lo", [P, NCH + 1, D], F32R, routed)
            G = sb("G", [P, NCH + 1, CAP], F32R, routed)
            Gt = sb("Gt", [P, CAPT, T], F32R, routed)
            hidu_hi = sb("hidu_hi", [P, FT, CAP], F32R, routed)
            hidu_lo = sb("hidu_lo", [P, FT, CAP], F32R, routed)
            place = sb("place", [P, NCH + 1, NE], F32, routed)
            before_c = sb("before_c", [P, NCH + 2, NE], F32, routed)
            n_units = sb("n_units", [P, NE], F32, routed)
            end_unit = sb("end_unit", [P, NE], F32, routed)
            is_expert = sb("is_expert", [P, MAXU + 1, NE], F32, routed)
            of_unit = sb("of_unit", [P, MAXU + 1], F32, routed)
            first_of = sb("first_of", [P, MAXU + 1], F32, routed)
            own8 = sb("own8", [P, NCH + 1, NE], F32, routed)
            own_place = sb("own_place", [P, NCH + 1], F32, routed)
            own_comb = sb("own_comb", [P, NCH + 1], F32, routed)
            cj = sb("cj", [P, CAPT], F32, routed)
            units = sb("units", [P, MAXU + 2], mybir.dt.int32, routed)
            raw_b1 = sb("raw_b1", [P, SLABMAX], F32, routed)
        ps = ctx.enter_context(nc.psum_tensor("ps", [P, 8, 512], F32))

        def con(name):
            a, b = CONST[name]
            return cst[:, a:b]

        def prm(layer, name):
            a, b = PACK[name]
            return par[:, layer, a:b]

        def view(buf, at, *shape):
            v = buf[:, at:at + int(np.prod(shape))]
            if len(shape) == 2:
                v = v.rearrange("p (a b) -> p a b", a=shape[0])
            if len(shape) == 3:
                v = v.rearrange("p (a b c) -> p a b c", a=shape[0], b=shape[1])
            return v

        def halves(v):
            return v.rearrange("p (a b) -> p a b", a=2)

        def seqs(v):
            return v.rearrange("p (b t) -> p b t", b=NB)

        def over(v, n):
            return v.unsqueeze(len(v.shape)).broadcast_to([*v.shape, n])

        ident, tri, ones = con("ident"), con("tri"), con("ones").to_broadcast([P, P])
        x = view(xreg, 0, KT, T)
        xs = mix[:, 0:KT, :]
        z = mix[:, XBC:XBC + KT, :]
        B0, C0 = KT, KT + GROUPS
        E = view(xreg, 0, GH, CH)
        Ce = view(xreg, 1024, GH, CH)
        S = view(xreg, 2048, GROUPS, GH * HD)
        xdt = view(xreg, 3072, GH * HD)
        xe = view(xreg, 3584, GH * HD)
        Bt = view(xreg, 4096, NST)
        cbm = view(xreg, 4224, CH)
        x_st = [raw[:, j // 2, SLAB + CH * (j % 2):SLAB + CH * (j % 2 + 1)] for j in range(GT)]
        B_st = raw[:, 0, SLAB + 2 * CH:SLAB + 3 * CH]
        dA_st = raw[:, 1, SLAB + 2 * CH:SLAB + 2 * CH + GH]
        yt = view(xreg, 0, KT, NS)
        E_s = view(xreg, 0, HEADS, NS)
        xdt_s = view(xreg, 1024, D)
        cbm_s = view(xreg, 4224, GROUPS, NS)
        S0 = view(wreg, 0, GROUPS, GH * HD)
        xe_s = view(wreg, 1024, D)
        Bt_s = view(wreg, 2048, 2 * NST)
        Bm = view(wreg, 2304, 2 * NST)
        ecum_s = view(wreg, 2560, HEADS, NS)
        yo_s = view(wreg, 3072, KT, NS)
        yd_s = view(wreg, 3328, KT, NS)
        ub = view(wreg, 3584, 3 + T)
        acc = view(wreg, 4131, T)
        gc_s = view(wreg, 4675, T)
        ya_f = view(wreg, 5219, T)
        dt_t = view(wreg, 5763, 5, HEADS)
        dA = view(wreg, 5843, 5, HEADS)
        cum = view(wreg, 5923, 5, HEADS)
        wend = view(wreg, 6003, 5, HEADS)
        dec = view(wreg, 6083, NCH, HEADS)
        dec_s = view(wreg, 6147, NB, HEADS)
        dA_s = view(wreg, 6275, NB, HEADS)
        nap = view(wreg, 6403, KT, 2)
        nbp = view(wreg, 6419, XBC, 3)
        expA = view(wreg, 6455, HEADS)
        sp_x = view(wreg, 4131, 5, HEADS)
        sp_e = view(wreg, 4211, 5, HEADS)
        sp_t = view(wreg, 4291, 5, HEADS)
        sp_l = view(wreg, 4371, 5, HEADS)
        sp_r = view(wreg, 4451, 5, HEADS)
        nar_t = gc_s
        yb_t = (acc, ub[:, 0:T])
        rg = (gc_s, ya_f)
        sq = view(wreg, 0, KT, T)
        rstd = view(wreg, KT * T, T)
        ta = view(wreg, KT * T + T, T)
        tb = view(wreg, KT * T + 2 * T, T)
        smp = view(wreg, KT * T + 3 * T, KT, NS)
        f_routed = sq
        ta_u = view(wreg, KT * T, CAP)
        tb_u = view(wreg, KT * T + CAP, CAP)
        yu = view(wreg, KT * T + 2 * CAP, 2, CAP)
        iota = view(wreg, KT * T + 4 * CAP, CAP)
        hu_hi, hu_lo = h_hi[:, :, 0:CAP], h_lo[:, :, 0:CAP]
        ye_hi, ye_lo = h_hi[:, 0:2, HALF:HALF + CAP], h_lo[:, 0:2, HALF:HALF + CAP]
        pr = view(wreg, 1024, 5, NE)
        pm = view(wreg, 1064, 5)
        rank = view(wreg, 1072, 5, NE)
        cmp = view(wreg, 1152, 5, NE, NE)
        cmq = view(wreg, 1472, 5, NE, NE)

        PRIME = 2
        params_in, x_in = sem("params_in"), sem("x_in")
        raw_landed = [sem("raw_landed0"), sem("raw_landed1")]
        raw_landed_b = [sem("raw_landed_b0"), sem("raw_landed_b1")]
        hi_split = sem("hi_split")
        lo_split = sem("lo_split")
        slabs_used = sem("slabs_used")
        taken = [sem("taken0"), sem("taken1")]
        ada_landed = [sem("ada_landed%d" % q) for q in range(ADA_SLOTS)]
        ada_used = sem("ada_used")
        ada_out = sem("ada_out")
        cond_ready = sem("cond_ready")
        sq_ready, stat_done, rstd_ready = sem("sq_ready"), sem("stat_done"), sem("rstd_ready")
        smp_ready, t_ready, hhi_ready, h_ready = sem("smp_ready"), sem("t_ready"), sem("hhi_ready"), sem("h_ready")
        x_ready = sem("x_ready")
        act_steps, dve_steps = sem("act_steps"), sem("dve_steps")
        narhi_ready, nar_ready, nar_done, nar_taken = (sem("narhi_ready"), sem("nar_ready"), sem("nar_done"),
                                                       sem("nar_taken"))
        dt_done, dt_x, dt_e, dA_ready = sem("dt_done"), sem("dt_x"), sem("dt_e"), sem("dA_ready")
        conv_done, xbc_ready = sem("conv_done"), sem("xbc_ready")
        yahi_ready, ya_ready = sem("yahi_ready"), sem("ya_ready")
        cum_done, cum_x, cum_e, cum_ready = sem("cum_done"), sem("cum_x"), sem("cum_e"), sem("cum_ready")
        smp_pe, smp_seg, smp_act, smp_G, smp_y, smp_done = (sem("smp_pe"), sem("smp_seg"), sem("smp_act"),
                                                            sem("smp_G"), sem("smp_y"), sem("smp_done"))
        chunk_pe, chunk_seg, chunk_act, chunk_G, chunk_Ce = (sem("chunk_pe"), sem("chunk_seg"), sem("chunk_act"),
                                                             sem("chunk_G"), sem("chunk_Ce"))
        chunk_y, seq_pe, seq_new = sem("chunk_y"), sem("seq_pe"), sem("seq_new")
        seq_in = [sem("seq_in0"), sem("seq_in1")]
        seq_out = [sem("seq_out0"), sem("seq_out1")]
        gz_ready, gy_ready, ybf_ready, ybhi_ready, yb_ready = (sem("gz_ready"), sem("gy_ready"), sem("ybf_ready"),
                                                               sem("ybhi_ready"), sem("yb_ready"))
        windows_in, windows_out, state_out, x_back, spill_out = (sem("windows_in"), sem("windows_out"),
                                                                 sem("state_out"), sem("x_back"), sem("spill_out"))
        hidhi_ready, hid_ready = sem("hidhi_ready"), sem("hid_ready")
        logits_done, router_x, router_e = sem("logits_done"), sem("router_x"), sem("router_e")
        y_out, staged, units_free = sem("y_out"), sem("staged"), sem("units_free")
        iota_in, chosen, counted, table_ready = sem("iota_in"), sem("chosen"), sem("counted"), sem("table_ready")
        tok_turned, tok_taken = sem("tok_turned"), sem("tok_taken")
        unit_steps, act_unit_steps = sem("unit_steps"), sem("act_unit_steps")
        G_ready, G_turned, Gt_ready = sem("G_ready"), sem("G_turned"), sem("Gt_ready")
        hi_gathered, lo_gathered = sem("hi_gathered"), sem("lo_gathered")
        hi_taken, lo_taken = sem("hi_taken"), sem("lo_taken")
        cj_done, cj_ready, y_turned = sem("cj_done"), sem("cj_ready"), sem("y_turned")
        yehi_ready, ye_ready, scattered = sem("yehi_ready"), sem("ye_ready"), sem("scattered")
        f_cleared, f_added, units_over = sem("f_cleared"), sem("f_added"), sem("units_over")

        FIRST, USES = [], []
        pair = 0
        for L in range(DEPTH):
            FIRST.append({"xbc": pair, "mix": pair + N_XBC // 2, "outA": pair + (N_XBC + N_MIX) // 2,
                          "outB": pair + (N_XBC + N_MIX + KT) // 2, "exp": pair + (N_XBC + N_MIX) // 2 + KT})
            pair += LAYER_PAIRS

        def bank(s):
            return ps[:, 2 * s:2 * s + 2, 0:HALF]

        def narrow_of(L, nth):
            return {(0, 0): (prm(0, "w_dt"), 1), (1, 0): (prm(1, "w_dt"), 2), (1, 1): (router[:, :], 3)}.get((L, nth))

        NORMS = 6
        PRE_MIX, GATE, POST_MIX, PRE_FFN, POST_FFN = 0, 1, 3, 4, 5
        SQ = {PRE_MIX: 0, GATE: 8, POST_MIX: 16, PRE_FFN: 24, POST_FFN: 32}

        def mod_bank(place, n):
            return {"cum": 6, "gate": 4, "post_ffn": 4 + n % 2}.get(place, 6 + n % 2)

        def sums(idx):
            b = 4 + 2 * (idx % 2)
            return ps[:, b:b + 2, 0:HALF]

        block = ctx.enter_context(nc.Block())

        def unit_raw(u, odd, i, s):
            if odd:
                return (raw_b0, raw_b1)[s][:, 0:SLABMAX], raw_landed_b[s], u * (16 * (EP // 2)) + (i * 16 + 16)
            return raw[:, s, :], raw_landed[s], u * (16 * (EP - EP // 2)) + (i * 16 + (FIRST[1]["exp"] * 16 + 16))

        @block.sync
        def _(sp):
            sp.dma_start(cond[:, :, :].rearrange("p k b -> p (k b)"), cT).then_inc(params_in, 16)
            sp.dma_start(cst[:, :], const).then_inc(params_in, 16)
            sp.dma_start(par[:, :, :].rearrange("p l n -> p (l n)"), pack).then_inc(params_in, 16)
            sp.dma_start(router[:, :], w_router).then_inc(params_in, 16)
            sp.dma_start(xreg[:, :], xT).then_inc(x_in, 16)

            def load_pair(m, src, cols):
                for s in range(2):
                    sp.wait_ge(lo_split, m * 2 + s + 1)
                    sp.dma_start(raw[:, s, 0:cols], src(s)).then_inc(raw_landed[s], 16)

            for L in range(DEPTH):
                first = FIRST[L]
                with sp.Fori(0, N_XBC // 2) as i:
                    load_pair(i + first["xbc"], lambda s: w_xbc[L, i * 2 + s], SLAB)
                with sp.Fori(0, N_MIX // 2) as i:
                    load_pair(i + first["mix"], lambda s: w_mix[L, i * 2 + s], SLAB)
                with sp.Fori(0, KT) as i:
                    load_pair(i + first["outA"], lambda s: w_out[L, i * 2 + s], SLAB)

                def expert(u, e):
                    with sp.Fori(0, FT) as j:
                        load_pair(u * EP + j + first["exp"], lambda s: w_gu[L][e, j * 2 + s], SLAB)
                    with sp.Fori(0, N_DOWN // 2) as j:
                        load_pair(u * EP + j + (FT + first["exp"]), lambda s: w_dn[L][e, j * 2 + s], SLABMAX)

                if L == 0:
                    with sp.Fori(0, NEXP[0]) as e:
                        expert(e, e)
                else:
                    sp.wait_ge(table_ready, 1)
                    n = sp.value_load(units[0:1, 0:1], min_val=1, max_val=MAXU)
                    with sp.Fori(0, n) as u:
                        e = sp.value_load(units[0:1, bass.ds(u + 1, 1)], min_val=0, max_val=NE - 1)
                        m0 = u * EP + first["exp"]

                        def load_for_unit(m, odd, i, src, cols, back=2):
                            for s in range(2):
                                to, landed, _ = unit_raw(u, odd, i, s)
                                sp.wait_ge(lo_split, m * 2 + (s + 1 + PRIME - 2 * back))
                                sp.dma_start(to[:, 0:cols], src(s)).then_inc(landed, 16)

                        load_for_unit(m0, 0, 0, lambda s: w_gu1[e, s], SLAB, 1)
                        with sp.Fori(0, FT // 2) as i:
                            load_for_unit(m0 + i * 2 + 1, 1, i, lambda s: w_gu1[e, i * 4 + (2 + s)], SLAB)
                            load_for_unit(m0 + i * 2 + 2, 0, i + 1, lambda s: w_gu1[e, i * 4 + (4 + s)], SLAB)
                        for j in range(N_DOWN // 2):
                            load_for_unit(m0 + FT + j, (FT + j) % 2, (FT + j) // 2, lambda s: w_dn1[e, j * 2 + s],
                                          SLABMAX)
            sp.wait_ge(x_ready, DEPTH * 2 * KT)
            sp.dma_start(yT, xreg[:, :]).then_inc(y_out, 16)
            sp.wait_ge(y_out, 16)

        @block.gpsimd
        def _(pool):
            def ada_load(n):
                for k in range(KT):
                    pool.wait_ge(ada_used, n * KT + (k + 1))
                    pool.dma_start(adaw[:, k % ADA_SLOTS, :], w_ada[n, k]).then_inc(ada_landed[k % ADA_SLOTS], 16)

            def ada_loads(L, place):
                for n in MOD_AT.get((L, place), ()):
                    ada_load(n)

            with pool.Fori(0, 4) as n:
                ada_load(n)
            for L in range(DEPTH):
                if L:
                    pool.wait_ge(x_ready, 2 * KT * L)
                    pool.dma_start(x_spill, xreg[:, :]).then_inc(spill_out, 16)
                ada_loads(L, "pre_mix")
                pool.dma_start(usb[:, :, :, 0:3], s_convb[L].rearrange("p (k b t) -> p k b t", k=XBC, b=NB)
                               ).then_inc(windows_in, 16)
                pool.dma_start(usa[:, :, :, 0:2], s_conva[L].rearrange("p (k b t) -> p k b t", k=KT, b=NB)
                               ).then_inc(windows_in, 16)
                ada_loads(L, "cum")
                pool.wait_ge(h_ready, (2 * L + 1) * KT)
                for g in range(GROUPS):
                    pool.dma_start(S0[:, g, :], s_ssm[L, 0, g]).then_inc(seq_in[g], 16)
                pool.wait_ge(xbc_ready, XBC * (L + 1) + 1)
                pool.wait_ge(dA_ready, L + 1)
                with pool.Fori(0, KT) as i:
                    pool.wait_ge(chunk_pe, i + (KT * L + 1))
                    for j in range(GT):
                        nc.gpsimd.tensor_copy(x_st[j], mix[:, (i % 2) * GT + j, bass.ds((i // 2) * CH, CH)])
                    nc.gpsimd.tensor_copy(B_st, mix[:, i % 2 + B0, bass.ds((i // 2) * CH, CH)])
                    nc.gpsimd.tensor_copy(dA_st, dA[:, i // 2, bass.ds((i % 2) * GH, GH)]).then_inc(staged, 1)
                    pool.wait_ge(chunk_act, i * 2 + (1 + 2 * KT * L))
                    nc.gpsimd.tensor_tensor(Ce, Ce, mix[:, i % 2 + C0, bass.ds((i // 2) * CH, CH)].unsqueeze(
                        1).broadcast_to([P, GH, CH]), ALU.mult).then_inc(chunk_Ce, 1)
                    for g in range(GROUPS):
                        pool.wait_ge(seq_new, i * 2 + (g + 1 + 2 * NB * L))
                        pool.dma_start(o_ss[L, i, g], S0[:, g, :]).then_inc(seq_out[g], 16)
                    for g in range(GROUPS):
                        pool.wait_ge(seq_out[g], i * 16 + (16 + 16 * NB * L))
                        pool.dma_start(S0[:, g, :], s_ssm[L, (i + 1) % NB, g]).then_inc(seq_in[g], 16)
                ada_loads(L, "gate")
                pool.wait_ge(ya_ready, KT * (L + 1))
                pool.wait_ge(units_free, (KT + 1) * (L + 1))
                pool.dma_start(o_sp[L], xreg[:, 2048:3072]).then_inc(state_out, 16)
                pool.dma_start(o_as[L].rearrange("p (k b t) -> p k b t", k=KT, b=NB), usa[:, :, :, TS:TS + 2]
                               ).then_inc(windows_out, 16)
                pool.dma_start(o_bs[L].rearrange("p (k b t) -> p k b t", k=XBC, b=NB), usb[:, :, :, TS:TS + 3]
                               ).then_inc(windows_out, 16)
                pool.dma_start(o_ap[L], nap.rearrange("p k t -> p (k t)")).then_inc(windows_out, 16)
                pool.dma_start(o_bp[L], nbp.rearrange("p k t -> p (k t)")).then_inc(windows_out, 16)
                pool.wait_ge(stat_done, NORMS * L + GATE + 2)
                if L:
                    pool.wait_ge(spill_out, 16 * L)
                pool.dma_start(z.rearrange("p k t -> p (k t)"), x_spill if L else xT).then_inc(x_back, 16)
                ada_loads(L, "post_mix")
                ada_loads(L, "pre_ffn")
                pool.wait_ge(windows_out, 64 * (L + 1))
                if L:
                    pool.wait_ge(x_ready, (2 * L + 1) * KT)
                    pool.dma_start(iota, count).then_inc(iota_in, 16)
                    pool.wait_ge(table_ready, 1)
                    nc.gpsimd.memset(f_routed, 0.0).then_inc(f_cleared, 1)
                if L == 0:
                    with pool.Fori(0, N_DOWN) as n:
                        ada_load(n + NG // 2)
                ada_loads(L, "post_ffn")

        @block.scalar
        def _(act):
            st = Tally(act_steps, act)

            def hi(m, s, cols, where=None):
                src, landed, value = where or (raw[:, s, :], raw_landed[s], m * 16 + 16)
                act.wait_ge(landed, value)
                act.wait_ge(slabs_used, m * 2 + (s + 1))
                nc.scalar.copy(whi[:, s, 0:cols], src[:, 0:cols]).then_inc(hi_split, 1)

            def used(m, s):
                act.wait_ge(slabs_used, m * 2 + (s + 1 + PRIME))

            def load_silu():
                st.step(nc.scalar.activation(warm[:, :], con("eps"), ACT.Silu))
                st.settle()

            def make_rstd(idx, n, to):
                st.step(nc.scalar.activation(warm[:, :], con("eps"), ACT.Ln))
                st.settle()
                act.wait_ge(stat_done, idx + 1)
                st.step(nc.scalar.activation(halves(to), sums(idx % NORMS), ACT.Ln, scale=1.0 / n, bias=con("eps")))
                st.settle()
                nc.scalar.activation(to, to, ACT.Exp, scale=-0.5).then_inc(rstd_ready, 1)

            def modulate(L, nth, shift):
                act.wait_ge(smp_ready, 2 * L + nth + 1)
                nc.scalar.copy(h_hi[:, :, SEQ:T], smp).then_inc(hhi_ready, 1)
                if narrow_of(L, nth):
                    w, _ = narrow_of(L, nth)
                    nc.scalar.copy(nar_hi[:, 0:w.shape[-1]], w).then_inc(narhi_ready, 1)
                base = (2 * L + nth) * KT

                def upper(k):
                    act.wait_ge(act_steps, scaled[k])
                    nc.scalar.copy(h_hi[:, k, 0:SEQ], sq[:, k, 0:SEQ]).then_inc(hhi_ready, 1)

                scaled = []
                for k in range(KT):
                    act.wait_ge(t_ready, base + k + 1)
                    st.step(nc.scalar.activation(sq[:, k, 0:SEQ], sq[:, k, 0:SEQ], ACT.Identity,
                                                 scale=coef[:, k, 0:1], bias=mod[:, L, k + shift, 0:1]))
                    scaled.append(st.base + st.n)
                    if k:
                        upper(k - 1)
                upper(KT - 1)

            act.wait_ge(params_in, 64)
            nc.scalar.activation(cond[:, :, :], cond[:, :, :], ACT.Silu).then_inc(cond_ready, 1)
            for s in range(2):
                hi(0, s, SLAB)
            act.wait_ge(x_in, 16)
            for L in range(DEPTH):
                first = FIRST[L]
                with act.Fori(0, KT) as k:
                    if L:
                        act.wait_ge(x_ready, k + (2 * KT * L - KT + 1))
                    nc.scalar.activation(sq[:, k, :], x[:, k, :], ACT.Square).then_inc(sq_ready, 1)
                make_rstd(NORMS * L + PRE_MIX, D, rstd)
                modulate(L, 0, 0)
                act.wait_ge(dt_x, 2 * L + 1)
                st.step(nc.scalar.activation(expA, prm(L, "a_log"), ACT.Exp))
                st.settle()
                nc.scalar.activation(sp_e, sp_e, ACT.Exp).then_inc(dt_e, 1)
                act.wait_ge(dt_x, 2 * L + 2)
                nc.scalar.activation(sp_l, sp_t, ACT.Ln).then_inc(dt_e, 1)
                load_silu()
                with act.Fori(0, N_XBC // 2) as i:
                    for s in range(2):
                        t = i * 2 + s
                        used(i + first["xbc"], s)
                        act.wait_ge(conv_done, t + (1 + (XBC + KT) * L))
                        nc.scalar.copy(halves(ub[:, 3:3 + T]), bank(s)).then_inc(taken[s], 1)
                        hi(i + (first["xbc"] + 1), s, SLAB)
                        act.wait_ge(conv_done, t + (2 + (XBC + KT) * L))
                        nc.scalar.activation(mix[:, t, :], acc, ACT.Silu).then_inc(xbc_ready, 1)
                act.wait_ge(cum_done, L + 1)
                act.wait_ge(cum_x, L + 1)
                st.step(nc.scalar.activation(dec, ps[:, 7, 64:128].rearrange("p (c h) -> p c h", c=NCH), ACT.Exp))
                st.step(nc.scalar.activation(dec_s, ps[:, 7, 160:288].rearrange("p (c h) -> p c h", c=NB), ACT.Exp))
                nc.scalar.activation(wend, wend, ACT.Exp).then_inc(cum_e, 1)
                act.wait_ge(smp_seg, L + 1)
                nc.scalar.activation(ecum_s, ps[:, 7, :].rearrange("p (h t) -> p h t", h=HEADS), ACT.Exp
                                     ).then_inc(smp_act, 1)
                nc.scalar.activation(E_s[0:NS], E_s[0:NS], ACT.Exp).then_inc(smp_act, 1)
                with act.Fori(0, KT) as i:
                    mA, mB = i * 2 + first["mix"], i * 2 + (first["mix"] + 1)
                    used(mA, 0)
                    nc.scalar.copy(halves(gc_s), bank(0)).then_inc(taken[0], 1)
                    hi(mB, 0, SLAB)
                    act.wait_ge(chunk_seg, i + (KT * L + 1))
                    nc.scalar.activation(Ce, ps[:, 4:6, :].rearrange("p a (h t) -> p (a h) t", h=4), ACT.Exp
                                         ).then_inc(chunk_act, 1)
                    nc.scalar.activation(E, E, ACT.Exp).then_inc(chunk_act, 1)
                    used(mA, 1)
                    hi(mB, 1, SLAB)
                    act.wait_ge(taken[0], mB + 2)
                    nc.scalar.copy(ya_hi[:, i, :], ya_f).then_inc(yahi_ready, 1)
                    hi(mB + 1, 0, SLAB)
                    used(mB, 1)
                    nc.scalar.copy(halves(mix[:, i + XBC, :]), bank(1)).then_inc(taken[1], 1)
                    hi(mB + 1, 1, SLAB)
                act.wait_ge(taken[1], first["outA"] + 1)
                load_silu()
                with act.Fori(0, KT) as k:
                    nc.scalar.activation(mix[:, k + XBC, :], mix[:, k + XBC, :], ACT.Silu).then_inc(gz_ready, 1)
                with act.Fori(0, KT) as k:
                    act.wait_ge(gy_ready, k + (KT * L + 1))
                    nc.scalar.activation(mix[:, k + XBC, :], mix[:, k, :], ACT.Square).then_inc(sq_ready, 1)
                act.wait_ge(state_out, 16 * (L + 1))

                def first_half(i, s):
                    used(i + first["outA"], s)
                    nc.scalar.copy(halves(x[:, i * 2 + s, :]), bank(s)).then_inc(taken[s], 1)
                    hi(i + (first["outA"] + 1), s, SLAB)

                def gated_upper(i, s):
                    act.wait_ge(ybf_ready, i * 2 + (s + 1 + KT * L))
                    nc.scalar.copy(h_hi[:, i * 2 + s, :], yb_t[s]).then_inc(ybhi_ready, 1)

                with act.Fori(0, KT // 4) as i:
                    for s in range(2):
                        first_half(i, s)
                for g in range(GROUPS):
                    make_rstd(NORMS * L + GATE + g, D // GROUPS, rg[g])
                with act.Fori(0, KT // 4) as i:
                    for s in range(2):
                        for odd in range(2):
                            gated_upper(i * 2 + s, odd)
                        first_half(i + KT // 4, s)
                for g in range(GROUPS):
                    act.wait_ge(seq_in[g], 16 * (NB + 1) * (L + 1))
                act.wait_ge(windows_out, 64 * (L + 1))
                act.wait_ge(yb_ready, KT * (L + 1))

                def second_half(i, ahead):
                    for s in range(2):
                        used(i + first["outB"], s)
                        if ahead:
                            hi(i + (first["outB"] + 1), s, SLAB)
                        act.wait_ge(taken[s], i + (first["outB"] + 2))
                        nc.scalar.activation(sq[:, i * 2 + s, :], x[:, i * 2 + s, :], ACT.Square).then_inc(sq_ready, 1)

                with act.Fori(0, KT // 2 - 1) as i:
                    second_half(i, True)
                second_half(KT // 2 - 1, L == 0)
                make_rstd(NORMS * L + POST_MIX, D, rstd)
                with act.Fori(0, KT) as k:
                    act.wait_ge(x_ready, k + (2 * KT * L + 1))
                    nc.scalar.activation(sq[:, k, :], x[:, k, :], ACT.Square).then_inc(sq_ready, 1)
                make_rstd(NORMS * L + PRE_FFN, D, rstd)
                modulate(L, 1, 3 * KT)
                if L:
                    act.wait_ge(router_x, 1)
                    nc.scalar.activation(pr, pr, ACT.Exp).then_inc(router_e, 1)

                def gate_up(m0, j, cols, ta, tb, gate, hid, where=lambda s: None):
                    m = m0 + j
                    hi(m + 1, 0, cols, where(0))
                    used(m, 0)
                    nc.scalar.activation(ta, gate, ACT.Silu).then_inc(taken[0], 1)
                    if cols == SLAB:
                        hi(m + 1, 1, cols, where(1))
                    act.wait_ge(taken[1], m + 2)
                    nc.scalar.copy(hid[:, j, :], tb).then_inc(hidhi_ready, 1)
                    if cols != SLAB:
                        hi(m + 1, 1, cols, where(1))

                if L == 0:
                    with act.Fori(0, NEXP[0]) as e:
                        outer = st.enter(e, 1)
                        m0 = e * EP + first["exp"]
                        load_silu()
                        with act.Fori(0, FT - 1) as j:
                            gate_up(m0, j, SLAB, halves(ta), tb, bank(0), hid_hi)
                        gate_up(m0, FT - 1, SLABMAX, halves(ta), tb, bank(0), hid_hi)
                        with act.Fori(0, N_DOWN // 2 - 1) as j:
                            for s in range(2):
                                used(m0 + FT + j, s)
                                hi(m0 + FT + 1 + j, s, SLABMAX)
                        for s in range(2):
                            used(m0 + (EP - 1), s)
                            hi(m0 + EP, s, SLAB)
                    st.leave(outer, NEXP[0])
                else:
                    for c in range(NCH + 1):
                        rows = CH if c < NCH else NS
                        for part, to in enumerate((htok_hi, htok_lo)):
                            act.wait_ge(tok_turned, 2 * c + part + 1)
                            nc.scalar.copy(to[0:rows, c, :].rearrange("p (a b) -> p a b", a=2),
                                           ps[0:rows, 2 * part:2 * part + 2, :]).then_inc(tok_taken, 1)
                    act.wait_ge(table_ready, 1)
                    n = act.value_load(units[0:1, 0:1], min_val=1, max_val=MAXU)

                    def ye_upper(u, k, s):
                        act.wait_ge(y_turned, u * KT + (k + 1))
                        nc.scalar.activation(ye_hi[:, s, :].rearrange("p (c f) -> p c f", c=CAPT)[:, 0, :],
                                             ps[:, 2 * s + 1, 0:P], ACT.Copy, scale=cj[:, 0:1])
                        nc.scalar.activation(ye_hi[:, s, :].rearrange("p (c f) -> p c f", c=CAPT)[:, 1, :],
                                             ps[:, 2 * s + 1, P:2 * P], ACT.Copy, scale=cj[:, 1:2]
                                             ).then_inc(yehi_ready, 1)

                    ut = Tally(act_unit_steps, act)
                    with act.Fori(0, n) as u:
                        ut.enter(u, 1)
                        m0 = u * EP + first["exp"]
                        for q in range(KT // 2):
                            act.wait_ge(hi_gathered, u * (KT // 2) + (q + 1))
                            nc.scalar.copy(hu_hi[:, 2 * q:2 * q + 2, :],
                                           ps[:, 4 + q % 2, :].rearrange("p (k t) -> p k t", k=2)
                                           ).then_inc(hi_taken, 1)
                            if q < 2:
                                hi(m0, q, SLAB, unit_raw(u, 0, 0, q))
                        act.wait_ge(G_turned, u + 1)
                        for c in range(CAPT):
                            nc.scalar.copy(Gt[:, c, 0:SEQ], ps[:, 2 * c + 1, :]).then_inc(Gt_ready, 1)
                        ut.step(nc.scalar.activation(warm[:, :], con("eps"), ACT.Silu))
                        ut.settle()
                        with act.Fori(0, FT // 2) as i:
                            for odd in range(2):
                                gate_up(m0, i * 2 + odd, SLAB, ta_u, tb_u, ps[:, 0, 0:CAP], hidu_hi,
                                        lambda s: unit_raw(u, 1 - odd, i + odd, s))
                        gate_up(m0, FT - 1, SLABMAX, ta_u, tb_u, ps[:, 0, 0:CAP], hidu_hi,
                                lambda s: unit_raw(u, 1, FT // 2, s))

                        def down(j, head, ahead):
                            for s in range(2):
                                m = m0 + FT + j
                                used(m, s)
                                nc.scalar.copy(yu[:, s, :], ps[:, 2 * s, 0:CAP]).then_inc(taken[s], 1)
                                if ahead:
                                    hi(m + 1, s, SLABMAX, unit_raw(u, (FT + j + 1) % 2, (FT + j + 1) // 2, s))
                                if s or not head:
                                    ye_upper(u, j * 2 + s - 1, 1 - s)

                        act.wait_ge(cj_ready, u + 1)
                        for j in range(N_DOWN // 2):
                            down(j, j == 0, j < N_DOWN // 2 - 1)
                        ye_upper(u, KT - 1, 1)
                if L:
                    act.wait_ge(units_over, 1)
                for k in range(KT):
                    if L == 0:
                        act.wait_ge(taken[k % 2], first["exp"] + EP * NEXP[0] - (N_DOWN // 2) + k // 2 + 2)
                        nc.scalar.activation(sq[:, k, :], f[:, k, :], ACT.Square).then_inc(sq_ready, 1)
                    else:
                        nc.scalar.activation(f[:, k, :], f_routed[:, k, :], ACT.Square).then_inc(sq_ready, 1)
                make_rstd(NORMS * L + POST_FFN, D, rstd)

        @block.vector
        def _(dve):
            st = Tally(dve_steps, dve)
            v = nc.vector

            def lo(m, s, cols, where=None):
                dve.wait_ge(hi_split, m * 2 + (s + 1))
                src = where[0] if where else raw[:, s, :]
                v.tensor_tensor(wlo[:, s, 0:cols], src[:, 0:cols], whi[:, s, 0:cols].bitcast(F32), ALU.subtract
                                ).then_inc(lo_split, 1)

            def used(m, s):
                dve.wait_ge(slabs_used, m * 2 + (s + 1 + PRIME))

            def link(ins):
                st.step(ins)
                st.settle()

            def coefficients(L, gain, which, one):
                m = mod[:, L, which * KT:(which + 1) * KT, :]
                if one:
                    link(v.tensor_scalar(coef[:, :, :], m, 1.0, None, ALU.add))
                    link(v.tensor_tensor(coef[:, :, :], coef[:, :, :], over(prm(L, gain), NM), ALU.mult))
                else:
                    link(v.tensor_tensor(coef[:, :, :], m, over(prm(L, gain), NM), ALU.mult))

            def by_seq(v4):
                return v4.rearrange("p k (b t) -> p k b t", b=NB)

            def times_rstd_samples(src):
                link(v.tensor_tensor(smp, src[:, :, SEQ:T], rstd[:, SEQ:T].unsqueeze(1).broadcast_to([P, KT, NS]),
                                     ALU.mult))
                link(v.tensor_tensor(by_seq(smp), by_seq(smp), over(coef[:, :, 1:NM], TS), ALU.mult))

            def modulate(L, nth, idx, gain, shift, scale):
                if nth or L:
                    dve.wait_ge(x_ready, (2 * L + nth) * KT)
                coefficients(L, gain, scale, True)
                dve.wait_ge(rstd_ready, NORMS * L + idx + 1)
                times_rstd_samples(x)
                v.tensor_tensor(by_seq(smp), by_seq(smp), over(mod[:, L, shift * KT:(shift + 1) * KT, 1:NM], TS),
                                ALU.add).then_inc(smp_ready, 1)
                base = (2 * L + nth)
                with dve.Fori(0, KT) as k:
                    v.tensor_tensor(sq[:, k, 0:SEQ], x[:, k, 0:SEQ], rstd[:, 0:SEQ], ALU.mult).then_inc(t_ready, 1)
                dve.wait_ge(hhi_ready, base * (KT + 1) + 1)
                link(v.tensor_tensor(h_lo[:, :, SEQ:T], smp, h_hi[:, :, SEQ:T].bitcast(F32), ALU.subtract))
                if narrow_of(L, nth):
                    w, count = narrow_of(L, nth)
                    n = w.shape[-1]
                    dve.wait_ge(narhi_ready, count)
                    v.tensor_tensor(nar_lo[:, 0:n], w, nar_hi[:, 0:n].bitcast(F32), ALU.subtract
                                    ).then_inc(nar_ready, 1)
                with dve.Fori(0, KT) as k:
                    dve.wait_ge(hhi_ready, k + (base * (KT + 1) + 2))
                    v.tensor_tensor(h_lo[:, k, 0:SEQ], sq[:, k, 0:SEQ], h_hi[:, k, 0:SEQ].bitcast(F32), ALU.subtract
                                    ).then_inc(h_ready, 1)

            def narrow_take(L, nth):
                w, count = narrow_of(L, nth)
                dve.wait_ge(nar_done, count)
                v.tensor_copy(halves(nar_t[0:w.shape[-1] // KT]), ps[0:w.shape[-1] // KT, 4:6, 0:HALF]
                              ).then_inc(nar_taken, 1)

            def residual(L, idx, gain, gate, src, old, scaled):
                coefficients(L, gain, gate, False)
                dve.wait_ge(rstd_ready, NORMS * L + idx + 1)
                times_rstd_samples(src)
                link(v.tensor_tensor(x[:, :, SEQ:T], smp, old[:, :, SEQ:T], ALU.add))
                made = []
                for k in range(KT + 1):
                    if k < KT:
                        st.step(v.tensor_tensor(scaled[:, k, 0:SEQ], src[:, k, 0:SEQ], rstd[:, 0:SEQ], ALU.mult))
                        made.append(st.base + st.n)
                    if k:
                        dve.wait_ge(dve_steps, made[k - 1])
                        v.scalar_tensor_tensor(x[:, k - 1, 0:SEQ], scaled[:, k - 1, 0:SEQ], coef[:, k - 1, 0:1],
                                               old[:, k - 1, 0:SEQ], ALU.mult, ALU.add).then_inc(x_ready, 1)

            def convolve(weights, taps, i, windows, tails, bias, before):
                n = weights.shape[-1] // taps
                o = 4 - taps
                st.step(v.tensor_copy(windows[:, i, :, taps - 1:taps - 1 + TS], seqs(ub[:, 3 + SEQ:3 + T])))
                st.step(v.tensor_copy(tails[:, i, :], ub[:, 3 + SEQ - (taps - 1):3 + SEQ]))
                before()
                st.settle()
                for j in range(taps):
                    w = weights[:, bass.ds(i + j * n, 1)]
                    a_p, a_s = ub[:, o + j:o + j + SEQ], windows[:, i, :, j:j + TS]
                    if j == 0:
                        st.step(v.tensor_scalar(acc[:, 0:SEQ], a_p, w, bias, ALU.mult, ALU.add))
                        st.step(v.tensor_scalar(seqs(acc[:, SEQ:T]), a_s, w, bias, ALU.mult, ALU.add))
                    else:
                        st.settle()
                        st.step(v.scalar_tensor_tensor(acc[:, 0:SEQ], a_p, w, acc[:, 0:SEQ], ALU.mult, ALU.add))
                        last = v.scalar_tensor_tensor(seqs(acc[:, SEQ:T]), a_s, w, seqs(acc[:, SEQ:T]), ALU.mult,
                                                      ALU.add)
                        if j < taps - 1:
                            st.step(last)
                last.then_inc(conv_done, 1)

            dve.sem_inc(lo_split, PRIME)
            dve.sem_inc(taken[0], 1)
            dve.sem_inc(taken[1], 1)
            dve.sem_inc(conv_done, 1)
            dve.sem_inc(xbc_ready, 1)
            dve.sem_inc(hid_ready, 1)
            for s in range(2):
                lo(0, s, SLAB)
            dve.wait_ge(params_in, 64)

            def ada_take(L, n, g, b):
                dve.wait_ge(ada_used, n * KT + (KT + ADA_SLOTS))
                dve.wait_ge(ada_out, n + 1)
                rows = ps[0:32, b, :].rearrange("p (t r b) -> p t r b", t=4, r=4)
                for r in range(4):
                    st.step(v.transpose(modT[32 * r:32 * r + 32, :, :], rows[:, :, r, :]))
                st.settle()
                v.tensor_tensor(mod[:, L, bass.ds(g * 4, 4), :], modT[:, :, 0:NM],
                                over(prm(L, "ada_b")[:, bass.ds(g * 4, 4)], NM), ALU.add).then_inc(ada_out, 1)

            def ada_takes(L, place):
                for n in MOD_AT.get((L, place), ()):
                    ada_take(n // (NG // 2), n, n % (NG // 2), mod_bank(place, n))
                    dve.wait_ge(ada_out, n + 2)

            with dve.Fori(0, 4) as n:
                outer = st.enter(n, 4)
                ada_take(0, n, n, 6)
            st.leave(outer, 4)
            for L in range(DEPTH):
                first = FIRST[L]
                if L == 0:
                    dve.wait_ge(ada_out, 4 + 1)
                    dve.wait_ge(x_in, 16)
                else:
                    dve.wait_ge(ada_out, 22 + 1)
                modulate(L, 0, PRE_MIX, "pre_mix", 0, 1)
                ada_takes(L, "pre_mix")
                dve.wait_ge(h_ready, (2 * L + 1) * KT)
                narrow_take(L, 0)
                link(v.memset(ub[:, 0:3], 0.0))
                link(v.memset(sp_x, 0.0))
                dve.wait_ge(dt_done, L + 1)
                bias = prm(L, "dt_bias").unsqueeze(1).broadcast_to([P, NCH, HEADS])
                st.step(v.tensor_tensor(sp_x[:, 0:NCH, :], ps[:, 5, 0:64].rearrange("p (c h) -> p c h", c=NCH), bias,
                                        ALU.add))
                link(v.tensor_tensor(sp_x[0:NS, NCH, :], ps[0:NS, 5, 64:80], prm(L, "dt_bias")[0:NS], ALU.add))
                v.scalar_tensor_tensor(sp_e, sp_x, -1.0, sp_x, ALU.mult, ALU.min).then_inc(dt_x, 1)
                dve.wait_ge(dt_e, 2 * L + 1)
                v.tensor_scalar(sp_t, sp_e, 1.0, None, ALU.add).then_inc(dt_x, 1)
                dve.wait_ge(dt_x, 2 * L + 2)
                link(v.tensor_scalar(sp_r, sp_t, -1.0, None, ALU.add))
                link(v.tensor_tensor(sp_e, sp_e, sp_r, ALU.subtract))
                link(v.reciprocal(sp_r, sp_t))
                link(v.tensor_tensor(sp_e, sp_e, sp_r, ALU.mult))
                dve.wait_ge(dt_e, 2 * L + 2)
                link(v.tensor_tensor(sp_e, sp_e, sp_l, ALU.add))
                link(v.scalar_tensor_tensor(dt_t, sp_x, 0.0, sp_e, ALU.max, ALU.add))
                link(v.scalar_tensor_tensor(dA, dt_t, -1.0, expA.unsqueeze(1).broadcast_to([P, 5, HEADS]), ALU.mult,
                                            ALU.mult))
                v.tensor_tensor(dA_s[0:NS], dA[0:NS, NCH:NCH + 1, :].broadcast_to([NS, NB, HEADS]),
                                over(con("in_seq")[0:NS], HEADS), ALU.mult).then_inc(dA_ready, 1)
                dve.wait_ge(windows_in, 32 * (L + 1))
                with dve.Fori(0, N_XBC // 2) as i:
                    outer = st.enter(i, 2 * 9)
                    for s in range(2):
                        t = i * 2 + s
                        dve.wait_ge(taken[s], i + (first["xbc"] + 2))
                        convolve(prm(L, "convb"), 4, t, usb, nbp, prm(L, "convb_b")[:, bass.ds(t, 1)],
                                 lambda: dve.wait_ge(xbc_ready, t + (XBC * L + 1)))
                        lo(i + (first["xbc"] + 1), s, SLAB)
                st.leave(outer, N_XBC // 2)
                if L:
                    dve.wait_ge(spill_out, 16 * L)
                link(v.memset(wend, 0.0))
                dve.wait_ge(cum_done, L + 1)
                st.step(v.tensor_copy(cum[:, 0:NCH, :], ps[:, 7, 0:64].rearrange("p (c h) -> p c h", c=NCH)))
                link(v.tensor_copy(cum[0:NS, NCH, :], ps[0:NS, 7, 128:144]))
                st.step(v.tensor_tensor(wend[:, 0:NCH, :], ps[:, 7, 64:128].rearrange("p (c h) -> p c h", c=NCH),
                                        cum[:, 0:NCH, :], ALU.subtract))
                v.tensor_tensor(wend[0:NS, NCH, :], ps[0:NS, 7, 144:160], cum[0:NS, NCH, :], ALU.subtract
                                ).then_inc(cum_x, 1)
                dve.wait_ge(cum_e, L + 1)
                link(v.tensor_tensor(wend, wend, dt_t, ALU.mult))
                ada_takes(L, "cum")
                dve.wait_ge(smp_pe, L + 1)
                st.step(v.tensor_copy(Bt_s[0:NS], ps[0:NS, 6, 0:256]))
                st.step(v.tensor_tensor(cbm_s[0:NS], ps[0:NS, 6, 256:320].rearrange("p (g t) -> p g t", g=GROUPS),
                                        con("tri_seq")[0:NS].unsqueeze(1).broadcast_to([NS, GROUPS, NS]), ALU.mult))
                xT_s = ps[0:NS, 4:6, :].rearrange("p a (h d) -> p (a h) d", d=HD)
                st.step(v.tensor_tensor(xdt_s[0:NS].rearrange("p (h d) -> p h d", h=HEADS), xT_s,
                                        over(dt_t[0:NS, NCH, :], HD), ALU.mult))
                st.step(v.tensor_tensor(xe_s[0:NS].rearrange("p (h d) -> p h d", h=HEADS), xT_s,
                                        over(wend[0:NS, NCH, :], HD), ALU.mult))
                link(v.tensor_tensor(E_s[0:NS], ps[0:NS, 7, :].rearrange("p (h t) -> p h t", h=HEADS),
                                     over(cum[0:NS, NCH, :], NS), ALU.subtract))
                v.tensor_scalar(E_s[0:NS], E_s[0:NS], 0.0, None, ALU.min).then_inc(smp_seg, 1)
                dve.wait_ge(smp_act, 2 * (L + 1))
                Eg = E_s[0:NS].rearrange("p (g h) t -> p g h t", g=GROUPS)
                v.tensor_tensor(Eg, Eg, cbm_s[0:NS].unsqueeze(2).broadcast_to([NS, GROUPS, GH, NS]), ALU.mult
                                ).then_inc(smp_G, 1)
                dve.wait_ge(smp_y, L + 1)
                st.step(v.tensor_copy(yd_s, ps[:, 6, 0:KT * NS].rearrange("p (k t) -> p k t", k=KT)))
                v.memset(S, 0.0).then_inc(units_free, 1)
                dve.wait_ge(units_free, (KT + 1) * L + 1)
                with dve.Fori(0, KT) as i:
                    outer = st.enter(i, 7 + 7 + 2 + 2 + 3)
                    c, h0 = i // 2, (i % 2) * GH
                    mA, mB = i * 2 + first["mix"], i * 2 + (first["mix"] + 1)
                    lo(mB, 0, SLAB)
                    dve.wait_ge(chunk_pe, i + (KT * L + 2))
                    st.step(v.tensor_scalar(Bm[0:NS], Bt_s[0:NS], con("in_seq")[0:NS, bass.ds(i, 1)], None, ALU.mult))
                    st.step(v.tensor_copy(Bt, ps[:, 7, 0:NST]))
                    st.step(v.tensor_copy(yo_s[:, :, bass.ds(i * TS, TS)],
                                          ps[:, 7, 256:288].rearrange("p (k t) -> p k t", k=KT)))
                    st.step(v.tensor_tensor(cbm, ps[:, 7, NST:2 * NST], tri, ALU.mult))
                    xT_c = ps[:, 6, :].rearrange("p (h d) -> p h d", h=GH)
                    st.step(v.tensor_tensor(xdt.rearrange("p (h d) -> p h d", h=GH), xT_c,
                                            over(dt_t[:, c, bass.ds(h0, GH)], HD), ALU.mult))
                    st.step(v.tensor_tensor(xe.rearrange("p (h d) -> p h d", h=GH), xT_c,
                                            over(wend[:, c, bass.ds(h0, GH)], HD), ALU.mult))
                    link(v.tensor_tensor(E, ps[:, 4:6, :].rearrange("p a (h t) -> p (a h) t", h=4),
                                         over(cum[:, c, bass.ds(h0, GH)], CH), ALU.subtract))
                    v.tensor_scalar(E, E, 0.0, None, ALU.min).then_inc(chunk_seg, 1)
                    dve.wait_ge(chunk_act, i * 2 + (2 + 2 * KT * L))
                    v.tensor_tensor(E, E, cbm.unsqueeze(1).broadcast_to([P, GH, CH]), ALU.mult).then_inc(chunk_G, 1)
                    used(mA, 1)
                    dve.wait_ge(taken[0], mA + 2)
                    v.tensor_tensor(halves(ub[:, 3:3 + T]), bank(1), halves(gc_s), ALU.mult).then_inc(taken[1], 1)
                    dve.wait_ge(taken[1], mA + 2)
                    convolve(prm(L, "conva"), 3, i, usa, nap, 0.0, lambda: None)
                    lo(mB, 1, SLAB)
                    used(mB, 0)
                    dve.wait_ge(conv_done, i + (XBC + 2 + (XBC + KT) * L))
                    v.tensor_tensor(halves(ya_f), bank(0), halves(acc), ALU.mult).then_inc(taken[0], 1)
                    dve.wait_ge(yahi_ready, i + (KT * L + 1))
                    v.tensor_tensor(ya_lo[:, i, :], ya_f, ya_hi[:, i, :].bitcast(F32), ALU.subtract
                                    ).then_inc(ya_ready, 1)
                    lo(mB + 1, 0, SLAB)
                    dve.wait_ge(seq_pe, i + (KT * L + 1))
                    for g in range(GROUPS):
                        S0g = S0[:, g, :].rearrange("p (h d) -> p h d", h=GH)
                        st.step(v.tensor_tensor(S0g, S0g, over(dec_s[:, i, g * GH:(g + 1) * GH], HD), ALU.mult))
                    st.settle()
                    for g in range(GROUPS):
                        v.tensor_tensor(S0[:, g, :], S0[:, g, :], ps[:, 4 + g, :], ALU.add).then_inc(seq_new, 1)
                    Sg = S[:, i % 2, :].rearrange("p (h d) -> p h d", h=GH)
                    link(v.tensor_tensor(Sg, Sg, over(dec[:, c, bass.ds(h0, GH)], HD), ALU.mult))
                    st.step(v.tensor_tensor(S[:, i % 2, :], S[:, i % 2, :], ps[:, 6, :], ALU.add))
                    for j in range(GT):
                        y = mix[:, (i % 2) * GT + j, bass.ds(c * CH, CH)]
                        ins = v.scalar_tensor_tensor(y, y, prm(L, "d_skip")[:, bass.ds((i % 2) * GT + j, 1)],
                                                     ps[:, 7, j * CH:(j + 1) * CH], ALU.mult, ALU.add)
                        if j < GT - 1:
                            st.step(ins)
                    ins.then_inc(units_free, 1)
                    lo(mB + 1, 1, SLAB)
                st.leave(outer, KT)
                dve.wait_ge(units_free, (KT + 1) * (L + 1))
                ec = ecum_s.rearrange("p (k a) t -> p k a t", a=2)
                st.step(v.tensor_tensor(yt[0:HD], yo_s[0:HD], ec[0:HD, :, 0, :], ALU.mult))
                st.step(v.tensor_tensor(yt[HD:P], yo_s[HD:P], ec[HD:P, :, 1, :], ALU.mult))
                link(v.tensor_tensor(xs[:, :, SEQ:T], xs[:, :, SEQ:T], over(prm(L, "d_skip"), NS), ALU.mult))
                link(v.tensor_tensor(yt, yt, yd_s, ALU.add))
                link(v.tensor_tensor(xs[:, :, SEQ:T], xs[:, :, SEQ:T], yt, ALU.add))
                with dve.Fori(0, KT) as k:
                    dve.wait_ge(gz_ready, k + (KT * L + 1))
                    v.tensor_tensor(mix[:, k, :], mix[:, k, :], mix[:, k + XBC, :], ALU.mult).then_inc(gy_ready, 1)
                dve.wait_ge(gy_ready, KT * (L + 1))
                for s in range(2):
                    lo(first["outA"] + 1, s, SLAB)
                ada_takes(L, "gate")
                for s in range(2):
                    lo(first["outA"] + 2, s, SLAB)
                for k in range(KT + 1):
                    if k < KT:
                        dve.wait_ge(rstd_ready, NORMS * L + GATE + 1 + k // GT)
                        if k >= 2:
                            dve.wait_ge(yb_ready, KT * L + k - 1)
                        v.scalar_tensor_tensor(yb_t[k % 2], mix[:, k, :], prm(L, "ssd_norm")[:, k:k + 1], rg[k // GT],
                                               ALU.mult, ALU.mult).then_inc(ybf_ready, 1)
                    if k:
                        dve.wait_ge(ybhi_ready, KT * L + k)
                        v.tensor_tensor(h_lo[:, k - 1, :], yb_t[(k - 1) % 2], h_hi[:, k - 1, :].bitcast(F32),
                                        ALU.subtract).then_inc(yb_ready, 1)
                        if k % 2 == 0:
                            lo(first["outA"] + 3 + (k - 1) // 4, (k // 2 - 1) % 2, SLAB)
                for s in range(2):
                    dve.wait_ge(taken[s], first["outB"] + 1)

                def second_half(i, ahead):
                    for s in range(2):
                        used(i + first["outB"], s)
                        m_k = halves(x[:, i * 2 + s, :])
                        v.tensor_tensor(m_k, m_k, bank(s), ALU.add).then_inc(taken[s], 1)
                        if ahead:
                            lo(i + (first["outB"] + 1), s, SLAB)

                with dve.Fori(0, KT // 2 - 1) as i:
                    second_half(i, True)
                second_half(KT // 2 - 1, L == 0)
                dve.wait_ge(x_back, 16 * (L + 1))
                residual(L, POST_MIX, "post_mix", 2, x, z, sq)
                ada_takes(L, "post_mix")
                modulate(L, 1, PRE_FFN, "pre_ffn", 3, 4)
                ada_takes(L, "pre_ffn")
                if L:
                    dve.wait_ge(h_ready, (2 * L + 2) * KT)
                    narrow_take(L, 1)
                    link(v.memset(pr, 0.0))
                    dve.wait_ge(logits_done, 1)
                    st.step(v.tensor_copy(pr[:, 0:NCH, :], ps[:, 7, 0:32].rearrange("p (c e) -> p c e", c=NCH)))
                    link(v.tensor_copy(pr[0:NS, NCH, :], ps[0:NS, 7, 32:40]))
                    link(v.tensor_reduce(pm, pr, axis=AX_X, op=ALU.max))
                    v.tensor_tensor(pr, pr, over(pm, NE), ALU.subtract).then_inc(router_x, 1)
                    dve.wait_ge(router_e, 1)
                    link(v.tensor_reduce(pm, pr, axis=AX_X, op=ALU.add))
                    link(v.reciprocal(pm, pm))
                    link(v.tensor_tensor(pr, pr, over(pm, NE), ALU.mult))
                    before = con("before").rearrange("p (e j) -> p e j", e=NE)
                    other = pr.unsqueeze(2).broadcast_to([P, NCH + 1, NE, NE])
                    own = over(pr, NE)
                    st.step(v.tensor_tensor(cmp, other, own, ALU.is_gt))
                    link(v.tensor_tensor(cmq, other, own, ALU.is_equal))
                    link(v.tensor_tensor(cmq, cmq, before.unsqueeze(1).broadcast_to([P, NCH + 1, NE, NE]), ALU.mult))
                    link(v.tensor_tensor(cmp, cmp, cmq, ALU.add))
                    link(v.tensor_reduce(rank, cmp, axis=AX_X, op=ALU.add))
                    link(v.tensor_scalar(rank, rank, 2.0, None, ALU.is_lt))
                    link(v.tensor_tensor(comb[:, :, :], rank, pr, ALU.mult))
                    link(v.tensor_reduce(pm, comb[:, :, :], axis=AX_X, op=ALU.add))
                    link(v.reciprocal(pm, pm))
                    link(v.tensor_tensor(comb[:, :, :], comb[:, :, :], over(pm, NE), ALU.mult))
                    v.tensor_scalar(rank, rank, 1.0, None, ALU.mult).then_inc(chosen, 1)
                    dve.wait_ge(chosen, 1)
                    dve.wait_ge(iota_in, 16)
                    st.step(v.memset(place[:, :, :], 0.0))
                    link(v.memset(before_c[:, :, :], 0.0))
                    dve.wait_ge(counted, 1)
                    st.step(v.tensor_copy(place[:, 0:NCH, :], ps[:, 7, 64:96].rearrange("p (c e) -> p c e", c=NCH)))
                    st.step(v.tensor_copy(place[0:NS, NCH, :], ps[0:NS, 7, 96:104]))
                    for c in range(NCH + 1):
                        link(v.tensor_tensor(before_c[:, c + 1, :], before_c[:, c, :],
                                             ps[:, 7, 128 + NE * c:128 + NE * (c + 1)], ALU.add))
                    total = before_c[:, NCH + 1, :]
                    link(v.tensor_scalar(n_units[:, :], total, 0.0, None, ALU.is_gt))
                    for c in range(1, -(-T // CAP)):
                        link(v.tensor_scalar(end_unit[:, :], total, float(c * CAP), None, ALU.is_gt))
                        link(v.tensor_tensor(n_units[:, :], n_units[:, :], end_unit[:, :], ALU.add))
                    link(v.tensor_tensor(cmp[:, 0], before, n_units[:, :].unsqueeze(1).broadcast_to([P, NE, NE]),
                                         ALU.mult))
                    link(v.tensor_reduce(end_unit[:, :], cmp[:, 0], axis=AX_X, op=ALU.add))
                    link(v.tensor_scalar(own8[:, 0, :], end_unit[:, :], float(CAP), None, ALU.mult))
                    link(v.tensor_tensor(before_c[:, 0:NCH + 1, :], before_c[:, 0:NCH + 1, :],
                                         own8[:, 0:1, :].broadcast_to([P, NCH + 1, NE]), ALU.add))
                    link(v.tensor_tensor(place[:, :, :], place[:, :, :], before_c[:, 0:NCH + 1, :], ALU.add))
                    link(v.tensor_tensor(place[:, :, :], place[:, :, :], rank, ALU.mult))
                    link(v.tensor_scalar(place[:, :, :], place[:, :, :], -1.0, None, ALU.add))
                    link(v.tensor_tensor(end_unit[:, :], end_unit[:, :], n_units[:, :], ALU.add))
                    link(v.tensor_tensor(is_expert[:, :, :], end_unit[:, :].unsqueeze(1).broadcast_to([P, MAXU + 1, NE]),
                                         over(iota[:, 0:MAXU + 1], NE), ALU.is_gt))
                    link(v.tensor_reduce(of_unit[:, :], is_expert[:, :, :], axis=AX_X, op=ALU.add))
                    link(v.tensor_scalar(of_unit[:, :], of_unit[:, :], -1.0, float(NE), ALU.mult, ALU.add))
                    link(v.tensor_tensor(is_expert[:, :, :], over(of_unit[:, :], NE),
                                         iota[:, 0:NE].unsqueeze(1).broadcast_to([P, MAXU + 1, NE]), ALU.is_equal))
                    link(v.tensor_scalar(first_of[:, :], iota[:, 0:MAXU + 1], -float(CAP), None, ALU.mult))
                    st.step(v.tensor_copy(units[:, 0:1], end_unit[:, NE - 1:NE]))
                    v.tensor_copy(units[:, 1:MAXU + 2], of_unit[:, :]).then_inc(table_ready, 1)
                else:
                    link(v.memset(f[:, :, :], 0.0))

                def gate_up(m0, tiles, j, cols, ta, tb, up, hi_of, lo_of, where=lambda s: None):
                    m = m0 + j
                    lo(m + 1, 0, cols, where(0))
                    dve.wait_ge(taken[0], m + 2)
                    used(m, 1)
                    dve.wait_ge(hid_ready, tiles + j + 1)
                    v.tensor_tensor(tb, up, ta, ALU.mult).then_inc(taken[1], 1)
                    if cols == SLAB:
                        lo(m + 1, 1, cols, where(1))
                    dve.wait_ge(hidhi_ready, tiles + j + 1)
                    v.tensor_tensor(lo_of[:, j, :], tb if len(tb.shape) == 2 else tb.rearrange("p a b -> p (a b)"),
                                    hi_of[:, j, :].bitcast(F32), ALU.subtract).then_inc(hid_ready, 1)
                    if cols != SLAB:
                        lo(m + 1, 1, cols, where(1))

                if L == 0:
                    with dve.Fori(0, NEXP[0]) as e:
                        outer2 = st.enter(e, 4 * N_DOWN // 2)
                        m0, tiles = e * EP + first["exp"], e * FT
                        with dve.Fori(0, FT - 1) as j:
                            gate_up(m0, tiles, j, SLAB, halves(ta), halves(tb), bank(1), hid_hi, hid_lo)
                        gate_up(m0, tiles, FT - 1, SLABMAX, halves(ta), halves(tb), bank(1), hid_hi, hid_lo)

                        def down(j, cols):
                            for s in range(2):
                                dve.wait_ge(hid_ready, tiles + (FT + 1))
                                used(m0 + FT + j, s)
                                f_k = halves(f[:, j * 2 + s, :])
                                v.tensor_tensor(f_k, f_k, bank(s), ALU.add).then_inc(taken[s], 1)
                                lo(m0 + FT + 1 + j, s, cols)
                            ada_take(1, e * (N_DOWN // 2) + j + NG // 2, e * (N_DOWN // 2) + j, 6)

                        with dve.Fori(0, N_DOWN // 2 - 1) as j:
                            outer = st.enter(j, 4)
                            down(j, SLABMAX)
                        st.leave(outer, N_DOWN // 2 - 1)
                        down(N_DOWN // 2 - 1, SLAB)
                    st.leave(outer2, NEXP[0])
                    residual(L, POST_FFN, "post_ffn", 5, f[:, :, :], x, sq)
                else:
                    ut = Tally(unit_steps, dve)

                    def make_places(u):
                        for src, to in ((comb, own_comb), (place, own_place)):
                            ut.step(v.tensor_tensor(own8[:, :, :], src[:, :, :],
                                                    is_expert[:, bass.ds(u, 1), :].broadcast_to([P, NCH + 1, NE]),
                                                    ALU.mult))
                            ut.settle()
                            ut.step(v.tensor_reduce(to[:, :], own8[:, :, :], axis=AX_X, op=ALU.add))
                            ut.settle()
                        ut.step(v.tensor_scalar(own_place[:, :], own_place[:, :], first_of[:, bass.ds(u, 1)], None,
                                                ALU.add))
                        ut.settle()
                        v.tensor_tensor(G[:, :, :], iota.unsqueeze(1).broadcast_to([P, NCH + 1, CAP]),
                                        over(own_place[:, :], CAP), ALU.is_equal).then_inc(G_ready, 1)

                    def ye_rest(u, k, s):
                        dve.wait_ge(yehi_ready, u * KT + (k + 1))
                        for c in range(CAPT):
                            ins = v.scalar_tensor_tensor(ye_lo[:, s, c * P:(c + 1) * P], ps[:, 2 * s + 1, c * P:(c + 1) * P],
                                                         cj[:, c:c + 1], ye_hi[:, s, c * P:(c + 1) * P].bitcast(F32),
                                                         ALU.mult, ALU.subtract)
                        ins.then_inc(ye_ready, 1)

                    def add(u, k, s):
                        dve.wait_ge(scattered, u * KT + (k + 1))
                        dve.wait_ge(f_cleared, 1)
                        dve.wait_ge(f_added, u * KT + PRIME)
                        f_k = halves(f_routed[:, k, :])
                        v.tensor_tensor(f_k, f_k, ps[:, 4 + 2 * s:6 + 2 * s, 0:HALF], ALU.add).then_inc(f_added, 1)

                    dve.sem_inc(f_added, PRIME)
                    make_places(0)
                    dve.wait_ge(table_ready, 1)
                    n = dve.value_load(units[0:1, 0:1], min_val=1, max_val=MAXU)
                    with dve.Fori(0, n) as u:
                        outer = ut.enter(u, 5)
                        m0, tiles = u * EP + first["exp"], (u + NEXP[0]) * FT
                        for q in range(KT // 2):
                            dve.wait_ge(lo_gathered, u * (KT // 2) + (q + 1))
                            v.tensor_copy(hu_lo[:, 2 * q:2 * q + 2, :],
                                          ps[:, 6 + q % 2, :].rearrange("p (k t) -> p k t", k=2)).then_inc(lo_taken, 1)
                            if q < 2:
                                lo(m0, q, SLAB, unit_raw(u, 0, 0, q))
                        with dve.Fori(0, FT // 2) as i:
                            for odd in range(2):
                                gate_up(m0, tiles, i * 2 + odd, SLAB, ta_u, tb_u, ps[:, 2, 0:CAP], hidu_hi, hidu_lo,
                                        lambda s: unit_raw(u, 1 - odd, i + odd, s))
                        gate_up(m0, tiles, FT - 1, SLABMAX, ta_u, tb_u, ps[:, 2, 0:CAP], hidu_hi, hidu_lo,
                                lambda s: unit_raw(u, 1, FT // 2, s))
                        dve.wait_ge(cj_done, u + 1)
                        v.tensor_copy(Gt[:, :, SEQ:T], ps[:, 6, 0:CAPT * NS].rearrange("p (c t) -> p c t", c=CAPT))
                        v.tensor_copy(cj[:, :], ps[:, 6, 128:128 + CAPT]).then_inc(cj_ready, 1)
                        dve.wait_ge(G_ready, u + 1)
                        make_places(u + 1)

                        def down(j, head, ahead):
                            for s in range(2):
                                if ahead:
                                    lo(m0 + FT + 1 + j, s, SLABMAX, unit_raw(u, (FT + j + 1) % 2, (FT + j + 1) // 2, s))
                                if s or not head:
                                    ye_rest(u, j * 2 + s - 1, 1 - s)
                                if not head:
                                    add(u, j * 2 + s - 2, s)

                        dve.wait_ge(cj_ready, u + 1)
                        for j in range(N_DOWN // 2):
                            down(j, j == 0, j < N_DOWN // 2 - 1)
                        ye_rest(u, KT - 1, 1)
                        for s in range(2):
                            add(u, KT - 2 + s, s)
                    v.memset(own8[:, :, :], 0.0).then_inc(units_over, 1)
                    dve.wait_ge(units_over, 1)
                    residual(L, POST_FFN, "post_ffn", 5, f_routed, x, f[:, :, :])
                ada_takes(L, "post_ffn")

        @block.tensor
        def _(pe):
            mm = nc.tensor.matmul

            def slab(m, s, kt, a_hi, a_lo, tile=None):
                pe.wait_ge(lo_split, m * 2 + (s + 1 + PRIME))
                pe.wait_ge(taken[s], m + 1)
                n = 0
                for k in range(kt):
                    if tile:
                        pe.wait_ge(tile[0], tile[1] + k + 1)
                    for w, a in ((whi, a_hi), (whi, a_lo), (wlo, a_hi)):
                        for half in range(2):
                            ins = mm(ps[:, 2 * s + half, 0:HALF], w[:, s, k * P:(k + 1) * P],
                                     a[:, k, half * HALF:(half + 1) * HALF], start=(n < 2), stop=(n >= 6 * kt - 2))
                            n += 1
                ins.then_inc(slabs_used, 1)

            def ada_group(n, b, strict=True, ks=range(KT)):
                if ks[0] == 0:
                    pe.wait_ge(ada_out, n + (1 if strict else 0))
                for k in ks:
                    pe.wait_ge(ada_landed[k % ADA_SLOTS], n * (16 * KT // ADA_SLOTS) + (16 * (k // ADA_SLOTS) + 16))
                    mm(ps[0:32, b, :], cond[:, k, :], adaw[:, k % ADA_SLOTS, :], start=(k == 0), stop=(k == KT - 1)
                       ).then_inc(ada_used, 1)

            def ada_groups(L, place):
                for n in MOD_AT.get((L, place), ()):
                    ada_group(n, mod_bank(place, n), n % 2 == 0)

            def sums_of(L, idx, src, ks, base):
                to = sums(idx)
                for n, k in enumerate(ks):
                    pe.wait_ge(sq_ready, 5 * KT * L + base + n + 1)
                    for half in range(2):
                        ins = mm(to[:, half, :], ones, src(k)[:, half * HALF:(half + 1) * HALF], start=(n == 0),
                                 stop=(n == len(ks) - 1))
                ins.then_inc(stat_done, 1)

            def by_token(L, nth, to):
                w, count = narrow_of(L, nth)
                n = w.shape[-1] // KT
                pe.wait_ge(nar_ready, count)
                for k in range(KT):
                    pe.wait_ge(h_ready, (2 * L + nth) * KT + k + 1)
                    for m, (w, a) in enumerate(((nar_hi, h_hi), (nar_hi, h_lo), (nar_lo, h_hi))):
                        for half in range(2):
                            ins = mm(ps[0:n, 4 + half, 0:HALF], w[:, n * k:n * (k + 1)],
                                     a[:, k, half * HALF:(half + 1) * HALF], start=(k + m == 0),
                                     stop=(k == KT - 1 and m == 2))
                ins.then_inc(nar_done, 1)
                pe.wait_ge(nar_taken, count)
                for c in range(NCH + 1):
                    rows = CH if c < NCH else NS
                    ins = mm(to[0:rows, n * c:n * (c + 1)], nar_t[0:n, c * CH:c * CH + rows], ident[0:n, 0:n],
                             start=True, stop=True)
                return ins

            pe.sem_inc(slabs_used, PRIME)
            pe.sem_inc(ada_used, ADA_SLOTS)
            pe.sem_inc(ada_out, 1)
            pe.wait_ge(cond_ready, 1)
            with pe.Fori(0, 2) as n:
                ada_group(n, 6)
            sums_of(0, PRE_MIX, lambda k: sq[:, k, :], range(KT), SQ[PRE_MIX])
            with pe.Fori(2, 4) as n:
                ada_group(n, 6)
            for L in range(DEPTH):
                first = FIRST[L]
                if L:
                    pe.wait_ge(ada_out, 21 + 2)
                    sums_of(L, PRE_MIX, lambda k: sq[:, k, :], range(KT), SQ[PRE_MIX])
                ada_groups(L, "pre_mix")
                by_token(L, 0, ps[:, 5, :]).then_inc(dt_done, 1)
                with pe.Fori(0, N_XBC // 2) as i:
                    for s in range(2):
                        slab(i + first["xbc"], s, KT, h_hi, h_lo)
                pe.wait_ge(dA_ready, L + 1)
                dA_p = dA[:, 0:NCH, :].rearrange("p c h -> p (c h)")
                mm(ps[:, 7, 0:64], tri, dA_p, start=True, stop=True)
                mm(ps[:, 7, 64:128], ones, dA_p, start=True, stop=True)
                mm(ps[0:NS, 7, 128:144], con("tri_seq")[0:NS], dA[0:NS, NCH, :], start=True, stop=True)
                mm(ps[0:NS, 7, 144:160], con("same_seq")[0:NS], dA[0:NS, NCH, :], start=True, stop=True)
                mm(ps[:, 7, 160:288], con("ones")[0:NS].to_broadcast([NS, P]), dA_s[0:NS].rearrange("p b h -> p (b h)"), start=True, stop=True
                   ).then_inc(cum_done, 1)
                ada_groups(L, "cum")
                pe.wait_ge(xbc_ready, XBC * (L + 1) + 1)
                pe.wait_ge(cum_e, L + 1)
                if L == 0:
                    pe.wait_ge(ada_out, 6 + 2)
                for k in range(KT):
                    nc.tensor.transpose(ps[0:NS, 4 + k // GT, (k % GT) * P:(k % GT + 1) * P], mix[:, k, SEQ:T], ident)
                for g in range(GROUPS):
                    nc.tensor.transpose(ps[0:NS, 6, g * P:(g + 1) * P], mix[:, B0 + g, SEQ:T], ident)
                for g in range(GROUPS):
                    mm(ps[0:NS, 6, 256 + NS * g:256 + NS * (g + 1)], mix[:, B0 + g, SEQ:T], mix[:, C0 + g, SEQ:T],
                       start=True, stop=True)
                for h in range(HEADS):
                    ins = mm(ps[:, 7, NS * h:NS * (h + 1)], dA[0:NS, NCH, h:h + 1].to_broadcast([NS, P]),
                             con("tri_seq")[0:NS], start=True, stop=True)
                ins.then_inc(smp_pe, 1)
                pe.wait_ge(smp_G, L + 1)
                for h in range(HEADS):
                    a = HD * (h % 2)
                    ins = mm(ps[a:a + HD, 6, (h // 2) * NS:(h // 2 + 1) * NS], xdt_s[0:NS, h * HD:(h + 1) * HD],
                             E_s[0:NS, h, :], start=True, stop=True)
                ins.then_inc(smp_y, 1)
                if L == 0:
                    pe.sem_inc(chunk_pe, 1)
                with pe.Fori(0, NCH) as c:
                    for g in range(GROUPS):
                        i = c * 2 + g
                        mA, mB = i * 2 + first["mix"], i * 2 + (first["mix"] + 1)
                        slab(mA, 0, KT, h_hi, h_lo)
                        pe.wait_ge(staged, i + (KT * L + 1))
                        pe.wait_ge(units_free, i + ((KT + 1) * L + 1))
                        for j in range(GT):
                            nc.tensor.transpose(ps[:, 6, j * P:(j + 1) * P], x_st[j], ident)
                        nc.tensor.transpose(ps[:, 7, 0:NST], B_st, ident)
                        for gg in range(GROUPS):
                            pe.wait_ge(seq_in[gg], i * 16 + (16 + 16 * (NB + 1) * L))
                        for k in range(KT):
                            mm(ps[:, 7, 256 + TS * k:256 + TS * (k + 1)], S0[:, k // GT, (k % GT) * P:(k % GT + 1) * P],
                               mix[:, C0 + k // GT, bass.ds(i * TS + SEQ, TS)], start=True, stop=True)
                        mm(ps[:, 7, NST:2 * NST], B_st, mix[:, C0 + g, bass.ds(c * CH, CH)], start=True, stop=True)
                        for h in range(GH):
                            ins = mm(ps[:, 4 + h // 4, (h % 4) * CH:(h % 4 + 1) * CH],
                                     dA_st[:, h:h + 1].to_broadcast([P, P]), tri, start=True, stop=True)
                        ins.then_inc(chunk_pe, 1)
                        slab(mA, 1, KT, h_hi, h_lo)
                        slab(mB, 0, KT, h_hi, h_lo)
                        pe.wait_ge(chunk_G, i + (KT * L + 1))
                        pe.wait_ge(chunk_Ce, i + (KT * L + 1))
                        for h in range(GH):
                            a = HD * (h % 2)
                            to = ps[a:a + HD, 7, (h // 2) * CH:(h // 2 + 1) * CH]
                            mm(to, xdt[:, h * HD:(h + 1) * HD], E[:, h, :], start=True, stop=False)
                            mm(to, S[:, g, h * HD:(h + 1) * HD], Ce[:, h, :], start=False, stop=True)
                        mm(ps[:, 6, :], Bt, xe, start=True, stop=True).then_inc(chunk_y, 1)
                        for gg in range(GROUPS):
                            ins = mm(ps[:, 4 + gg, :], Bm[0:NS, gg * NST:(gg + 1) * NST],
                                     xe_s[0:NS, gg * GH * HD:(gg + 1) * GH * HD], start=True, stop=True)
                        ins.then_inc(seq_pe, 1)
                        slab(mB, 1, KT, h_hi, h_lo)
                pe.wait_ge(ya_ready, KT * (L + 1))
                for s in range(2):
                    slab(first["outA"], s, KT, ya_hi, ya_lo)
                ada_groups(L, "gate")
                for s in range(2):
                    slab(first["outA"] + 1, s, KT, ya_hi, ya_lo)
                for g in range(GROUPS):
                    if L == 0 and g == 1:
                        pe.wait_ge(ada_out, 7 + 2)
                    sums_of(L, GATE + g, lambda k: z[:, k, :], range(GT * g, GT * (g + 1)), SQ[GATE] + GT * g)
                with pe.Fori(2, KT // 2) as i:
                    for s in range(2):
                        slab(i + first["outA"], s, KT, ya_hi, ya_lo)
                slab(first["outB"], 0, KT, h_hi, h_lo, (yb_ready, KT * L))
                slab(first["outB"], 1, KT, h_hi, h_lo)
                with pe.Fori(1, KT // 2) as i:
                    for s in range(2):
                        slab(i + first["outB"], s, KT, h_hi, h_lo)
                sums_of(L, POST_MIX, lambda k: sq[:, k, :], range(KT), SQ[POST_MIX])
                pe.wait_ge(rstd_ready, NORMS * L + POST_MIX + 1)
                ada_groups(L, "post_mix")
                sums_of(L, PRE_FFN, lambda k: sq[:, k, :], range(KT), SQ[PRE_FFN])
                ada_groups(L, "pre_ffn")
                if L == 0:
                    pe.wait_ge(h_ready, 2 * KT)
                    with pe.Fori(0, NEXP[0]) as e:
                        m0 = e * EP + first["exp"]
                        with pe.Fori(0, FT) as j:
                            slab(m0 + j, 0, KT, h_hi, h_lo)
                            slab(m0 + j, 1, KT, h_hi, h_lo)
                        with pe.Fori(0, N_DOWN // 2) as j:
                            for s in range(2):
                                pe.wait_ge(hid_ready, e * FT + (FT + 1))
                                slab(m0 + FT + j, s, FT, hid_hi, hid_lo)
                                ada_group(e * (N_DOWN // 2) + j + NG // 2, 6, ks=range(s * KT // 2, (s + 1) * KT // 2))
                    pe.wait_ge(ada_out, 19 + 2)
                    sums_of(L, POST_FFN, lambda k: sq[:, k, :], range(KT), SQ[POST_FFN])
                    ada_groups(L, "post_ffn")
                    continue
                by_token(L, 1, ps[:, 7, :]).then_inc(logits_done, 1)
                for c in range(NCH + 1):
                    rows = CH if c < NCH else NS
                    if c == NCH - 1:
                        pe.wait_ge(chosen, 1)
                        rank_p = rank[:, 0:NCH, :].rearrange("p c e -> p (c e)")
                        mm(ps[:, 7, 64:96], tri, rank_p, start=True, stop=True)
                        mm(ps[0:NS, 7, 96:104], tri[0:NS, 0:NS], rank[0:NS, NCH, :], start=True, stop=True)
                        mm(ps[:, 7, 128:160], ones, rank_p, start=True, stop=True)
                        mm(ps[:, 7, 160:168], con("ones")[0:NS].to_broadcast([NS, P]), rank[0:NS, NCH, :], start=True, stop=True
                           ).then_inc(counted, 1)
                    for part, h in enumerate((h_hi, h_lo)):
                        if c:
                            pe.wait_ge(tok_taken, 2 * c - 1 + part)
                        for k in range(KT):
                            ins = nc.tensor.transpose(ps[0:rows, 2 * part + k // 4, (k % 4) * P:(k % 4 + 1) * P],
                                                      h[:, k, c * CH:c * CH + rows].bitcast(F32), ident)
                        ins.then_inc(tok_turned, 1)
                pe.wait_ge(tok_taken, 2 * (NCH + 1))
                pe.wait_ge(table_ready, 1)
                n_of = pe.value_load(units[0:1, 0:1], min_val=1, max_val=MAXU)

                def unit_slab(m, s, kt, a_hi, a_lo):
                    pe.wait_ge(lo_split, m * 2 + (s + 1 + PRIME))
                    pe.wait_ge(taken[s], m + 1)
                    n = 0
                    for k in range(kt):
                        for w, a in ((whi, a_hi), (whi, a_lo), (wlo, a_hi)):
                            ins = mm(ps[:, 2 * s, 0:CAP], w[:, s, k * P:(k + 1) * P], a[:, k, 0:CAP], start=(n == 0),
                                     stop=(n == 3 * kt - 1))
                            n += 1
                    ins.then_inc(slabs_used, 1)

                with pe.Fori(0, n_of) as u:
                    m0 = u * EP + first["exp"]
                    pe.wait_ge(G_ready, u + 1)
                    for c in range(CAPT):
                        for q in range(NCH):
                            ins = nc.tensor.transpose(ps[:, 2 * c + 1, q * P:(q + 1) * P],
                                                      G[:, q, c * P:(c + 1) * P].bitcast(F32), ident)
                    ins.then_inc(G_turned, 1)
                    for q in range(KT // 2):
                        for part, (tok, gathered, gone) in enumerate(((htok_hi, hi_gathered, hi_taken),
                                                                      (htok_lo, lo_gathered, lo_taken))):
                            if q < 2:
                                pe.wait_ge(f_added, u * KT + PRIME)
                            else:
                                pe.wait_ge(gone, u * (KT // 2) + (q - 1))
                            for k in (2 * q, 2 * q + 1):
                                for c in range(NCH + 1):
                                    rows = CH if c < NCH else NS
                                    ins = mm(ps[:, 4 + 2 * part + q % 2, (k % 2) * CAP:(k % 2 + 1) * CAP],
                                             tok[0:rows, c, k * P:(k + 1) * P], G[0:rows, c, :], start=(c == 0),
                                             stop=(c == NCH))
                            ins.then_inc(gathered, 1)
                    with pe.Fori(0, FT) as j:
                        pe.wait_ge(hi_taken, u * (KT // 2) + KT // 2)
                        pe.wait_ge(lo_taken, u * (KT // 2) + KT // 2)
                        unit_slab(m0 + j, 0, KT, hu_hi, hu_lo)
                        unit_slab(m0 + j, 1, KT, hu_hi, hu_lo)

                    pe.wait_ge(lo_taken, u * (KT // 2) + (KT // 2 - 1))
                    for c in range(CAPT):
                        mm(ps[:, 6, c * NS:(c + 1) * NS], G[0:NS, NCH, c * P:(c + 1) * P].bitcast(F32),
                           ident[0:NS, 0:NS], start=True, stop=True)
                    for c in range(CAPT):
                        for q in range(NCH + 1):
                            rows = CH if q < NCH else NS
                            ins = mm(ps[:, 6, 128 + c:129 + c], G[0:rows, q, c * P:(c + 1) * P].bitcast(F32),
                                     own_comb[0:rows, q:q + 1], start=(q == 0), stop=(q == NCH))
                    ins.then_inc(cj_done, 1)
                    def turn(j, s):
                        pe.wait_ge(taken[s], m0 + FT + j + 2)
                        for c in range(CAPT):
                            ins = nc.tensor.transpose(ps[:, 2 * s + 1, c * P:(c + 1) * P], yu[:, s, c * P:(c + 1) * P],
                                                      ident)
                        ins.then_inc(y_turned, 1)

                    def scatter(j, s):
                        pe.wait_ge(ye_ready, u * KT + j * 2 + (s + 1))
                        pe.wait_ge(f_added, u * KT + j * 2 + (s + 1))
                        n = 0
                        for c in range(CAPT):
                            for ye in (ye_hi, ye_lo):
                                for half in range(2):
                                    ins = mm(ps[:, 4 + 2 * s + half, 0:HALF], ye[:, s, c * P:(c + 1) * P],
                                             Gt[:, c, half * HALF:(half + 1) * HALF], start=(n < 2), stop=(n >= 6))
                                    n += 1
                        ins.then_inc(scattered, 1)

                    def down(j, s):
                        pe.wait_ge(hid_ready, (u + (NEXP[0] + 1)) * FT + 1)
                        unit_slab(m0 + FT + j, s, FT, hidu_hi, hidu_lo)

                    down(0, 0)
                    down(0, 1)
                    turn(0, 0)
                    with pe.Fori(1, N_DOWN // 2) as j:
                        down(j, 0)
                        turn(j - 1, 1)
                        scatter(j - 1, 0)
                        down(j, 1)
                        turn(j, 0)
                        scatter(j - 1, 1)
                    turn(N_DOWN // 2 - 1, 1)
                    scatter(N_DOWN // 2 - 1, 0)
                    scatter(N_DOWN // 2 - 1, 1)
                sums_of(L, POST_FFN, lambda k: f[:, k, :], range(KT), SQ[POST_FFN])


def kernel(**inputs):
    import concourse.bacc as _bacc
    from concourse.bass_utils import run_bass_kernel_spmd as _run

    a = {k: np.asarray(v) for k, v in inputs.items()}

    def tiles(w):
        *lead, k, n = w.shape
        w = w.reshape(*lead, k // P, P, n // P, P)
        d = len(lead)
        return np.ascontiguousarray(np.moveaxis(w, (d + 2, d + 1, d, d + 3), (d, d + 1, d + 2, d + 3))).reshape(
            *lead, n // P, P, k)

    def by_feature(v):
        v = v.reshape(*v.shape[:-1], v.shape[-1] // P, P)
        return np.ascontiguousarray(np.moveaxis(v, (-1, -2), (0, 1)))

    xall = np.concatenate([a["x_prompt"].reshape(SEQ, D), a["x_sample"].reshape(NS, D)])
    call = np.concatenate([a["c_prompt"], a["c_sample"], np.zeros((32 - NM, D), np.float32)])
    pack = []
    w_dt0 = a["w_in"].shape[-1] - HEADS
    for L in range(DEPTH):
        cols = [by_feature(a["ada_b"][L]), by_feature(a["norm_pre_mix"][L]), by_feature(a["norm_post_mix"][L]),
                by_feature(a["norm_pre_ffn"][L]), by_feature(a["norm_post_ffn"][L]),
                np.moveaxis(by_feature(a["conva_w"][L]), 2, 1), np.moveaxis(by_feature(a["convb_w"][L]), 2, 1),
                by_feature(a["convb_b"][L]), by_feature(a["ssd_norm"][L]),
                by_feature(np.broadcast_to(a["d_skip"][L][:, None], (HEADS, HD)).reshape(-1)),
                a["w_in"][L][:, w_dt0:].reshape(KT, P, HEADS).transpose(1, 0, 2),
                np.broadcast_to(a["dt_bias"][L], (P, HEADS)), np.broadcast_to(a["a_log"][L], (P, HEADS))]
        pack += [c.reshape(P, -1) for c in cols]
    s, q = np.arange(P)[:, None], np.arange(P)[None, :]
    s2, q2 = s, np.arange(NS)[None, :]
    e2 = np.arange(NE)
    const = [(s <= q), (s == q), np.ones((P, 1)), (s2 // TS == q2 // TS) & (s2 <= q2), (s2 // TS == q2 // TS),
             (s // TS == np.arange(NB)[None, :]), np.full((P, 1), EPS),
             np.broadcast_to((e2[None, :] < e2[:, None]).reshape(1, -1), (P, NE * NE))]
    count = np.ascontiguousarray(np.broadcast_to(np.arange(CAP, dtype=np.float32), (P, CAP)))
    w_in = tiles(a["w_in"][:, :, :w_dt0])
    c = KT
    ff = a["ffd_w_gate"].shape[-1] // 2

    def gate_up(wg, wu):
        g, u = tiles(wg), tiles(wu)
        return np.stack([g, u], 2).reshape(g.shape[0], -1, P, D)

    def states(v):
        v = v.reshape(DEPTH, NB, v.shape[2], -1, P)
        return np.ascontiguousarray(v.transpose(0, 4, 3, 1, 2)).reshape(DEPTH, P, -1)

    split = a["ffd_w_gate"][0].reshape(D, 2, ff).transpose(1, 0, 2)
    splitu = a["ffd_w_up"][0].reshape(D, 2, ff).transpose(1, 0, 2)
    w_out = tiles(a["w_out"]).reshape(DEPTH, KT, P, 2, D).transpose(0, 3, 1, 2, 4)
    arrays = {
        "xT": by_feature(xall).reshape(P, -1),
        "cT": by_feature(call).reshape(P, -1),
        "pack": np.concatenate(pack, 1),
        "const": np.concatenate([v.astype(np.float32) for v in const], 1),
        "count": count,
        "w_router": a["moe_router"][0].reshape(KT, P, NE).transpose(1, 0, 2).reshape(P, -1),
        "s_conva": states(a["state_conva"]),
        "s_convb": states(a["state_convb"]),
        "s_ssm": a["state_ssm"].reshape(DEPTH, NB, GROUPS, GH * HD, NST).transpose(0, 1, 2, 4, 3),
        "w_ada": a["ada_w"].reshape(DEPTH, KT, P, NG // 2, 512).transpose(0, 3, 1, 2, 4).reshape(NG, KT, P, 512),
        "w_xbc": w_in[:, 4 * c:],
        "w_mix": np.stack([w_in[:, c:2 * c], w_in[:, 2 * c:3 * c], w_in[:, 0:c], w_in[:, 3 * c:4 * c]], 2).reshape(
            DEPTH, 4 * c, P, D),
        "w_out": w_out.reshape(DEPTH, 2 * KT, P, D),
        "w_gu0": gate_up(split, splitu),
        "w_dn0": tiles(a["ffd_w_down"][0].reshape(2, ff, D)),
        "w_gu1": gate_up(a["moe_w_gate"][0], a["moe_w_up"][0]),
        "w_dn1": tiles(a["moe_w_down"][0]),
    }
    arrays = {k: np.ascontiguousarray(v) for k, v in arrays.items()}
    outs = {"yT": (P, KT * T), "o_ap": (DEPTH, P, KT * 2), "o_bp": (DEPTH, P, XBC * 3),
            "o_sp": (DEPTH, P, HEADS * HD), "o_as": (DEPTH, P, KT * NB * 2), "o_bs": (DEPTH, P, XBC * NB * 3),
            "o_ss": (DEPTH, NB, GROUPS, P, GH * HD)}
    nc = _bacc.Bacc("TRN2", target_bir_lowering=False, num_devices=1)
    args = [nc.dram_tensor(k, v.shape, mybir.dt.from_np(v.dtype), kind="ExternalInput").ap() for k, v in arrays.items()]
    args += [nc.dram_tensor(k, v, F32, kind="ExternalOutput").ap() for k, v in outs.items()]
    hybrid_decoder(nc, *args)
    r = _run(nc, [arrays], core_ids=[0]).results[0]
    y = r["yT"].reshape(P, KT, T).transpose(2, 1, 0).reshape(T, D)

    def rows(v, n, tile):
        v = v.reshape(DEPTH, P, tile, *n)
        return np.ascontiguousarray(np.moveaxis(v, (2, 1), (-2, -1))).reshape(DEPTH, *n, tile * P)

    return (y[:SEQ].reshape(1, SEQ, D), y[SEQ:].reshape(NB, TS, D),
            rows(r["o_ap"], (1, 2), KT), rows(r["o_bp"], (1, 3), XBC),
            np.ascontiguousarray(r["o_sp"].reshape(DEPTH, 1, P, HEADS, HD).transpose(0, 1, 3, 4, 2)),
            rows(r["o_as"], (NB, 2), KT), rows(r["o_bs"], (NB, 3), XBC),
            np.ascontiguousarray(r["o_ss"].reshape(DEPTH, NB, GROUPS, P, GH, HD).transpose(0, 1, 2, 4, 5, 3)).reshape(
                DEPTH, NB, HEADS, HD, NST))
```
